# Optimizing a Trainium2 kernel written in Bass

```python
import jax, jax.numpy as jnp
from jax import lax
import numpy as np

D_MODEL = 2048
BATCH = 1
SEQ = 256
DEPTH = 1

CHUNK = 64
MIX_WIDTH = D_MODEL
GMLP_WIDTH = MIX_WIDTH // 2
GMLP_GROUPS = 8
GMLP_GROUP_DIM = GMLP_WIDTH // GMLP_GROUPS
GMLP_BLOCK = 128
MLA_WIDTH = MIX_WIDTH - GMLP_WIDTH
MLA_HEADS = 8
QK_NOPE_DIM = 128
QK_ROPE_DIM = 64
V_HEAD_DIM = MLA_WIDTH // MLA_HEADS
Q_LORA_RANK = 512
KV_LORA_RANK = 256
QK_HEAD_DIM = QK_NOPE_DIM + QK_ROPE_DIM
D_FF = 4 * D_MODEL
ROPE_THETA = 10000.0
EPS = 1e-6
Q_BLOCK = 128
N_MOD = 6
IN_SPLITS = (GMLP_WIDTH, GMLP_WIDTH, Q_LORA_RANK, KV_LORA_RANK, QK_ROPE_DIM)
IN_PROJ = sum(IN_SPLITS)

kernel_name = "hybrid_gmlp_mla_sandwich_adaln_block"

def rms_norm(x, g):
    xf = x.astype(jnp.float32)
    y = xf * lax.rsqrt(jnp.mean(xf * xf, axis=-1, keepdims=True) + EPS)
    return (y * g.astype(jnp.float32)).astype(x.dtype)

def layer_norm(x, g, b):
    xf = x.astype(jnp.float32)
    mu = jnp.mean(xf, axis=-1, keepdims=True)
    var = jnp.mean(jnp.square(xf - mu), axis=-1, keepdims=True)
    y = (xf - mu) * lax.rsqrt(var + EPS)
    return (y * g.astype(jnp.float32) + b.astype(jnp.float32)).astype(x.dtype)

def rope(x, positions):
    dr = x.shape[-1]
    freqs = ROPE_THETA ** (-jnp.arange(0, dr, 2, dtype=jnp.float32) / dr)
    ang = positions.astype(jnp.float32)[:, :, None] * freqs
    cos = jnp.cos(ang)[:, :, None, :].astype(x.dtype)
    sin = jnp.sin(ang)[:, :, None, :].astype(x.dtype)
    x1, x2 = jnp.split(x, 2, axis=-1)
    return jnp.concatenate([x1 * cos - x2 * sin, x2 * cos + x1 * sin], axis=-1)

def gmlp_mixer(u, v, ln_g, ln_b, w_s, b_s):
    u = jax.nn.gelu(u, approximate=False)
    v = layer_norm(jax.nn.gelu(v, approximate=False), ln_g, ln_b)
    B, S, _ = v.shape
    nb = S // GMLP_BLOCK
    vb = v.reshape(B, nb, GMLP_BLOCK, GMLP_GROUPS, GMLP_GROUP_DIM)
    ch = jnp.arange(GMLP_BLOCK) // CHUNK
    mask = (ch[None, :] <= ch[:, None]).astype(w_s.dtype)
    w = w_s * mask[None]
    s = jnp.einsum('gij,bnjgc->bnigc', w, vb) + jnp.transpose(b_s)[None, None, :, :, None]
    return u * s.reshape(B, S, GMLP_WIDTH)

def mla_mixer(q_lat, kv_lat, k_rope, positions, q_norm_g, w_q_b, kv_norm_g, w_kv_b):
    B, S, _ = q_lat.shape
    q = (rms_norm(q_lat, q_norm_g) @ w_q_b).reshape(B, S, MLA_HEADS, QK_HEAD_DIM)
    q_nope, q_pe = q[..., :QK_NOPE_DIM], q[..., QK_NOPE_DIM:]
    q = jnp.concatenate([q_nope, rope(q_pe, positions)], axis=-1)
    kv = (rms_norm(kv_lat, kv_norm_g) @ w_kv_b).reshape(B, S, MLA_HEADS, QK_NOPE_DIM + V_HEAD_DIM)
    k_nope, v = kv[..., :QK_NOPE_DIM], kv[..., QK_NOPE_DIM:]
    k_pe = rope(k_rope[:, :, None, :], positions)
    k = jnp.concatenate([k_nope, jnp.broadcast_to(k_pe, (B, S, MLA_HEADS, QK_ROPE_DIM))], axis=-1)
    scale = QK_HEAD_DIM ** -0.5
    outs = []
    for blk in range(S // Q_BLOCK):
        q0 = blk * Q_BLOCK
        kend = q0 + Q_BLOCK
        sc = jnp.einsum('bqhd,bkhd->bhqk', q[:, q0:kend], k[:, :kend]).astype(jnp.float32) * scale
        qc = (q0 + jnp.arange(Q_BLOCK)) // CHUNK
        kc = jnp.arange(kend) // CHUNK
        sc = jnp.where(kc[None, :] <= qc[:, None], sc, -jnp.inf)
        p = jax.nn.softmax(sc, axis=-1).astype(v.dtype)
        outs.append(jnp.einsum('bhqk,bkhd->bqhd', p, v[:, :kend]))
    return jnp.concatenate(outs, axis=1).reshape(B, S, MLA_WIDTH)

def setup_inputs(seed: int = 0) -> dict:
    key = jax.random.key(seed)
    ks = jax.random.split(key, 24)
    f32 = jnp.float32
    L = DEPTH

    def nrm(k, shape, s):
        return jax.random.normal(k, shape, f32) * s

    def gain(k, n):
        return 1.0 + 0.05 * jax.random.normal(k, (L, n), f32)

    return {
        "x": jax.random.normal(ks[0], (BATCH, SEQ, D_MODEL), f32),
        "c": jax.random.normal(ks[1], (BATCH, D_MODEL), f32),
        "positions": jnp.broadcast_to(jnp.arange(SEQ, dtype=jnp.int32)[None, :], (BATCH, SEQ)),
        "w_ada": nrm(ks[2], (L, D_MODEL, N_MOD * D_MODEL), 0.5 * D_MODEL ** -0.5),
        "b_ada": nrm(ks[3], (L, N_MOD * D_MODEL), 0.02),
        "pre_norm1_g": gain(ks[4], D_MODEL),
        "w_in": nrm(ks[5], (L, D_MODEL, IN_PROJ), D_MODEL ** -0.5),
        "ln_v_g": gain(ks[6], GMLP_WIDTH),
        "ln_v_b": nrm(ks[7], (L, GMLP_WIDTH), 0.02),
        "w_s": nrm(ks[8], (L, GMLP_GROUPS, GMLP_BLOCK, GMLP_BLOCK), 0.5 * GMLP_BLOCK ** -0.5),
        "b_s": 1.0 + 0.05 * jax.random.normal(ks[9], (L, GMLP_GROUPS, GMLP_BLOCK), f32),
        "q_norm_g": gain(ks[10], Q_LORA_RANK),
        "w_q_b": nrm(ks[11], (L, Q_LORA_RANK, MLA_HEADS * QK_HEAD_DIM), Q_LORA_RANK ** -0.5),
        "kv_norm_g": gain(ks[12], KV_LORA_RANK),
        "w_kv_b": nrm(ks[13], (L, KV_LORA_RANK, MLA_HEADS * (QK_NOPE_DIM + V_HEAD_DIM)), KV_LORA_RANK ** -0.5),
        "grp_norm_a_g": gain(ks[14], GMLP_WIDTH),
        "grp_norm_b_g": gain(ks[15], MLA_WIDTH),
        "w_o": nrm(ks[16], (L, MIX_WIDTH, D_MODEL), MIX_WIDTH ** -0.5),
        "post_norm1_g": gain(ks[17], D_MODEL),
        "pre_norm2_g": gain(ks[18], D_MODEL),
        "w_ff1": nrm(ks[19], (L, D_MODEL, D_FF), D_MODEL ** -0.5),
        "w_ff2": nrm(ks[20], (L, D_FF, D_MODEL), D_FF ** -0.5),
        "post_norm2_g": gain(ks[21], D_MODEL),
    }

def reference(x, c, positions, w_ada, b_ada, pre_norm1_g, w_in, ln_v_g, ln_v_b, w_s, b_s,
              q_norm_g, w_q_b, kv_norm_g, w_kv_b, grp_norm_a_g, grp_norm_b_g, w_o,
              post_norm1_g, pre_norm2_g, w_ff1, w_ff2, post_norm2_g):
    cs = jax.nn.silu(c)
    offs = np.cumsum(IN_SPLITS)[:-1].tolist()
    for l in range(DEPTH):
        mod = cs @ w_ada[l] + b_ada[l]
        sh1, sc1, g1, sh2, sc2, g2 = [m[:, None, :] for m in jnp.split(mod, N_MOD, axis=-1)]

        h = rms_norm(x, pre_norm1_g[l]) * (1.0 + sc1) + sh1
        z = h @ w_in[l]
        u, v, q_lat, kv_lat, k_rope = jnp.split(z, offs, axis=-1)
        a = gmlp_mixer(u, v, ln_v_g[l], ln_v_b[l], w_s[l], b_s[l])
        m = mla_mixer(q_lat, kv_lat, k_rope, positions, q_norm_g[l], w_q_b[l],
                      kv_norm_g[l], w_kv_b[l])
        y = jnp.concatenate([rms_norm(a, grp_norm_a_g[l]), rms_norm(m, grp_norm_b_g[l])], axis=-1) @ w_o[l]
        x = x + g1 * rms_norm(y, post_norm1_g[l])

        h = rms_norm(x, pre_norm2_g[l]) * (1.0 + sc2) + sh2
        f = jnp.square(jax.nn.relu(h @ w_ff1[l])) @ w_ff2[l]
        x = x + g2 * rms_norm(f, post_norm2_g[l])
    return x


_drawn_inputs = setup_inputs


def setup_inputs(seed=0):
    import zlib

    import numpy as np

    out = dict(_drawn_inputs(seed))
    spreads = {}
    factors = {'pre_norm1_g': 4.306,
     'ln_v_g': 32.022,
     'ln_v_b': 171.533,
     'b_s': 29.183,
     'q_norm_g': 8.0,
     'kv_norm_g': 5.636,
     'grp_norm_a_g': 5.523,
     'grp_norm_b_g': 5.557,
     'post_norm1_g': 3.896,
     'pre_norm2_g': 3.614,
     'post_norm2_g': 3.985}
    for name, (base, spread) in spreads.items():
        noise = np.random.default_rng([zlib.crc32(name.encode()), seed]).standard_normal(out[name].shape)
        drawn = base * np.exp(spread * noise) if base else spread * noise
        out[name] = __import__('jax').numpy.asarray(drawn.astype(out[name].dtype))
    for name, factor in factors.items():
        out[name] = (out[name] * factor).astype(out[name].dtype)
    return out
```

```python
import concourse.bass as bass
from concourse import mybir
from contextlib import ExitStack

P = 128
SEQ = 256
D = 2048
KT = D // P
CHUNK = 64
GW = 1024
GROUPS = 8
HEADS = 8
NOPE, ROPE, VD = 128, 64, 128
QL, KVL = 512, 256
QHD = NOPE + ROPE
DFF = 8192
FT = DFF // P
EPS = 1e-6
NEG = -1e30
ROPE_THETA = 10000.0
UNIT = 2048
RING = 4

COLS = {}
_at = 0
for _name, _n in (("c", 16), ("b_ada", 96), ("pre1", 16), ("post1", 16), ("pre2", 16), ("post2", 16),
                  ("qn", 4), ("kvn", 2), ("ga", 8), ("gb", 8)):
    COLS[_name] = (_at, _at + _n)
    _at += _n
NCOLS = _at
C_IDENT, C_SWAP, C_FREQ, NCONST = 0, 128, 256, 257

TWO_PI = (6.28125, 0.0019350051879882812, 3.0199159819504e-07)
ROUND = 12582912.0
PI = 3.1415925

NORMS = {}
_at = 0
for _i, (_name, _n) in enumerate((("x", 8), ("kv", 1), ("q", 2), ("a", 4), ("m", 4), ("y", 8), ("x1", 8), ("f", 8))):
    NORMS[_name] = (_i, _at, _n)
    _at += _n

W_ROPE = KT
W_U = W_ROPE + 1
W_O = W_U + 8
W_F1 = W_O + 16
W_F2 = W_F1 + 64

ITEMS = ([("rope", 0), ("u", 0), ("u", 1), ("kvb", 0), ("kvb", 1)] + [("qb", i) for i in range(4)]
         + [("u", i) for i in range(2, 8)] + [("wo", i) for i in range(16)])
ADA_AFTER = [2] * 17 + [1] * 14
STREAM = []
for _i, _item in enumerate(ITEMS):
    STREAM.append((_item, _i))
    for _ in range(ADA_AFTER[_i]):
        STREAM.append((("ada", sum(1 for s in STREAM if s[0][0] == "ada")), _i))
N_IN = KT
N_FF1 = N_IN + len(STREAM)
N_FF2 = N_FF1 + 64
ADA_HALVES = [(2 * D, 32), (2 * D + 1024, 40), (4 * D, 64), (4 * D + 1024, 72), (3 * D, 48), (3 * D + 1024, 56)]
CONV_AFTER = {5: 0, 9: 1, 13: 2, 17: 3, 24: 4, 30: 5}


def block_kernel(nc, A, out):
    f32, f32r, i32 = mybir.dt.float32, mybir.dt.float32r, mybir.dt.int32
    ALU = mybir.AluOpType
    ACT = mybir.ActivationFunctionType
    AX = mybir.AxisListType

    w_ada, w_in, w_qb, w_kvb = A["w_ada"], A["w_in"], A["w_q_b"], A["w_kv_b"]
    w_o, w_ff1, w_ff2 = A["w_o"], A["w_ff1"], A["w_ff2"]

    ctx = ExitStack()
    with ctx:
        def sb(name, shape, dt=f32):
            return ctx.enter_context(nc.sbuf_tensor(name, shape, dt))

        def sem(name):
            return ctx.enter_context(nc.semaphore(name))

        xT = sb("xT", [P, KT, SEQ])
        big = sb("big", [P, FT * SEQ])
        raw = sb("raw", [P, RING, UNIT])
        w_hi = sb("w_hi", [P, 2, UNIT], f32r)
        w_lo = sb("w_lo", [P, 2, UNIT], f32r)
        a_hi = sb("a_hi", [P, KT, SEQ], f32r)
        a_lo = sb("a_lo", [P, KT, SEQ], f32r)
        cols = sb("cols", [P, NCOLS])
        cst = sb("cst", [P, NCONST])
        ones = sb("ones", [P, P])
        eps = sb("eps", [P, 1])
        cs = sb("cs", [P, KT])
        mods = sb("mods", [P, 96])
        gain1 = sb("gain1", [P, KT])
        gain2 = sb("gain2", [P, KT])
        gate1 = sb("gate1", [P, KT])
        gate2 = sb("gate2", [P, KT])
        cosT = sb("cosT", [P, SEQ])
        sinT = sb("sinT", [P, SEQ])
        std = sb("std", [P, SEQ])
        R = sb("R", [P, SEQ])
        h32 = sb("h32", [P, 2, SEQ])
        sqb = sb("sqb", [P, 2, 2 * SEQ])
        gm_w = sb("gm_w", [P, 2048])
        acc = sb("acc", [P, 2, 1024])
        mx = sb("mx", [P, 2])
        nb = sb("nb", [P, 2])
        rsum = sb("rsum", [P, 2])
        rinv = sb("rinv", [P, 2])
        bst = sb("bst", [P, 2, 2, 6])
        mv = sb("mv", [P, 2, 2])
        vstd = sb("vstd", [P, 2])
        vrs = sb("vrs", [P, 2])
        ps = ctx.enter_context(nc.psum_tensor("ps", [P, 8, 512], f32))

        wsT = gm_w[:, 0:1024]
        bs_rows = gm_w[:, 1024:2048]
        ada_g2 = gm_w
        ident = cst[:, C_IDENT:C_IDENT + P]
        swap = cst[:, C_SWAP:C_SWAP + P]
        freq = cst[:, C_FREQ:C_FREQ + 1]

        def region(lo, n):
            return big[:, lo:lo + n]
        ada_ring = region(0, 8 * UNIT).rearrange("p (s n) -> p s n", s=8)
        rope_a = raw[:, 0, 0:512].rearrange("p (s n) -> p s n", s=2)
        v_tok = region(0, 2048).rearrange("p (t n) -> p t n", t=2)
        u_all = region(2048, 2048)
        u_t = u_all.rearrange("p (t n) -> p t n", n=SEQ)
        q_lat = region(4096, 1024).rearrange("p (t n) -> p t n", n=SEQ)
        kv_lat = region(5120, 512).rearrange("p (t n) -> p t n", n=SEQ)
        prob = region(4096, 768).rearrange("p (s n) -> p s n", s=2)
        probT = region(4864, 768).rearrange("p (s n) -> p s n", s=2)
        k_pe = region(5632, 256)
        qT = region(5888, 2048).rearrange("p (t n) -> p t n", n=SEQ)
        q_pe = region(7936, 1024).rearrange("p (t n) -> p t n", n=SEQ)
        kT = region(8960, 2048).rearrange("p (t n) -> p t n", n=SEQ)
        v_att = region(11008, 2048).rearrange("p (t n) -> p t n", t=2)
        m_all = region(13056, 2048)
        m_t = m_all.rearrange("p (t n) -> p t n", n=SEQ)
        ln_rows = m_all.rearrange("p (t n) -> p t n", t=2)
        rtmp = region(15104, 256)
        y_all = region(6144, 4096)
        y_t = y_all.rearrange("p (t n) -> p t n", n=SEQ)
        f_t = region(0, 4096).rearrange("p (t n) -> p t n", n=SEQ)
        h1 = big

        small_in = sem("small_in")
        x_in = sem("x_in")
        gm_in = sem("gm_in")
        ws_masked = sem("ws_masked")
        ln_in = sem("ln_in")
        raw_in = [sem(f"raw_in{s}") for s in range(RING)]
        ada_in = [sem(f"ada_in{s}") for s in range(8)]
        g2_in = sem("g2_in")
        out_done = sem("out_done")
        consts_ready = sem("consts_ready")
        cs_ready = sem("cs_ready")
        hi_ready = sem("hi_ready")
        lo_ready = sem("lo_ready")
        w_used = sem("w_used")
        ada_pe_used = sem("ada_pe_used")
        ada_dve_used = sem("ada_dve_used")
        ada_used = sem("ada_used")
        acc_ready = sem("acc_ready")
        mod_sum = sem("mod_sum")
        mod_read = sem("mod_read")
        act32_ready = sem("act32_ready")
        ahi_ready = sem("ahi_ready")
        alo_ready = sem("alo_ready")
        sq_ready = sem("sq_ready")
        sq_used = sem("sq_used")
        std_ready = sem("std_ready")
        inv_ready = sem("inv_ready")
        ang_ready = sem("ang_ready")
        trig_ready = sem("trig_ready")
        lat_ready = sem("lat_ready")
        vgelu_ready = sem("vgelu_ready")
        vstat_ready = sem("vstat_ready")
        vstd_ready = sem("vstd_ready")
        vnorm_ready = sem("vnorm_ready")
        latn_ready = sem("latn_ready")
        rope_raw = sem("rope_raw")
        proj_ready = sem("proj_ready")
        proj_out = sem("proj_out")
        b3_ready = sem("b3_ready")
        b3_read = sem("b3_read")
        pe_rot = sem("pe_rot")
        u_out = sem("u_out")
        s_ready = sem("s_ready")
        nb_ready = sem("nb_ready")
        exp_ready = sem("exp_ready")
        p_ready = sem("p_ready")
        pt_ready = sem("pt_ready")
        pt_out = sem("pt_out")
        pv_ready = sem("pv_ready")
        m_out = sem("m_out")
        gelu_u = sem("gelu_u")
        gm_ready = sem("gm_ready")
        gm_out = sem("gm_out")
        y_out = sem("y_out")
        x1_ready = sem("x1_ready")
        z_ready = sem("z_ready")
        relu_ready = sem("relu_ready")
        h1_ready = sem("h1_ready")
        g2_sum = sem("g2_sum")
        g2_ready = sem("g2_ready")
        f_ready = sem("f_ready")
        f_out = sem("f_out")
        o_ready = sem("o_ready")
        act_step = sem("act_step")
        dve_step = sem("dve_step")

        def col(name, t=0, n=1):
            return cols[:, COLS[name][0] + t:COLS[name][0] + t + n]

        def consumer(n):
            if n < N_IN:
                return lo_ready, n + 1
            if n >= N_FF1:
                return lo_ready, W_F1 + n - N_FF1 + 1
            (kind, i), _ = STREAM[n - N_IN]
            if kind == "ada":
                return ada_used, i + 1
            if kind == "kvb":
                return proj_ready, 6 * (i + 1)
            if kind == "qb":
                return proj_ready, 12 + 3 * (i + 1)
            return lo_ready, {"rope": W_ROPE, "u": W_U, "wo": W_O}[kind] + i + 1

        ring_number = {item: N_IN + n for n, (item, _) in enumerate(STREAM)}

        def arrivals(n):
            return 16 * (n // RING + 1)

        def arrived(eng, n):
            eng.wait_ge(raw_in[n % RING], arrivals(n))

        block = ctx.enter_context(nc.Block())

        @block.sync
        def _(sp):
            def load_ada(kp):
                for j in range(4):
                    n = 4 * kp + j
                    c0 = (D if j < 2 else 0) + kp * 256
                    r0 = (j % 2) * 1024
                    if n >= 8:
                        m = n - 8
                        if j < 2:
                            sp.wait_ge(ada_pe_used, 2 * (m // 4) + m % 4 + 1)
                        else:
                            sp.wait_ge(ada_dve_used, 2 * (m // 4) + m % 4 - 1)
                    sp.dma_start(ada_ring[:, n % 8, :].rearrange("p (k c) -> p k c", c=256),
                                 w_ada[r0:r0 + 1024, c0:c0 + 256].rearrange("(k p) c -> p k c", p=P)
                                 ).then_inc(ada_in[n % 8], 16)

            def slot_free(n):
                if n >= RING:
                    sp.wait_ge(*consumer(n - RING))

            def load_in(k):
                slot_free(k)
                sp.dma_start(raw[:, k % RING, 0:1792], w_in[k * P:(k + 1) * P, 1024:2816]
                             ).then_inc(raw_in[k % RING], 16)

            load_ada(0)
            sp.dma_start(xT[:, :, :], A["xT"].rearrange("(t p) n -> p t n", p=P)).then_inc(x_in, 16)
            sp.wait_ge(trig_ready, 2)
            for kp in range(8):
                if kp < 7:
                    load_ada(kp + 1)
                load_in(2 * kp)
                load_in(2 * kp + 1)
            sp.wait_ge(ada_pe_used, 16)
            sp.wait_ge(ada_dve_used, 16)
            for i, name in enumerate(("ln_v_g", "ln_v_b")):
                sp.dma_start(ln_rows[:, i, :], A[name].to_broadcast([P, 1024])).then_inc(ln_in, 16)
            for (kind, i), _ in STREAM:
                n = ring_number[kind, i]
                slot_free(n)
                slot = raw[:, n % RING, :]
                if kind == "rope":
                    dst = slot[:, 0:1024].rearrange("p (k c) -> p k c", c=64)
                    src = w_in[:, 2816:2880].rearrange("(k p) c -> p k c", p=P)
                elif kind in ("u", "wo"):
                    dst = slot.rearrange("p (k c) -> p k c", c=256)
                    r0, c0 = (i % 2) * 1024, (i // 2) * 256
                    src = (w_in if kind == "u" else w_o)[r0:r0 + 1024, c0:c0 + 256].rearrange("(k p) c -> p k c", p=P)
                elif kind == "kvb":
                    dst = slot.rearrange("p (k c) -> p k c", c=1024)
                    src = w_kvb[:, i * 1024:(i + 1) * 1024].rearrange("(k p) c -> p k c", p=P)
                elif kind == "qb":
                    dst = slot[:, 0:1536].rearrange("p (k c) -> p k c", c=384)
                    src = w_qb[:, i * 384:(i + 1) * 384].rearrange("(k p) c -> p k c", p=P)
                else:
                    c0 = ADA_HALVES[i // 8][0]
                    r0 = (i % 8) * 256
                    dst = slot.rearrange("p (k c) -> p k c", c=1024)
                    src = w_ada[r0:r0 + 256, c0:c0 + 1024].rearrange("(k p) c -> p k c", p=P)
                sp.dma_start(dst, src).then_inc(raw_in[n % RING], 16)

            def load_ff1(i, j, after):
                sp.wait_ge(*after)
                s = (N_FF1 + j) % RING
                c0 = i * 512 + (j // 2) * 256
                r0 = (j % 2) * 1024
                sp.dma_start(raw[:, s, :].rearrange("p (k c) -> p k c", c=256),
                             w_ff1[r0:r0 + 1024, bass.ds(c0, 256)].rearrange("(k p) c -> p k c", p=P)
                             ).then_inc(raw_in[s], 16)

            def load_g2(i):
                sp.dma_start(ada_g2[:, :], w_ada[bass.ds(i * P, P), 5 * D:6 * D]).then_inc(g2_in, 16)

            for j in range(4):
                load_ff1(0, j, consumer(N_FF1 + j - RING))
            sp.wait_ge(gm_out, 8)
            load_g2(0)
            with sp.Fori(1, 16) as i:
                for j in range(4):
                    load_ff1(i, j, (lo_ready, i * 4 + (W_F1 + j - 3)))
                sp.wait_ge(ada_used, i + 48)
                load_g2(i)

            def load_ff2(i, j, n):
                sp.wait_ge(lo_ready, n)
                s = (N_FF2 + j) % RING
                sp.dma_start(raw[:, s, :], w_ff2[bass.ds(i * 512 + j * P, P), :]).then_inc(raw_in[s], 16)

            with sp.Fori(0, 16) as i:
                for j in range(4):
                    load_ff2(i, j, i * 4 + (W_F2 + j - 3))
            for g in range(4):
                sp.wait_ge(o_ready, 2 * g + 2)
                sp.dma_start(out[g * 512:(g + 1) * 512, :].rearrange("(t p) n -> p t n", p=P),
                             xT[:, 4 * g:4 * g + 4, :]).then_inc(out_done, 16)
            sp.wait_ge(out_done, 64)

        @block.gpsimd
        def _(pool):
            nc.gpsimd.memset(ones[:, :], 1.0).then_inc(consts_ready, 1)
            nc.gpsimd.memset(eps[:, :], EPS).then_inc(consts_ready, 1)
            pool.wait_ge(consts_ready, 2)
            pool.wait_ge(gm_in, 32)
            nc.gpsimd.memset(wsT.rearrange("p (g i) -> p g i", i=P)[CHUNK:P, :, 0:CHUNK], 0.0).then_inc(ws_masked, 1)

        @block.scalar
        def _(act):
            steps = [0]

            def link(ins):
                steps[0] += 1
                ins.then_inc(act_step, 1)
                act.wait_ge(act_step, steps[0])

            act.dma_start(cols[:, :], A["cols"]).then_inc(small_in, 16)
            act.dma_start(cst[:, :], A["consts"]).then_inc(small_in, 16)
            act.dma_start(h32[:, 0, :].bitcast(i32), A["positions"].to_broadcast([P, SEQ])).then_inc(small_in, 16)
            act.dma_start(wsT, A["w_sT"]).then_inc(gm_in, 16)
            act.dma_start(bs_rows, A["b_s"].to_broadcast([P, 1024])).then_inc(gm_in, 16)
            act.wait_ge(small_in, 48)
            nc.scalar.activation(cs[:, :], col("c", 0, 16), ACT.Silu).then_inc(cs_ready, 1)

            def split_hi(w):
                n = w if w < N_IN else ring_number[("rope", 0) if w == W_ROPE else ("u", w - W_U) if w < W_O
                                                   else ("wo", w - W_O)] if w < W_F1 else N_FF1 + w - W_F1
                arrived(act, n)
                if w >= 2:
                    act.wait_ge(w_used, w - 1)
                src, dst = raw[:, n % RING, :], w_hi[:, w % 2, :]
                if w < N_IN:
                    src, dst = src[:, 0:1792], dst[:, 0:1792]
                elif w == W_ROPE:
                    for r in range(2):
                        ins = nc.scalar.activation(
                            dst.rearrange("p (k r c) -> p k r c", r=2, c=64)[:, :, r, :],
                            src[:, 0:1024].rearrange("p (k c) -> p k c", c=64), ACT.Copy)
                    ins.then_inc(hi_ready, 1)
                    return
                nc.scalar.activation(dst, src, ACT.Copy).then_inc(hi_ready, 1)

            def act_hi(n, slot):
                act.wait_ge(act32_ready, n + 1)
                nc.scalar.activation(a_hi[:, slot, :], h32[:, n % 2, :], ACT.Copy).then_inc(ahi_ready, 1)

            def squares(name, j, src):
                g = NORMS[name][1] + j
                if g >= 2:
                    act.wait_ge(sq_used, g - 1)
                nc.scalar.activation(sqb[:, g % 2, :], src, ACT.Square).then_inc(sq_ready, 1)

            def make_std(name, width, src):
                i, first, chunks = NORMS[name]
                act.wait_ge(sq_used, first + chunks)
                if i:
                    act.wait_ge(inv_ready, i)
                nc.scalar.activation(std[:, :], src, ACT.Sqrt, bias=eps[:, 0:1], scale=1.0 / width).then_inc(std_ready, 1)

            act.wait_ge(ang_ready, 1)
            nc.scalar.activation(sinT[:, :], rope_a[:, 0, :], ACT.Sin).then_inc(trig_ready, 1)
            nc.scalar.activation(cosT[:, :], rope_a[:, 1, :], ACT.Sin).then_inc(trig_ready, 1)
            act.wait_ge(x_in, 16)
            act.wait_ge(consts_ready, 2)
            for j in range(8):
                squares("x", j, xT[:, 2 * j:2 * j + 2, :].rearrange("p t n -> p (t n)"))
            make_std("x", D, ps[:, 0, 0:SEQ])

            for k in range(KT):
                split_hi(k)
                act_hi(k, k)
            split_hi(W_ROPE)
            act.wait_ge(w_used, KT)
            nc.scalar.activation(kv_lat.rearrange("p t n -> p (t n)"), ps[:, 6, :], ACT.Copy).then_inc(lat_ready, 1)
            nc.scalar.activation(q_lat.rearrange("p t n -> p (t n)"), ps[:, 4:6, :].rearrange("p b n -> p (b n)"),
                                 ACT.Copy).then_inc(lat_ready, 1)
            act.wait_ge(lat_ready, 2)
            split_hi(W_U)
            squares("kv", 0, kv_lat.rearrange("p t n -> p (t n)"))
            for j in range(2):
                squares("q", j, q_lat[:, 2 * j:2 * j + 2, :].rearrange("p t n -> p (t n)"))
            nc.scalar.activation(v_tok.rearrange("p t n -> p (t n)"), ps[:, 0:4, :].rearrange("p b n -> p (b n)"),
                                 ACT.Gelu).then_inc(vgelu_ready, 1)
            act.wait_ge(w_used, W_ROPE + 1)
            nc.scalar.activation(k_pe, ps[:, 7, 0:SEQ], ACT.Copy).then_inc(rope_raw, 1)
            make_std("kv", KVL, ps[:, 6, 0:SEQ])
            make_std("q", QL, ps[:, 7, 0:SEQ])
            split_hi(W_U + 1)
            act.wait_ge(vstat_ready, 1)
            nc.scalar.activation(vstd[:, :], mv[:, :, 1], ACT.Sqrt, bias=eps[:, 0:1]).then_inc(vstd_ready, 1)

            def u_evac(p):
                act.wait_ge(w_used, W_U + 2 * p + 2)
                b = 4 + 2 * (p % 2)
                nc.scalar.activation(u_t[:, 2 * p:2 * p + 2, :], ps[:, b:b + 2, 0:SEQ], ACT.Copy).then_inc(u_out, 1)

            proj = [0]

            def proj_evac(dst, width):
                n = proj[0]
                act.wait_ge(proj_ready, n + 1)
                nc.scalar.activation(dst, ps[:, n % 3, 0:width], ACT.Copy).then_inc(proj_out, 1)
                proj[0] += 1

            u_evac(0)
            for g in range(2):
                for h in range(4 * g, 4 * g + 4):
                    proj_evac(kT[:, h, :], SEQ)
                for t in range(2):
                    proj_evac(v_att[:, t, g * 512:(g + 1) * 512], 512)
            for i in range(4):
                proj_evac(q_pe[:, i, :], SEQ)
                proj_evac(qT[:, 2 * i, :], SEQ)
                proj_evac(qT[:, 2 * i + 1, :], SEQ)
            split_hi(W_U + 2)

            def exps(h):
                act.wait_ge(nb_ready, h + 1)
                s = h % 2
                nc.scalar.activation(prob[:, s, 0:128], ps[:, 0, 0:128], ACT.Exp, bias=nb[:, 0:1],
                                     scale=float(QHD) ** -0.5, accum_out=rsum[:, 0:1]).then_inc(exp_ready, 1)
                nc.scalar.activation(prob[:, s, 128:384], ps[:, 0, 128:384], ACT.Exp, bias=nb[:, 1:2],
                                     scale=float(QHD) ** -0.5, accum_out=rsum[:, 1:2]).then_inc(exp_ready, 1)

            def pt_evac(h):
                act.wait_ge(pt_ready, h + 1)
                nc.scalar.activation(probT[:, h % 2, :], ps[:, 1, 0:384], ACT.Copy).then_inc(pt_out, 1)

            def m_evac(h):
                act.wait_ge(pv_ready, h + 1)
                nc.scalar.activation(m_t[:, h, :], ps[:, 2, 0:SEQ], ACT.Copy).then_inc(m_out, 1)

            for j in range(8):
                exps(j)
                if j < 7:
                    split_hi(W_U + 3 + j)
                if j:
                    m_evac(j - 1)
                pt_evac(j)
                if j in (1, 3, 5):
                    u_evac((j + 1) // 2)
                if j == 5:
                    act.wait_ge(u_out, 4)
                    nc.scalar.activation(u_all, u_all, ACT.Gelu).then_inc(gelu_u, 1)
            m_evac(7)
            act.wait_ge(gm_out, 8)
            for j in range(4):
                squares("a", j, u_all[:, j * 512:(j + 1) * 512])
            make_std("a", GW, ps[:, 1, 0:SEQ])
            act.wait_ge(m_out, 8)
            for j in range(4):
                squares("m", j, m_all[:, j * 512:(j + 1) * 512])
            make_std("m", GW, ps[:, 0, 0:SEQ])
            for t in range(16):
                act_hi(16 + t, t)

            def y_evac(p):
                act.wait_ge(w_used, W_O + 2 * p + 2)
                b = 4 + 2 * (p % 2)
                nc.scalar.activation(y_t[:, 2 * p:2 * p + 2, :], ps[:, b:b + 2, 0:SEQ], ACT.Copy).then_inc(y_out, 1)
                act.wait_ge(y_out, p + 1)
                squares("y", p, y_all[:, p * 512:(p + 1) * 512])

            for i in range(2, 16):
                split_hi(W_O + i)
                if i % 2 and i >= 3:
                    y_evac((i - 3) // 2)
            split_hi(W_F1)
            y_evac(7)
            split_hi(W_F1 + 1)
            make_std("y", D, ps[:, 2, 0:SEQ])
            for j in range(8):
                act.wait_ge(x1_ready, j + 1)
                squares("x1", j, xT[:, 2 * j:2 * j + 2, :].rearrange("p t n -> p (t n)"))
            make_std("x1", D, ps[:, 1, 0:SEQ])
            for t in range(16):
                act_hi(32 + t, t)

            def ff_hi(s_unit, arrived_at, used):
                s, w = s_unit
                act.wait_ge(raw_in[s], arrived_at)
                act.wait_ge(w_used, used)
                nc.scalar.activation(w_hi[:, w, :], raw[:, s, :], ACT.Copy).then_inc(hi_ready, 1)

            def slots(n0, w0, j):
                return (n0 + j) % RING, (w0 + j) % 2

            def relu2(i, t):
                if t % 2 == 0:
                    act.wait_ge(z_ready, i * 2 + (t // 2 + 1))
                else:
                    act.wait_ge(w_used, i * 4 + (W_F1 + t + 1))
                relu = sqb[:, t // 2, (t % 2) * SEQ:(t % 2 + 1) * SEQ]
                nc.scalar.activation(relu, ps[:, t, 0:SEQ], ACT.Relu).then_inc(relu_ready, 1)
                act.wait_ge(relu_ready, i * 4 + (t + 1))
                act.wait_ge(x1_ready, 8)
                nc.scalar.activation(h1[:, bass.ds(i * 1024 + t * SEQ, SEQ)], relu, ACT.Square).then_inc(h1_ready, 1)

            with act.Fori(0, 16) as i:
                for j in (2, 3):
                    ff_hi(slots(N_FF1, W_F1, j), i * 16 + arrivals(N_FF1 + j), i * 4 + (W_F1 + j - 1))
                relu2(i, 0)
                relu2(i, 1)
                for j in (4, 5):
                    ff_hi(slots(N_FF1, W_F1, j), i * 16 + arrivals(N_FF1 + j), i * 4 + (W_F1 + j - 1))
                relu2(i, 2)
                relu2(i, 3)

            def h_hi(i, j, used):
                act.wait_ge(w_used, used)
                act.wait_ge(h1_ready, 64)
                nc.scalar.activation(a_hi[:, j % 4, :], h1[:, bass.ds(i * 1024 + j * SEQ, SEQ)], ACT.Copy).then_inc(ahi_ready, 1)

            for j in range(2):
                h_hi(0, j, W_F2)
            with act.Fori(0, 15) as i:
                for j in range(2, 6):
                    h_hi(i, j, i * 4 + (W_F2 + j - 3))
                    ff_hi(slots(N_FF2, W_F2, j), i * 16 + arrivals(N_FF2 + j), i * 4 + (W_F2 + j - 1))
            for j in range(2, 4):
                h_hi(15, j, W_F2 + 60 + j - 3)
                ff_hi(slots(N_FF2, W_F2, 60 + j), arrivals(N_FF2 + 60 + j), W_F2 + 60 + j - 1)
            for b in range(8):
                act.wait_ge(f_ready, b + 1)
                nc.scalar.activation(f_t[:, 2 * b:2 * b + 2, :].rearrange("p t n -> p (t n)"), ps[:, b, :],
                                     ACT.Copy).then_inc(f_out, 1)
                act.wait_ge(f_out, b + 1)
                squares("f", b, f_t[:, 2 * b:2 * b + 2, :].rearrange("p t n -> p (t n)"))
            make_std("f", D, ps[:, 0, 0:SEQ])

        @block.vector
        def _(dve):
            steps = [0]

            def link(ins):
                steps[0] += 1
                ins.then_inc(dve_step, 1)
                dve.wait_ge(dve_step, steps[0])

            V = nc.vector
            dve.wait_ge(small_in, 48)
            ang, t0 = rope_a[:, 0, :], rope_a[:, 1, :]
            link(V.tensor_copy(ang, h32[:, 0, :].bitcast(i32)))
            link(V.tensor_scalar(ang, ang, freq, None, ALU.mult))
            for turns in (4096.0, 1.0):
                link(V.tensor_scalar(t0, ang, 1.0 / (turns * 6.283185307179586), ROUND, ALU.mult, ALU.add))
                link(V.tensor_scalar(t0, t0, ROUND, None, ALU.subtract))
                for piece in TWO_PI:
                    link(V.scalar_tensor_tensor(out=ang, in0=t0, scalar=-turns * piece, in1=ang,
                                                op0=ALU.mult, op1=ALU.add))
            link(V.tensor_scalar(ang, ang, PI, -PI, ALU.min, ALU.max))
            link(V.tensor_scalar(t0, ang, -1.0, None, ALU.mult))
            link(V.tensor_tensor(t0, t0, ang, ALU.min))
            V.tensor_scalar(t0, t0, 1.5707963267948966, None, ALU.add).then_inc(ang_ready, 1)

            def ada_shift(kp):
                a = acc[:, 0, (kp % 2) * 256:(kp % 2) * 256 + 256]
                for j in range(2):
                    n = 4 * kp + 2 + j
                    dve.wait_ge(ada_in[n % 8], 16 * (n // 8 + 1))
                    for k in range(8):
                        src = ada_ring[:, n % 8, k * 256:(k + 1) * 256]
                        c = cs[:, 8 * j + k:8 * j + k + 1]
                        if j == 0 and k == 0:
                            if kp >= 2:
                                dve.wait_ge(mod_sum, kp - 1)
                            link(V.tensor_scalar(a, src, c, None, ALU.mult))
                        elif k == 7:
                            V.scalar_tensor_tensor(out=a, in0=src, scalar=c, in1=a, op0=ALU.mult,
                                                   op1=ALU.add).then_inc(ada_dve_used, 1)
                            dve.wait_ge(ada_dve_used, 2 * kp + j + 1)
                        else:
                            link(V.scalar_tensor_tensor(out=a, in0=src, scalar=c, in1=a, op0=ALU.mult, op1=ALU.add))

            def make_inv(name):
                i = NORMS[name][0]
                dve.wait_ge(std_ready, i + 1)
                V.reciprocal(R[:, :], std[:, :]).then_inc(inv_ready, 1)
                dve.wait_ge(inv_ready, i + 1)

            def act_lo(n, slot):
                dve.wait_ge(ahi_ready, n + 1)
                V.tensor_tensor(a_lo[:, slot, :], h32[:, n % 2, :], a_hi[:, slot, :].bitcast(f32),
                                ALU.subtract).then_inc(alo_ready, 1)

            def modulated(n, t, gain, shift0):
                h = h32[:, n % 2, :]
                if n >= 2:
                    dve.wait_ge(alo_ready, n - 1)
                link(V.scalar_tensor_tensor(out=h, in0=xT[:, t, :], scalar=gain[:, t:t + 1], in1=R[:, :],
                                            op0=ALU.mult, op1=ALU.mult))
                V.tensor_scalar(h, h, mods[:, shift0 + t:shift0 + t + 1], None, ALU.add).then_inc(act32_ready, 1)

            def split_lo(w):
                n = w if w < N_IN else ring_number[("rope", 0) if w == W_ROPE else ("u", w - W_U) if w < W_O
                                                   else ("wo", w - W_O)] if w < W_F1 else N_FF1 + w - W_F1
                dve.wait_ge(hi_ready, w + 1)
                if w >= 2:
                    dve.wait_ge(w_used, w - 1)
                src, hi, lo = raw[:, n % RING, :], w_hi[:, w % 2, :].bitcast(f32), w_lo[:, w % 2, :]
                if w < N_IN:
                    src, hi, lo = src[:, 0:1792], hi[:, 0:1792], lo[:, 0:1792]
                elif w == W_ROPE:
                    src = src[:, 0:1024].rearrange("p (k c) -> p k c", c=64)
                    hi = hi.rearrange("p (k r c) -> p k r c", r=2, c=64)
                    lo = lo.rearrange("p (k r c) -> p k r c", r=2, c=64)
                    for r in range(2):
                        ins = V.tensor_tensor(lo[:, :, r, :], src, hi[:, :, r, :], ALU.subtract)
                    ins.then_inc(lo_ready, 1)
                    return
                V.tensor_tensor(lo, src, hi, ALU.subtract).then_inc(lo_ready, 1)

            dve.wait_ge(cs_ready, 1)
            ada_shift(0)
            make_inv("x")

            def modulation(kp):
                dve.wait_ge(mod_sum, kp + 1)
                t = 2 * kp
                V.tensor_tensor(mods[:, 16 + t:18 + t], ps[:, 7, 0:2], col("b_ada", 16 + t, 2), ALU.add)
                V.tensor_tensor(mods[:, t:t + 2], ps[:, 7, 2:4], col("b_ada", t, 2), ALU.add).then_inc(mod_read, 1)
                dve.wait_ge(mod_read, kp + 1)
                link(V.scalar_tensor_tensor(out=gain1[:, t:t + 2], in0=mods[:, 16 + t:18 + t], scalar=1.0,
                                            in1=col("pre1", t, 2), op0=ALU.add, op1=ALU.mult))

            for kp in range(8):
                if kp < 7:
                    ada_shift(kp + 1)
                modulation(kp)
                modulated(2 * kp, 2 * kp, gain1, 0)
                modulated(2 * kp + 1, 2 * kp + 1, gain1, 0)
                split_lo(2 * kp)
                act_lo(2 * kp, 2 * kp)
                split_lo(2 * kp + 1)
                act_lo(2 * kp + 1, 2 * kp + 1)

            def ada_unit(i):
                hp, r = i // 8, i % 8
                n = ring_number["ada", i]
                arrived(dve, n)
                a = acc[:, hp % 2, :]
                if r == 0:
                    if hp < 2:
                        dve.wait_ge(mod_sum, 8)
                    else:
                        dve.wait_ge(b3_ready, CONV_B3[hp - 2] + 1)
                for k in range(2):
                    src = raw[:, n % RING, k * 1024:(k + 1) * 1024]
                    c = cs[:, 2 * r + k:2 * r + k + 1]
                    if r == 0 and k == 0:
                        link(V.tensor_scalar(a, src, c, None, ALU.mult))
                    elif k == 0:
                        link(V.scalar_tensor_tensor(out=a, in0=src, scalar=c, in1=a, op0=ALU.mult, op1=ALU.add))
                    else:
                        V.scalar_tensor_tensor(out=a, in0=src, scalar=c, in1=a, op0=ALU.mult,
                                               op1=ALU.add).then_inc(ada_used, 1)
                        dve.wait_ge(ada_used, i + 1)

            def process(idx):
                kind, i = ITEMS[idx]
                if kind in ("rope", "u", "wo"):
                    split_lo({"rope": W_ROPE, "u": W_U, "wo": W_O}[kind] + i)
                for (k2, i2), at in STREAM:
                    if k2 == "ada" and at == idx:
                        ada_unit(i2)

            def rotate(b3, dst):
                dve.wait_ge(b3_ready, b3 + 1)
                if b3:
                    dve.wait_ge(pe_rot, b3 - 1)
                V.tensor_tensor(rtmp, ps[:, 3, 0:SEQ], sinT[:, :], ALU.mult).then_inc(b3_read, 1)
                dve.wait_ge(b3_read, b3 + 1)
                link(V.tensor_tensor(dst, dst, cosT[:, :], ALU.mult))
                V.tensor_tensor(dst, dst, rtmp, ALU.add).then_inc(pe_rot, 1)

            def conv_read(hp):
                b3 = CONV_B3[hp]
                m0 = ADA_HALVES[hp][1]
                dve.wait_ge(b3_ready, b3 + 1)
                V.tensor_tensor(mods[:, m0:m0 + 8], ps[:, 3, 0:8], col("b_ada", m0, 8), ALU.add).then_inc(b3_read, 1)
                dve.wait_ge(b3_read, b3 + 1)

            process(0)
            process(1)
            make_inv("kv")
            for t in range(2):
                V.scalar_tensor_tensor(out=kv_lat[:, t, :], in0=kv_lat[:, t, :], scalar=col("kvn", t), in1=R[:, :],
                                       op0=ALU.mult, op1=ALU.mult).then_inc(latn_ready, 1)
            dve.wait_ge(latn_ready, 2)
            make_inv("q")
            for t in range(4):
                V.scalar_tensor_tensor(out=q_lat[:, t, :], in0=q_lat[:, t, :], scalar=col("qn", t), in1=R[:, :],
                                       op0=ALU.mult, op1=ALU.mult).then_inc(latn_ready, 1)
            dve.wait_ge(vgelu_ready, 1)
            for t in range(2):
                for j in range(2):
                    link(V.bn_stats(bst[:, t, j, :], v_tok[:, t, j * 512:(j + 1) * 512]))
            V.bn_aggr(mv[:, 0, :], bst[:, 0, :, :].rearrange("p a b -> p (a b)"))
            V.bn_aggr(mv[:, 1, :], bst[:, 1, :, :].rearrange("p a b -> p (a b)")).then_inc(vstat_ready, 1)
            process(2)
            dve.wait_ge(vstd_ready, 1)
            link(V.reciprocal(vrs[:, :], vstd[:, :]))
            dve.wait_ge(ln_in, 32)
            for t in range(2):
                link(V.tensor_scalar(v_tok[:, t, :], v_tok[:, t, :], mv[:, t, 0:1], vrs[:, t:t + 1],
                                     ALU.subtract, ALU.mult))
                link(V.tensor_tensor(v_tok[:, t, :], v_tok[:, t, :], ln_rows[:, 0, :], ALU.mult))
                V.tensor_tensor(v_tok[:, t, :], v_tok[:, t, :], ln_rows[:, 1, :], ALU.add).then_inc(vnorm_ready, 1)
            process(3)
            process(4)
            rotate(0, k_pe)
            process(5)
            process(6)
            conv_read(0)
            rotate(2, q_pe[:, 0, :])
            process(7)
            rotate(3, q_pe[:, 1, :])
            process(8)
            process(9)
            rotate(4, q_pe[:, 2, :])
            rotate(5, q_pe[:, 3, :])

            def row_max(h):
                dve.wait_ge(s_ready, h + 1)
                if h:
                    dve.wait_ge(exp_ready, 2 * h)
                V.memset(ps[0:64, 0, 64:128], NEG)
                link(V.memset(ps[0:64, 0, 320:384], NEG))
                V.reduce_max(mx[:, 0:1], ps[:, 0, 0:128], AX.X)
                link(V.reduce_max(mx[:, 1:2], ps[:, 0, 128:384], AX.X))
                V.tensor_scalar(nb[:, :], mx[:, :], -float(QHD) ** -0.5, None, ALU.mult).then_inc(nb_ready, 1)

            def normalise(h):
                dve.wait_ge(exp_ready, 2 * h + 2)
                link(V.reciprocal(rinv[:, :], rsum[:, :]))
                p = prob[:, h % 2, :]
                V.tensor_scalar(p[:, 0:128], p[:, 0:128], rinv[:, 0:1], None, ALU.mult)
                V.tensor_scalar(p[:, 128:384], p[:, 128:384], rinv[:, 1:2], None, ALU.mult).then_inc(p_ready, 1)

            def gate_u(g):
                t = h32[:, g % 2, :]
                if g >= 2:
                    dve.wait_ge(gm_out, g - 1)
                link(V.tensor_tensor(t.rearrange("p (n i) -> p n i", i=128),
                                     ps[:, 4 + g // 2, (g % 2) * 256:(g % 2) * 256 + 256].rearrange("p (n i) -> p n i", i=128),
                                     bs_rows[:, g * 128:(g + 1) * 128].rearrange("p (n i) -> p n i", n=1).to_broadcast([P, 2, 128]),
                                     ALU.add))
                V.tensor_tensor(u_t[:, g, :], t, u_t[:, g, :], ALU.mult).then_inc(gm_out, 1)

            for j in range(8):
                row_max(j)
                if j < 7:
                    process(10 + j)
                normalise(j)
                if j == 1:
                    conv_read(1)
                if j == 5:
                    conv_read(2)
                if j == 6:
                    dve.wait_ge(gm_ready, 1)
                    dve.wait_ge(gelu_u, 1)
                    dve.wait_ge(gm_in, 32)
                    for g in range(4):
                        gate_u(g)
            dve.wait_ge(gm_ready, 2)
            for g in range(4, 8):
                gate_u(g)

            def normed(name, n0, slot0, src, gain):
                for t in range(8):
                    dve.wait_ge(alo_ready, n0 + t - 1)
                    V.scalar_tensor_tensor(out=h32[:, t % 2, :], in0=src[:, t, :], scalar=col(gain, t), in1=R[:, :],
                                           op0=ALU.mult, op1=ALU.mult).then_inc(act32_ready, 1)
                    if t:
                        act_lo(n0 + t - 1, slot0 + t - 1)
                act_lo(n0 + 7, slot0 + 7)

            make_inv("a")
            dve.wait_ge(w_used, W_O)
            normed("a", 16, 0, u_t, "ga")
            make_inv("m")
            normed("m", 24, 8, m_t, "gb")
            for i in range(17, 31):
                process(i)
                if i == 18:
                    conv_read(3)
                if i == 25:
                    conv_read(4)
            split_lo(W_F1)
            conv_read(5)
            split_lo(W_F1 + 1)
            link(V.tensor_tensor(gate1[:, :], mods[:, 32:48], col("post1", 0, 16), ALU.mult))
            link(V.scalar_tensor_tensor(out=gain2[:, :], in0=mods[:, 64:80], scalar=1.0, in1=col("pre2", 0, 16),
                                        op0=ALU.add, op1=ALU.mult))
            make_inv("y")
            for j in range(8):
                for t in (2 * j, 2 * j + 1):
                    link(V.scalar_tensor_tensor(out=y_t[:, t, :], in0=y_t[:, t, :], scalar=gate1[:, t:t + 1],
                                                in1=R[:, :], op0=ALU.mult, op1=ALU.mult))
                x2 = xT[:, 2 * j:2 * j + 2, :].rearrange("p t n -> p (t n)")
                V.tensor_tensor(x2, x2, y_all[:, j * 512:(j + 1) * 512], ALU.add).then_inc(x1_ready, 1)
            make_inv("x1")
            for t in range(16):
                modulated(32 + t, t, gain2, 48)
                if t:
                    act_lo(31 + t, t - 1)
            act_lo(47, 15)

            def ff_lo(s_unit, hi, used):
                s, w = s_unit
                dve.wait_ge(hi_ready, hi)
                dve.wait_ge(w_used, used)
                V.tensor_tensor(w_lo[:, w, :], raw[:, s, :], w_hi[:, w, :].bitcast(f32), ALU.subtract).then_inc(lo_ready, 1)

            def slots(n0, w0, j):
                return (n0 + j) % RING, (w0 + j) % 2

            acc_all = acc[:, :, :].rearrange("p a n -> p (a n)")
            link(V.memset(acc_all, 0.0))
            with dve.Fori(0, 16) as i:
                for j in (2, 3):
                    ff_lo(slots(N_FF1, W_F1, j), i * 4 + (W_F1 + j + 1), i * 4 + (W_F1 + j - 1))
                dve.wait_ge(g2_in, i * 16 + 16)
                V.scalar_tensor_tensor(out=acc_all, in0=ada_g2[:, :], scalar=cs[:, bass.ds(i, 1)], in1=acc_all,
                                       op0=ALU.mult, op1=ALU.add).then_inc(ada_used, 1)
                dve.wait_ge(ada_used, i + 49)
                for j in (4, 5):
                    ff_lo(slots(N_FF1, W_F1, j), i * 4 + (W_F1 + j + 1), i * 4 + (W_F1 + j - 1))
            dve.wait_ge(g2_sum, 1)
            V.tensor_tensor(mods[:, 80:96], ps[:, 7, 0:16], col("b_ada", 80, 16), ALU.add).then_inc(g2_ready, 1)
            dve.wait_ge(g2_ready, 1)
            link(V.tensor_tensor(gate2[:, :], mods[:, 80:96], col("post2", 0, 16), ALU.mult))

            def h_lo(i, j, n):
                dve.wait_ge(ahi_ready, n)
                V.tensor_tensor(a_lo[:, j % 4, :], h1[:, bass.ds(i * 1024 + j * SEQ, SEQ)], a_hi[:, j % 4, :].bitcast(f32),
                                ALU.subtract).then_inc(alo_ready, 1)

            for j in range(2):
                h_lo(0, j, 49 + j)
            with dve.Fori(0, 15) as i:
                for j in range(2, 6):
                    h_lo(i, j, i * 4 + (49 + j))
                    ff_lo(slots(N_FF2, W_F2, j), i * 4 + (W_F2 + j + 1), i * 4 + (W_F2 + j - 1))
            for j in range(2, 4):
                h_lo(15, j, 48 + 60 + j + 1)
                ff_lo(slots(N_FF2, W_F2, 60 + j), W_F2 + 60 + j + 1, W_F2 + 60 + j - 1)
            make_inv("f")
            for j in range(8):
                for t in (2 * j, 2 * j + 1):
                    link(V.scalar_tensor_tensor(out=f_t[:, t, :], in0=f_t[:, t, :], scalar=gate2[:, t:t + 1],
                                                in1=R[:, :], op0=ALU.mult, op1=ALU.mult))
                x2 = xT[:, 2 * j:2 * j + 2, :].rearrange("p t n -> p (t n)")
                V.tensor_tensor(x2, x2, f_t[:, 2 * j:2 * j + 2, :].rearrange("p t n -> p (t n)"),
                                ALU.add).then_inc(o_ready, 1)

        @block.tensor
        def _(pe):
            mm = nc.tensor.matmul

            def add_squares(name, j, dst):
                _, first, chunks = NORMS[name]
                g = first + j
                pe.wait_ge(sq_ready, g + 1)
                for t in range(2):
                    ins = mm(dst, ones[:, :], sqb[:, g % 2, t * SEQ:(t + 1) * SEQ],
                             start=(j == 0 and t == 0), stop=(j == chunks - 1 and t == 1))
                ins.then_inc(sq_used, 1)

            def ada(kp):
                if kp:
                    pe.wait_ge(mod_read, kp)
                for q in range(2):
                    n = 4 * kp + q
                    pe.wait_ge(ada_in[n % 8], 16 * (n // 8 + 1))
                    for j in range(2):
                        for k in range(8):
                            ins = mm(ps[:, 7, j:j + 1], ada_ring[:, n % 8, k * 256 + j * P:k * 256 + (j + 1) * P],
                                     cs[:, 8 * q + k:8 * q + k + 1], start=(q == 0 and j == 0 and k == 0),
                                     stop=(q == 1 and k == 7), skip_group_check=True)
                    ins.then_inc(ada_pe_used, 1)
                pe.wait_ge(ada_dve_used, 2 * kp + 2)
                for j in range(2):
                    ins = mm(ps[:, 7, 2 + j:3 + j], acc[:, 0, (kp % 2) * 256 + j * P:(kp % 2) * 256 + (j + 1) * P],
                             ones[:, 0:1], start=False, stop=True, skip_group_check=True)
                ins.then_inc(mod_sum, 1)

            def three(dst, w, a, start, stop, stationary_weights=True):
                (wh, wl), (ah, al) = w, a
                for n, (x, y) in enumerate(((wh, ah), (wh, al), (wl, ah)) if stationary_weights else
                                           ((ah, wh), (ah, wl), (al, wh))):
                    ins = mm(dst, x, y, start=(start and n == 0), stop=(stop and n == 2), skip_group_check=True)
                return ins

            def in_rows(k):
                s = k % 2
                pe.wait_ge(lo_ready, k + 1)
                pe.wait_ge(alo_ready, k + 1)
                for t in range(2):
                    a = (a_hi[:, k, t * P:(t + 1) * P], a_lo[:, k, t * P:(t + 1) * P])
                    for n in range(2):
                        w = (w_hi[:, s, n * 512:(n + 1) * 512], w_lo[:, s, n * 512:(n + 1) * 512])
                        three(ps[:, 2 * t + n, :], w, a, k == 0, k == KT - 1, stationary_weights=False)
                for f in range(6):
                    c = 1024 + f * P
                    ins = three(ps[:, 4 + f // 2, (f % 2) * SEQ:(f % 2 + 1) * SEQ],
                                (w_hi[:, s, c:c + P], w_lo[:, s, c:c + P]), (a_hi[:, k, :], a_lo[:, k, :]),
                                k == 0 and f % 2 == 0, k == KT - 1)
                ins.then_inc(w_used, 1)

            pe.wait_ge(cs_ready, 1)
            pe.wait_ge(consts_ready, 2)
            ada(0)
            for j in range(8):
                add_squares("x", j, ps[:, 0, 0:SEQ])
            for kp in range(8):
                if kp < 7:
                    ada(kp + 1)
                in_rows(2 * kp)
                in_rows(2 * kp + 1)

            pe.wait_ge(lo_ready, W_ROPE + 1)
            pe.wait_ge(mod_read, 8)
            s = W_ROPE % 2
            for k in range(KT):
                ins = three(ps[:, 7, 0:SEQ], (w_hi[:, s, k * P:(k + 1) * P], w_lo[:, s, k * P:(k + 1) * P]),
                            (a_hi[:, k, :], a_lo[:, k, :]), k == 0, k == KT - 1)
            ins.then_inc(w_used, 1)

            def pair_unit(w, q, bank, act_tiles=None):
                pe.wait_ge(lo_ready, w + 1)
                for j in range(2):
                    for k in range(8):
                        if act_tiles is not None and j == 0:
                            pe.wait_ge(alo_ready, act_tiles + 8 * q + k + 1)
                        c = k * 256 + j * P
                        ins = three(ps[:, bank + j, 0:SEQ], (w_hi[:, w % 2, c:c + P], w_lo[:, w % 2, c:c + P]),
                                    (a_hi[:, 8 * q + k, :], a_lo[:, 8 * q + k, :]),
                                    q == 0 and k == 0, q == 1 and k == 7)
                ins.then_inc(w_used, 1)

            def u_unit(i):
                if i == 0:
                    pe.wait_ge(lat_ready, 2)
                if i == 2:
                    pe.wait_ge(rope_raw, 1)
                    pe.wait_ge(std_ready, 3)
                if i in (4, 6):
                    pe.wait_ge(u_out, i // 2 - 1)
                pair_unit(W_U + i, i % 2, 4 + 2 * ((i // 2) % 2))

            b3 = [0]

            def take_b3():
                if b3[0]:
                    pe.wait_ge(b3_read, b3[0])
                b3[0] += 1

            def conv(hp):
                take_b3()
                pe.wait_ge(ada_used, 8 * (hp + 1))
                for f in range(8):
                    ins = mm(ps[:, 3, f:f + 1], acc[:, hp % 2, f * P:(f + 1) * P], ones[:, 0:1], start=True, stop=True)
                ins.then_inc(b3_ready, 1)

            def swap_halves(src, n):
                take_b3()
                if n is None:
                    pe.wait_ge(rope_raw, 1)
                else:
                    pe.wait_ge(proj_out, n)
                mm(ps[:, 3, 0:SEQ], swap, src, start=True, stop=True).then_inc(b3_ready, 1)

            proj = [0]

            def project(terms, width):
                n = proj[0]
                if n >= 3:
                    pe.wait_ge(proj_out, n - 2)
                dst = ps[:, n % 3, 0:width]
                for m, (x, y) in enumerate(terms):
                    ins = mm(dst, x, y, start=(m == 0), stop=(m == len(terms) - 1))
                ins.then_inc(proj_ready, 1)
                proj[0] += 1
                return ins

            def kvb_unit(g):
                n = ring_number["kvb", g]
                arrived(pe, n)
                w = raw[:, n % RING, :].rearrange("p (k h c) -> p k h c", k=2, c=NOPE + VD)
                for h in range(4):
                    project([(w[:, k, h, 0:NOPE], kv_lat[:, k, :]) for k in range(2)], SEQ)
                for t in range(2):
                    m = proj[0]
                    pe.wait_ge(proj_out, m - 2)
                    for k in range(2):
                        ins = mm(ps[:, m % 3, :].rearrange("p (h c) -> p h c", c=P), kv_lat[:, k, t * P:(t + 1) * P],
                                 w[:, k, :, NOPE:NOPE + VD], start=(k == 0), stop=(k == 1))
                    ins.then_inc(proj_ready, 1)
                    proj[0] += 1

            def qb_unit(i):
                n = ring_number["qb", i]
                arrived(pe, n)
                w = raw[:, n % RING, 0:1536].rearrange("p (k c) -> p k c", k=4)
                m = proj[0]
                pe.wait_ge(proj_out, m - 2)
                for k in range(4):
                    ins = mm(ps[:, m % 3, 0:SEQ], w[:, k, 2 * NOPE:2 * QHD], q_lat[:, k, :], start=(k == 0), stop=(k == 3))
                ins.then_inc(proj_ready, 1)
                proj[0] += 1
                for h in range(2):
                    project([(w[:, k, h * NOPE:(h + 1) * NOPE], q_lat[:, k, :]) for k in range(4)], SEQ)

            u_unit(0)
            add_squares("kv", 0, ps[:, 6, 0:SEQ])
            for j in range(2):
                if j == 0:
                    pe.wait_ge(rope_raw, 1)
                add_squares("q", j, ps[:, 7, 0:SEQ])
            u_unit(1)
            pe.wait_ge(vgelu_ready, 1)
            pe.wait_ge(latn_ready, 2)
            kvb_unit(0)
            swap_halves(k_pe, None)
            kvb_unit(1)
            pe.wait_ge(latn_ready, 6)
            qb_unit(0)
            conv(0)
            qb_unit(1)
            swap_halves(q_pe[:, 0, :], 13)
            qb_unit(2)
            swap_halves(q_pe[:, 1, :], 16)
            qb_unit(3)
            swap_halves(q_pe[:, 2, :], 19)
            swap_halves(q_pe[:, 3, :], 22)

            def scores(h):
                r = (h % 2) * 64
                if h:
                    pe.wait_ge(exp_ready, 2 * h)
                else:
                    pe.wait_ge(proj_out, 24)
                pe.wait_ge(pe_rot, 2 + h // 2)
                for b in range(2):
                    dst = ps[:, 0, 128 * b:128 + 256 * b]
                    keys = P * (b + 1)
                    mm(dst, qT[:, h, b * P:(b + 1) * P], kT[:, h, 0:keys], start=True, stop=False)
                    ins = mm(dst, q_pe[r:r + 64, h // 2, b * P:(b + 1) * P], k_pe[r:r + 64, 0:keys],
                             start=False, stop=True)
                ins.then_inc(s_ready, 1)

            def transposes(h):
                pe.wait_ge(p_ready, h + 1)
                if h:
                    pe.wait_ge(pt_out, h)
                for b in range(3):
                    ins = nc.tensor.transpose(ps[:, 1, b * P:(b + 1) * P], prob[:, h % 2, b * P:(b + 1) * P], ident)
                ins.then_inc(pt_ready, 1)

            def values(h):
                pe.wait_ge(pt_out, h + 1)
                if h:
                    pe.wait_ge(m_out, h)
                pt = probT[:, h % 2, :]
                mm(ps[:, 2, 0:SEQ], v_att[:, 0, h * P:(h + 1) * P], pt[:, 0:256], start=True, stop=False,
                   skip_group_check=True)
                mm(ps[:, 2, P:SEQ], v_att[:, 1, h * P:(h + 1) * P], pt[:, 256:384], start=False, stop=True,
                   skip_group_check=True).then_inc(pv_ready, 1)

            def spatial(half):
                if half == 0:
                    pe.wait_ge(vnorm_ready, 2)
                    pe.wait_ge(ws_masked, 1)
                    pe.wait_ge(u_out, 3)
                else:
                    pe.wait_ge(u_out, 4)
                for g in range(4 * half, 4 * half + 4):
                    for n in range(2):
                        c = (g % 2) * 256 + n * P
                        ins = mm(ps[:, 4 + g // 2, c:c + P], v_tok[:, n, g * P:(g + 1) * P],
                                 wsT[:, g * P:(g + 1) * P], start=True, stop=True)
                ins.then_inc(gm_ready, 1)

            for j in range(8):
                scores(j)
                if j < 6:
                    u_unit(2 + j)
                else:
                    spatial(j - 6)
                if j:
                    values(j - 1)
                transposes(j)
                if j == 0:
                    conv(1)
                if j == 4:
                    conv(2)
            values(7)
            pe.wait_ge(pt_out, 8)
            for j in range(4):
                add_squares("a", j, ps[:, 1, 0:SEQ])
            for j in range(4):
                add_squares("m", j, ps[:, 0, 0:SEQ])

            for i in range(16):
                p = i // 2
                if p < 2:
                    pe.wait_ge(gm_out, 8)
                elif i % 2 == 0:
                    pe.wait_ge(y_out, p - 1)
                pair_unit(W_O + i, i % 2, 4 + 2 * (p % 2), act_tiles=16 if i < 2 else None)
                if i % 2 and p:
                    if p == 1:
                        pe.wait_ge(m_out, 8)
                    add_squares("y", p - 1, ps[:, 2, 0:SEQ])
                if 15 + i in CONV_AFTER:
                    conv(CONV_AFTER[15 + i])
            add_squares("y", 7, ps[:, 2, 0:SEQ])
            pe.wait_ge(std_ready, 4)
            for j in range(8):
                add_squares("x1", j, ps[:, 1, 0:SEQ])

            def ff1_unit(i, j, w_wait, bank_wait, act_waits):
                w = (W_F1 + j) % 2
                q = j % 2
                pe.wait_ge(lo_ready, w_wait)
                if bank_wait is not None:
                    pe.wait_ge(h1_ready, bank_wait)
                for c in range(2):
                    for k in range(8):
                        if act_waits and c == 0:
                            pe.wait_ge(alo_ready, 32 + 8 * q + k + 1)
                        o = k * 256 + c * P
                        ins = three(ps[:, 2 * (j // 2) + c, 0:SEQ], (w_hi[:, w, o:o + P], w_lo[:, w, o:o + P]),
                                    (a_hi[:, 8 * q + k, :], a_lo[:, 8 * q + k, :]),
                                    q == 0 and k == 0, q == 1 and k == 7)
                        if q == 1 and k == 7 and c == 0:
                            ins.then_inc(z_ready, 1)
                ins.then_inc(w_used, 1)

            pe.wait_ge(std_ready, 7)
            pe.wait_ge(b3_read, 11)
            for j in range(4):
                ff1_unit(0, j, W_F1 + j + 1, None, j < 2)
            with pe.Fori(1, 16) as i:
                for j in range(4):
                    ff1_unit(i, j, i * 4 + (W_F1 + j + 1), i * 4 + (2 * (j // 2) - 2) if j % 2 == 0 else None, False)

            pe.wait_ge(ada_used, 64)
            for f in range(16):
                ins = mm(ps[:, 7, f:f + 1], acc[:, f // 8, (f % 8) * P:(f % 8 + 1) * P], ones[:, 0:1],
                         start=True, stop=True)
            ins.then_inc(g2_sum, 1)

            def ff2_dst(d):
                return ps[:, d // 2, (d % 2) * SEQ:(d % 2 + 1) * SEQ]

            def ff2_part(w, j, d, first, last):
                return three(ff2_dst(d), (w_hi[:, w, d * P:(d + 1) * P], w_lo[:, w, d * P:(d + 1) * P]),
                             (a_hi[:, j, :], a_lo[:, j, :]), first and d % 2 == 0, last)

            def ff2_unit(j, w_wait, a_wait, first=False):
                w = (W_F2 + j) % 2
                pe.wait_ge(lo_ready, w_wait)
                pe.wait_ge(alo_ready, a_wait)
                for d in range(16):
                    if first and d == 14:
                        pe.wait_ge(g2_ready, 1)
                    ins = ff2_part(w, j, d, first, False)
                ins.then_inc(w_used, 1)

            pe.wait_ge(h1_ready, 64)
            for j in range(4):
                ff2_unit(j, W_F2 + j + 1, 48 + j + 1, first=(j == 0))
            with pe.Fori(1, 15) as i:
                for j in range(4):
                    ff2_unit(j, i * 4 + (W_F2 + j + 1), i * 4 + (48 + j + 1))
            for j in range(2):
                ff2_unit(j, W_F2 + 60 + j + 1, 48 + 60 + j + 1)
            pe.wait_ge(lo_ready, W_F2 + 64)
            pe.wait_ge(alo_ready, 48 + 64)
            for d in range(16):
                for j in (2, 3):
                    ins = ff2_part((W_F2 + j) % 2, j, d, False, j == 3)
                if d % 2:
                    ins.then_inc(f_ready, 1)
            for j in range(8):
                if j == 0:
                    pe.wait_ge(f_out, 1)
                add_squares("f", j, ps[:, 0, 0:SEQ])


CONV_B3 = [1, 6, 7, 8, 9, 10]

_COLUMNS = [("c", "c"), ("b_ada", "b_ada"), ("pre1", "pre_norm1_g"), ("post1", "post_norm1_g"),
            ("pre2", "pre_norm2_g"), ("post2", "post_norm2_g"), ("qn", "q_norm_g"), ("kvn", "kv_norm_g"),
            ("ga", "grp_norm_a_g"), ("gb", "grp_norm_b_g")]


def kernel(**inputs):
    import numpy as np
    import concourse.bacc as bacc
    from concourse.bass_utils import run_bass_kernel_spmd

    a = {k: np.asarray(v) for k, v in inputs.items()}
    qb = a["w_q_b"][0].reshape(QL, HEADS // 2, 2, QHD)
    qb = np.concatenate([qb[..., :NOPE].reshape(QL, 4, 2 * NOPE), qb[..., NOPE:].reshape(QL, 4, 2 * ROPE)], axis=2)
    arrays = {
        "xT": np.ascontiguousarray(a["x"][0].T),
        "positions": a["positions"].reshape(1, SEQ),
        "cols": np.ascontiguousarray(np.concatenate([a[src].reshape(-1, P) for _, src in _COLUMNS], axis=0).T),
        "w_sT": np.ascontiguousarray(a["w_s"][0].transpose(2, 0, 1)).reshape(P, GROUPS * P),
        "b_s": a["b_s"].reshape(1, GROUPS * P),
        "ln_v_g": a["ln_v_g"].reshape(1, GW),
        "ln_v_b": a["ln_v_b"].reshape(1, GW),
        "w_ada": a["w_ada"][0], "w_in": a["w_in"][0], "w_q_b": np.ascontiguousarray(qb.reshape(QL, HEADS * QHD)), "w_kv_b": a["w_kv_b"][0],
        "w_o": a["w_o"][0], "w_ff1": a["w_ff1"][0], "w_ff2": a["w_ff2"][0],
    }
    consts = np.zeros((P, NCONST), np.float32)
    rows = np.arange(P)
    consts[rows, C_IDENT + rows] = 1.0
    consts[rows, C_SWAP + (rows ^ 32)] = 1.0
    f = np.float32(ROPE_THETA) ** (-np.arange(0, ROPE, 2, dtype=np.float32) / np.float32(ROPE))
    consts[:, C_FREQ] = np.where(rows % 64 < 32, -1.0, 1.0) * f[rows % 32]
    arrays["consts"] = consts

    nc = bacc.Bacc("TRN2", target_bir_lowering=False, num_devices=1)
    aps = {k: nc.dram_tensor("in_" + k, v.shape, mybir.dt.from_np(v.dtype), kind="ExternalInput").ap() for k, v in arrays.items()}
    out = nc.dram_tensor("outT", (D, SEQ), mybir.dt.float32, kind="ExternalOutput").ap()
    block_kernel(nc, aps, out)
    r = run_bass_kernel_spmd(nc, [{"in_" + k: v for k, v in arrays.items()}], core_ids=[0])
    return np.ascontiguousarray(r.results[0]["outT"].T).reshape(1, SEQ, D)
```

```python
import concourse.bass as bass
from concourse import mybir
from contextlib import ExitStack

P = 128
SEQ = 256
D = 2048
KT = D // P
CHUNK = 64
GW = 1024
GROUPS = 8
HEADS = 8
NOPE, ROPE, VD = 128, 64, 128
QL, KVL = 512, 256
QHD = NOPE + ROPE
DFF = 8192
FT = DFF // P
EPS = 1e-6
NEG = -1e30
ROPE_THETA = 10000.0
UNIT = 2048
RING = 4

COLS = {}
_at = 0
for _name, _n in (("c", 16), ("b_ada", 96), ("pre1", 16), ("post1", 16), ("pre2", 16), ("post2", 16),
                  ("qn", 4), ("kvn", 2), ("ga", 8), ("gb", 8)):
    COLS[_name] = (_at, _at + _n)
    _at += _n
NCOLS = _at
C_IDENT, C_SWAP, C_FREQ, NCONST = 0, 128, 256, 257

TWO_PI = (6.28125, 0.0019350051879882812, 3.0199159819504e-07)
ROUND = 12582912.0
PI = 3.1415925

NORMS = {"x": 8, "kv": 1, "q": 2, "a": 4, "m": 4, "y": 8, "x1": 8, "f": 8}
NORM_NUMBER = {_name: _i for _i, _name in enumerate(NORMS)}
CHUNKS = ([("x", _j) for _j in range(8)] + [("kv", 0), ("q", 0), ("q", 1), ("m", 0), ("m", 1), ("m", 2)]
          + [("a", _j) for _j in range(4)] + [("m", 3)]
          + [(_name, _j) for _name in ("y", "x1", "f") for _j in range(8)])

W_ROPE = KT
W_U = W_ROPE + 1
W_O = W_U + 8
W_F1 = W_O + 16
W_F2 = W_F1 + 64

ITEMS = ([("rope", 0), ("u", 0), ("u", 1), ("kvb", 0), ("kvb", 1)] + [("qb", i) for i in range(4)]
         + [("u", i) for i in range(2, 8)] + [("wo", i) for i in range(16)])
ADA_AFTER = [2] * 17 + [1] * 14
STREAM = []
for _i, _item in enumerate(ITEMS):
    STREAM.append((_item, _i))
    for _ in range(ADA_AFTER[_i]):
        STREAM.append((("ada", sum(1 for s in STREAM if s[0][0] == "ada")), _i))
N_IN = KT
N_FF1 = N_IN + len(STREAM)
N_FF2 = N_FF1 + 64
ADA_HALVES = [(2 * D, 32), (2 * D + 1024, 40), (4 * D, 64), (4 * D + 1024, 72), (3 * D, 48), (3 * D + 1024, 56)]
CONV_AFTER = {5: 0, 9: 1, 13: 2, 17: 3, 24: 4, 30: 5}


def block_kernel(nc, A, out):
    f32, f32r, i32 = mybir.dt.float32, mybir.dt.float32r, mybir.dt.int32
    ALU = mybir.AluOpType
    ACT = mybir.ActivationFunctionType
    AX = mybir.AxisListType

    w_ada, w_in, w_qb, w_kvb = A["w_ada"], A["w_in"], A["w_q_b"], A["w_kv_b"]
    w_o, w_ff1, w_ff2 = A["w_o"], A["w_ff1"], A["w_ff2"]

    ctx = ExitStack()
    with ctx:
        def sb(name, shape, dt=f32):
            return ctx.enter_context(nc.sbuf_tensor(name, shape, dt))

        def sem(name):
            return ctx.enter_context(nc.semaphore(name))

        xT = sb("xT", [P, KT, SEQ])
        big = sb("big", [P, FT * SEQ])
        raw = sb("raw", [P, RING, UNIT])
        w_hi = sb("w_hi", [P, 2, UNIT], f32r)
        w_lo = sb("w_lo", [P, 2, UNIT], f32r)
        a_hi = sb("a_hi", [P, KT, SEQ], f32r)
        a_lo = sb("a_lo", [P, KT, SEQ], f32r)
        cols = sb("cols", [P, NCOLS])
        cst = sb("cst", [P, NCONST])
        ones = sb("ones", [P, P])
        eps = sb("eps", [P, 1])
        cs = sb("cs", [P, KT])
        mods = sb("mods", [P, 96])
        gain1 = sb("gain1", [P, KT])
        gain2 = sb("gain2", [P, KT])
        gate1 = sb("gate1", [P, KT])
        gate2 = sb("gate2", [P, KT])
        cosT = sb("cosT", [P, SEQ])
        sinT = sb("sinT", [P, SEQ])
        std = sb("std", [P, SEQ])
        R = sb("R", [P, SEQ])
        h32 = sb("h32", [P, 2, SEQ])
        sqb = sb("sqb", [P, 2, 2 * SEQ])
        gm_w = sb("gm_w", [P, 2048])
        acc = sb("acc", [P, 2, 1024])
        mx = sb("mx", [P, 2])
        nb = sb("nb", [P, 2])
        rsum = sb("rsum", [P, 2])
        rinv = sb("rinv", [P, 2])
        bst = sb("bst", [P, 2, 2, 6])
        mv = sb("mv", [P, 2, 2])
        vstd = sb("vstd", [P, 2])
        vrs = sb("vrs", [P, 2])
        ps = ctx.enter_context(nc.psum_tensor("ps", [P, 8, 512], f32))

        wsT = gm_w[:, 0:1024]
        bs_rows = gm_w[:, 1024:2048]
        ada_g2 = gm_w
        ident = cst[:, C_IDENT:C_IDENT + P]
        swap = cst[:, C_SWAP:C_SWAP + P]
        freq = cst[:, C_FREQ:C_FREQ + 1]

        def region(lo, n):
            return big[:, lo:lo + n]
        ada_ring = region(0, 8 * UNIT).rearrange("p (s n) -> p s n", s=8)
        rope_a = raw[:, 0, 0:512].rearrange("p (s n) -> p s n", s=2)
        v_tok = region(0, 2048).rearrange("p (t n) -> p t n", t=2)
        u_all = region(2048, 2048)
        u_t = u_all.rearrange("p (t n) -> p t n", n=SEQ)
        q_lat = region(4096, 1024).rearrange("p (t n) -> p t n", n=SEQ)
        kv_lat = region(5120, 512).rearrange("p (t n) -> p t n", n=SEQ)
        prob = region(4096, 768).rearrange("p (s n) -> p s n", s=2)
        probT = region(4864, 768).rearrange("p (s n) -> p s n", s=2)
        k_pe = region(5632, 256)
        qT = region(5888, 2048).rearrange("p (t n) -> p t n", n=SEQ)
        q_pe = region(7936, 1024).rearrange("p (t n) -> p t n", n=SEQ)
        kT = region(8960, 2048).rearrange("p (t n) -> p t n", n=SEQ)
        v_att = region(11008, 2048).rearrange("p (t n) -> p t n", t=2)
        m_all = region(13056, 2048)
        m_t = m_all.rearrange("p (t n) -> p t n", n=SEQ)
        ln_rows = m_all.rearrange("p (t n) -> p t n", t=2)
        rtmp = region(15104, 256)
        y_all = region(6144, 4096)
        y_t = y_all.rearrange("p (t n) -> p t n", n=SEQ)
        f_t = region(0, 4096).rearrange("p (t n) -> p t n", n=SEQ)
        h1 = big

        small_in = sem("small_in")
        x_in = sem("x_in")
        gm_in = sem("gm_in")
        ws_masked = sem("ws_masked")
        ln_in = sem("ln_in")
        raw_in = [sem(f"raw_in{s}") for s in range(RING)]
        ada_in = [sem(f"ada_in{s}") for s in range(8)]
        g2_in = sem("g2_in")
        out_done = sem("out_done")
        consts_ready = sem("consts_ready")
        cs_ready = sem("cs_ready")
        hi_ready = sem("hi_ready")
        lo_ready = sem("lo_ready")
        w_used = sem("w_used")
        acc_step = sem("acc_step")
        ada_used = sem("ada_used")
        acc_ready = sem("acc_ready")
        mod_sum = sem("mod_sum")
        mod_read = sem("mod_read")
        act32_ready = sem("act32_ready")
        ahi_ready = sem("ahi_ready")
        alo_ready = sem("alo_ready")
        sq_ready = sem("sq_ready")
        sq_used = sem("sq_used")
        std_ready = sem("std_ready")
        inv_ready = sem("inv_ready")
        ang_ready = sem("ang_ready")
        trig_ready = sem("trig_ready")
        lat_ready = sem("lat_ready")
        vgelu_ready = sem("vgelu_ready")
        vstat_ready = sem("vstat_ready")
        vstd_ready = sem("vstd_ready")
        vnorm_ready = sem("vnorm_ready")
        latn_ready = sem("latn_ready")
        rope_raw = sem("rope_raw")
        proj_ready = sem("proj_ready")
        proj_out = sem("proj_out")
        b3_ready = sem("b3_ready")
        b3_read = sem("b3_read")
        pe_rot = sem("pe_rot")
        u_out = sem("u_out")
        s_ready = sem("s_ready")
        nb_ready = sem("nb_ready")
        exp_ready = sem("exp_ready")
        p_ready = sem("p_ready")
        pt_ready = sem("pt_ready")
        pt_out = sem("pt_out")
        pv_ready = sem("pv_ready")
        m_out = sem("m_out")
        gelu_u = sem("gelu_u")
        gm_ready = sem("gm_ready")
        gm_out = sem("gm_out")
        y_out = sem("y_out")
        gate_ready = sem("gate_ready")
        x1_ready = sem("x1_ready")
        z_ready = sem("z_ready")
        relu_ready = sem("relu_ready")
        h1_ready = sem("h1_ready")
        g2_sum = sem("g2_sum")
        g2_ready = sem("g2_ready")
        f_ready = sem("f_ready")
        f_out = sem("f_out")
        o_ready = sem("o_ready")
        act_step = sem("act_step")
        dve_step = sem("dve_step")

        def col(name, t=0, n=1):
            return cols[:, COLS[name][0] + t:COLS[name][0] + t + n]

        def consumer(n):
            if n < N_IN:
                return lo_ready, n + 1
            if n >= N_FF1:
                return lo_ready, W_F1 + n - N_FF1 + 1
            (kind, i), _ = STREAM[n - N_IN]
            if kind == "ada":
                return ada_used, i + 1
            if kind == "kvb":
                return proj_ready, 6 * (i + 1)
            if kind == "qb":
                return proj_ready, 12 + 3 * (i + 1)
            return lo_ready, {"rope": W_ROPE, "u": W_U, "wo": W_O}[kind] + i + 1

        ring_number = {item: N_IN + n for n, (item, _) in enumerate(STREAM)}

        def arrivals(n):
            return 16 * (n // RING + 1)

        def arrived(eng, n):
            eng.wait_ge(raw_in[n % RING], arrivals(n))

        block = ctx.enter_context(nc.Block())

        @block.sync
        def _(sp):
            def load_ada(q, r):
                for part in range(2):
                    if q:
                        sp.wait_ge(acc_step, 32 * (q - 1) + 8 * r + 7 + part)
                    c0 = (1 - part) * D + q * 512
                    sp.dma_start(ada_ring[:, 2 * r + part, :].rearrange("p (k c) -> p k c", c=512),
                                 w_ada[r * 512:(r + 1) * 512, c0:c0 + 512].rearrange("(k p) c -> p k c", p=P)
                                 ).then_inc(ada_in[2 * r + part], 16)

            def slot_free(n):
                if n >= RING:
                    sp.wait_ge(*consumer(n - RING))

            def load_in(k):
                slot_free(k)
                sp.dma_start(raw[:, k % RING, 0:1792], w_in[k * P:(k + 1) * P, 1024:2816]
                             ).then_inc(raw_in[k % RING], 16)

            load_ada(0, 0)
            sp.dma_start(xT[:, :, :], A["xT"].rearrange("(t p) n -> p t n", p=P)).then_inc(x_in, 16)
            for r in range(1, 4):
                load_ada(0, r)
            sp.wait_ge(trig_ready, 2)
            for k in range(KT):
                if k < 12:
                    load_ada(k // 4 + 1, k % 4)
                load_in(k)
            for (kind, i), _ in STREAM:
                n = ring_number[kind, i]
                slot_free(n)
                slot = raw[:, n % RING, :]
                if kind == "rope":
                    dst = slot[:, 0:1024].rearrange("p (k c) -> p k c", c=64)
                    src = w_in[:, 2816:2880].rearrange("(k p) c -> p k c", p=P)
                elif kind in ("u", "wo"):
                    dst = slot.rearrange("p (k c) -> p k c", c=256)
                    r0, c0 = (i % 2) * 1024, (i // 2) * 256
                    src = (w_in if kind == "u" else w_o)[r0:r0 + 1024, c0:c0 + 256].rearrange("(k p) c -> p k c", p=P)
                elif kind == "kvb":
                    dst = slot.rearrange("p (k c) -> p k c", c=1024)
                    src = w_kvb[:, i * 1024:(i + 1) * 1024].rearrange("(k p) c -> p k c", p=P)
                elif kind == "qb":
                    dst = slot[:, 0:1536].rearrange("p (k c) -> p k c", c=384)
                    src = w_qb[:, i * 384:(i + 1) * 384].rearrange("(k p) c -> p k c", p=P)
                else:
                    c0 = ADA_HALVES[i // 8][0]
                    r0 = (i % 8) * 256
                    dst = slot.rearrange("p (k c) -> p k c", c=1024)
                    src = w_ada[r0:r0 + 256, c0:c0 + 1024].rearrange("(k p) c -> p k c", p=P)
                sp.dma_start(dst, src).then_inc(raw_in[n % RING], 16)

            def load_ff1(i, j, after):
                sp.wait_ge(*after)
                s = (N_FF1 + j) % RING
                c0 = i * 512 + (j // 2) * 256
                r0 = (j % 2) * 1024
                sp.dma_start(raw[:, s, :].rearrange("p (k c) -> p k c", c=256),
                             w_ff1[r0:r0 + 1024, bass.ds(c0, 256)].rearrange("(k p) c -> p k c", p=P)
                             ).then_inc(raw_in[s], 16)

            def load_g2(i):
                sp.dma_start(ada_g2[:, :], w_ada[bass.ds(i * P, P), 5 * D:6 * D]).then_inc(g2_in, 16)

            for j in range(4):
                load_ff1(0, j, consumer(N_FF1 + j - RING))
            sp.wait_ge(gm_out, 8)
            load_g2(0)
            with sp.Fori(1, 16) as i:
                for j in range(4):
                    load_ff1(i, j, (lo_ready, i * 4 + (W_F1 + j - 3)))
                sp.wait_ge(ada_used, i + 48)
                load_g2(i)

            def load_ff2(i, j, n):
                sp.wait_ge(lo_ready, n)
                s = (N_FF2 + j) % RING
                sp.dma_start(raw[:, s, :], w_ff2[bass.ds(i * 512 + j * P, P), :]).then_inc(raw_in[s], 16)

            with sp.Fori(0, 16) as i:
                for j in range(4):
                    load_ff2(i, j, i * 4 + (W_F2 + j - 3))
            for g in range(4):
                sp.wait_ge(o_ready, 2 * g + 2)
                sp.dma_start(out[g * 512:(g + 1) * 512, :].rearrange("(t p) n -> p t n", p=P),
                             xT[:, 4 * g:4 * g + 4, :]).then_inc(out_done, 16)
            sp.wait_ge(out_done, 64)

        @block.gpsimd
        def _(pool):
            nc.gpsimd.memset(ones[:, :], 1.0).then_inc(consts_ready, 1)
            nc.gpsimd.memset(eps[:, :], EPS).then_inc(consts_ready, 1)
            pool.wait_ge(consts_ready, 2)
            pool.wait_ge(gm_in, 32)
            nc.gpsimd.memset(wsT.rearrange("p (g i) -> p g i", i=P)[CHUNK:P, :, 0:CHUNK], 0.0).then_inc(ws_masked, 1)

        @block.scalar
        def _(act):
            steps = [0]

            def link(ins):
                steps[0] += 1
                ins.then_inc(act_step, 1)
                act.wait_ge(act_step, steps[0])

            act.dma_start(cols[:, :], A["cols"]).then_inc(small_in, 16)
            act.dma_start(cst[:, :], A["consts"]).then_inc(small_in, 16)
            act.dma_start(h32[:, 0, :].bitcast(i32), A["positions"].to_broadcast([P, SEQ])).then_inc(small_in, 16)
            act.dma_start(wsT, A["w_sT"]).then_inc(gm_in, 16)
            act.dma_start(bs_rows, A["b_s"].to_broadcast([P, 1024])).then_inc(gm_in, 16)
            act.wait_ge(small_in, 48)
            nc.scalar.activation(cs[:, :], col("c", 0, 16), ACT.Silu).then_inc(cs_ready, 1)

            def split_hi(w):
                n = w if w < N_IN else ring_number[("rope", 0) if w == W_ROPE else ("u", w - W_U) if w < W_O
                                                   else ("wo", w - W_O)] if w < W_F1 else N_FF1 + w - W_F1
                arrived(act, n)
                if w >= 2:
                    act.wait_ge(w_used, w - 1)
                src, dst = raw[:, n % RING, :], w_hi[:, w % 2, :]
                if w < N_IN:
                    src, dst = src[:, 0:1792], dst[:, 0:1792]
                elif w == W_ROPE:
                    for r in range(2):
                        ins = nc.scalar.activation(
                            dst.rearrange("p (k r c) -> p k r c", r=2, c=64)[:, :, r, :],
                            src[:, 0:1024].rearrange("p (k c) -> p k c", c=64), ACT.Copy)
                    ins.then_inc(hi_ready, 1)
                    return
                nc.scalar.activation(dst, src, ACT.Copy).then_inc(hi_ready, 1)

            def act_hi(n, slot, shift=None):
                act.wait_ge(act32_ready, n + 1)
                if shift is None:
                    ins = nc.scalar.activation(a_hi[:, slot, :], h32[:, n % 2, :], ACT.Copy)
                else:
                    ins = nc.scalar.activation(a_hi[:, slot, :], h32[:, n % 2, :], ACT.Identity,
                                               bias=mods[:, shift + slot:shift + slot + 1])
                ins.then_inc(ahi_ready, 1)

            def squares(name, j, src):
                g = CHUNKS.index((name, j))
                if g >= 2:
                    act.wait_ge(sq_used, g - 1)
                dst = sqb[:, g % 2, :]
                if len(src.shape) == 3:
                    dst = dst.rearrange("p (t n) -> p t n", t=2)
                nc.scalar.activation(dst, src, ACT.Square).then_inc(sq_ready, 1)

            def make_std(name, width, src):
                i = NORM_NUMBER[name]
                act.wait_ge(sq_used, CHUNKS.index((name, NORMS[name] - 1)) + 1)
                if i:
                    act.wait_ge(inv_ready, i)
                nc.scalar.activation(std[:, :], src, ACT.Sqrt, bias=eps[:, 0:1], scale=1.0 / width).then_inc(std_ready, 1)

            act.wait_ge(ang_ready, 1)
            nc.scalar.activation(sinT[:, :], rope_a[:, 0, :], ACT.Sin).then_inc(trig_ready, 1)
            nc.scalar.activation(cosT[:, :], rope_a[:, 1, :], ACT.Sin).then_inc(trig_ready, 1)
            act.wait_ge(x_in, 16)
            act.wait_ge(consts_ready, 2)
            for j in range(8):
                squares("x", j, xT[:, 2 * j:2 * j + 2, :].rearrange("p t n -> p (t n)"))
            make_std("x", D, ps[:, 0, 0:SEQ])

            for k in range(KT):
                split_hi(k)
                act_hi(k, k, shift=0)
            split_hi(W_ROPE)
            act.wait_ge(w_used, KT)
            nc.scalar.activation(kv_lat.rearrange("p t n -> p (t n)"), ps[:, 6, :], ACT.Copy).then_inc(lat_ready, 1)
            nc.scalar.activation(q_lat.rearrange("p t n -> p (t n)"), ps[:, 4:6, :].rearrange("p b n -> p (b n)"),
                                 ACT.Copy).then_inc(lat_ready, 1)
            act.wait_ge(lat_ready, 2)
            act.wait_ge(acc_step, 128)
            for i, name in enumerate(("ln_v_g", "ln_v_b")):
                act.dma_start(ln_rows[:, i, :], A[name].to_broadcast([P, 1024])).then_inc(ln_in, 16)
            split_hi(W_U)
            squares("kv", 0, kv_lat.rearrange("p t n -> p (t n)"))
            for j in range(2):
                squares("q", j, q_lat[:, 2 * j:2 * j + 2, :].rearrange("p t n -> p (t n)"))
            nc.scalar.activation(v_tok.rearrange("p t n -> p (t n)"), ps[:, 0:4, :].rearrange("p b n -> p (b n)"),
                                 ACT.Gelu).then_inc(vgelu_ready, 1)
            act.wait_ge(w_used, W_ROPE + 1)
            nc.scalar.activation(k_pe, ps[:, 7, 0:SEQ], ACT.Copy).then_inc(rope_raw, 1)
            make_std("kv", KVL, ps[:, 6, 0:SEQ])
            make_std("q", QL, ps[:, 7, 0:SEQ])
            split_hi(W_U + 1)
            act.wait_ge(vstat_ready, 1)
            nc.scalar.activation(vstd[:, :], mv[:, :, 1], ACT.Sqrt, bias=eps[:, 0:1]).then_inc(vstd_ready, 1)

            def u_evac(p):
                act.wait_ge(w_used, W_U + 2 * p + 2)
                b = 4 + 2 * (p % 2)
                nc.scalar.activation(u_t[:, 2 * p:2 * p + 2, :], ps[:, b:b + 2, 0:SEQ], ACT.Copy).then_inc(u_out, 1)

            proj = [0]

            def proj_evac(dst, width):
                n = proj[0]
                act.wait_ge(proj_ready, n + 1)
                nc.scalar.activation(dst, ps[:, n % 3, 0:width], ACT.Copy).then_inc(proj_out, 1)
                proj[0] += 1

            u_evac(0)
            for g in range(2):
                for h in range(4 * g, 4 * g + 4):
                    proj_evac(kT[:, h, :], SEQ)
                for t in range(2):
                    proj_evac(v_att[:, t, g * 512:(g + 1) * 512], 512)
            for i in range(4):
                proj_evac(q_pe[:, i, :], SEQ)
                proj_evac(qT[:, 2 * i, :], SEQ)
                proj_evac(qT[:, 2 * i + 1, :], SEQ)
            split_hi(W_U + 2)
            split_hi(W_U + 3)

            def exps(h):
                act.wait_ge(nb_ready, h + 1)
                s = h % 2
                nc.scalar.activation(prob[:, s, 0:128], ps[:, 0, 0:128], ACT.Exp, bias=nb[:, 0:1],
                                     scale=float(QHD) ** -0.5, accum_out=rsum[:, 0:1]).then_inc(exp_ready, 1)
                nc.scalar.activation(prob[:, s, 128:384], ps[:, 0, 128:384], ACT.Exp, bias=nb[:, 1:2],
                                     scale=float(QHD) ** -0.5, accum_out=rsum[:, 1:2]).then_inc(exp_ready, 1)

            def pt_evac(h):
                act.wait_ge(pt_ready, h + 1)
                nc.scalar.activation(probT[:, h % 2, :], ps[:, 1, 0:384], ACT.Copy).then_inc(pt_out, 1)

            def m_evac(h):
                act.wait_ge(pv_ready, h + 1)
                nc.scalar.activation(m_t[:, h, :], ps[:, 2, 0:SEQ], ACT.Copy).then_inc(m_out, 1)

            for j in range(8):
                exps(j)
                if j in (6, 7):
                    for c in ((0, 1) if j == 6 else (2,)):
                        act.wait_ge(m_out, 2 * c + 2)
                        squares("m", c, m_all[:, c * 512:(c + 1) * 512])
                if j:
                    m_evac(j - 1)
                if j == 7:
                    act.wait_ge(gm_out, 8)
                    for c in range(2):
                        squares("a", c, u_all[:, c * 512:(c + 1) * 512])
                pt_evac(j)
                if j in (1, 3, 5):
                    u_evac((j + 1) // 2)
                if j < 6:
                    split_hi(W_U + 4 + j)
                if j == 5:
                    act.wait_ge(u_out, 4)
                    nc.scalar.activation(u_all, u_all, ACT.Gelu).then_inc(gelu_u, 1)
            for c in range(2, 4):
                squares("a", c, u_all[:, c * 512:(c + 1) * 512])
            m_evac(7)
            make_std("a", GW, ps[:, 0, 0:SEQ])
            act.wait_ge(m_out, 8)
            squares("m", 3, m_all[:, 1536:2048])
            make_std("m", GW, ps[:, 3, 0:SEQ])
            for t in range(16):
                act_hi(16 + t, t)

            def y_evac(p):
                act.wait_ge(w_used, W_O + 2 * p + 2)
                if p == 0:
                    act.wait_ge(gate_ready, 1)
                b = 4 + 2 * (p % 2)
                squares("y", p, ps[:, b:b + 2, 0:SEQ])
                for t in range(2):
                    nc.scalar.activation(y_t[:, 2 * p + t, :], ps[:, b + t, 0:SEQ], ACT.Copy,
                                         scale=gate1[:, 2 * p + t:2 * p + t + 1]).then_inc(y_out, 1)

            for i in range(2, 16):
                split_hi(W_O + i)
                if i % 2 and i >= 3:
                    y_evac((i - 3) // 2)
            split_hi(W_F1)
            y_evac(7)
            split_hi(W_F1 + 1)
            make_std("y", D, ps[:, 2, 0:SEQ])
            for j in range(8):
                act.wait_ge(x1_ready, j + 1)
                squares("x1", j, xT[:, 2 * j:2 * j + 2, :].rearrange("p t n -> p (t n)"))
            make_std("x1", D, ps[:, 1, 0:SEQ])
            for t in range(16):
                act_hi(32 + t, t, shift=48)

            def ff_hi(s_unit, arrived_at, used):
                s, w = s_unit
                act.wait_ge(raw_in[s], arrived_at)
                act.wait_ge(w_used, used)
                nc.scalar.activation(w_hi[:, w, :], raw[:, s, :], ACT.Copy).then_inc(hi_ready, 1)

            def slots(n0, w0, j):
                return (n0 + j) % RING, (w0 + j) % 2

            def relu2(i, t):
                if t % 2 == 0:
                    act.wait_ge(z_ready, i * 2 + (t // 2 + 1))
                else:
                    act.wait_ge(w_used, i * 4 + (W_F1 + t + 1))
                relu = sqb[:, t // 2, (t % 2) * SEQ:(t % 2 + 1) * SEQ]
                nc.scalar.activation(relu, ps[:, t, 0:SEQ], ACT.Relu).then_inc(relu_ready, 1)
                act.wait_ge(relu_ready, i * 4 + (t + 1))
                act.wait_ge(x1_ready, 8)
                nc.scalar.activation(h1[:, bass.ds(i * 1024 + t * SEQ, SEQ)], relu, ACT.Square).then_inc(h1_ready, 1)

            with act.Fori(0, 16) as i:
                for j in (2, 3):
                    ff_hi(slots(N_FF1, W_F1, j), i * 16 + arrivals(N_FF1 + j), i * 4 + (W_F1 + j - 1))
                relu2(i, 0)
                relu2(i, 1)
                for j in (4, 5):
                    ff_hi(slots(N_FF1, W_F1, j), i * 16 + arrivals(N_FF1 + j), i * 4 + (W_F1 + j - 1))
                relu2(i, 2)
                relu2(i, 3)

            def h_hi(i, j, used):
                act.wait_ge(w_used, used)
                act.wait_ge(h1_ready, 64)
                nc.scalar.activation(a_hi[:, j % 4, :], h1[:, bass.ds(i * 1024 + j * SEQ, SEQ)], ACT.Copy).then_inc(ahi_ready, 1)

            for j in range(2):
                h_hi(0, j, W_F2)
            with act.Fori(0, 15) as i:
                for j in range(2, 6):
                    h_hi(i, j, i * 4 + (W_F2 + j - 3))
                    ff_hi(slots(N_FF2, W_F2, j), i * 16 + arrivals(N_FF2 + j), i * 4 + (W_F2 + j - 1))
            for j in range(2, 4):
                h_hi(15, j, W_F2 + 60 + j - 3)
                ff_hi(slots(N_FF2, W_F2, 60 + j), arrivals(N_FF2 + 60 + j), W_F2 + 60 + j - 1)
            act.wait_ge(gate_ready, 2)
            for b in range(8):
                act.wait_ge(f_ready, b + 1)
                squares("f", b, ps[:, b, :])
                for t in range(2):
                    nc.scalar.activation(f_t[:, 2 * b + t, :], ps[:, b, t * SEQ:(t + 1) * SEQ], ACT.Copy,
                                         scale=gate2[:, 2 * b + t:2 * b + t + 1]).then_inc(f_out, 1)
            make_std("f", D, ps[:, 0, 0:SEQ])

        @block.vector
        def _(dve):
            steps = [0]

            def link(ins):
                steps[0] += 1
                ins.then_inc(dve_step, 1)
                dve.wait_ge(dve_step, steps[0])

            V = nc.vector
            dve.wait_ge(small_in, 48)
            ang, t0 = rope_a[:, 0, :], rope_a[:, 1, :]
            link(V.tensor_copy(ang, h32[:, 0, :].bitcast(i32)))
            link(V.tensor_scalar(ang, ang, freq, None, ALU.mult))
            for turns in (4096.0, 1.0):
                link(V.tensor_scalar(t0, ang, 1.0 / (turns * 6.283185307179586), ROUND, ALU.mult, ALU.add))
                link(V.tensor_scalar(t0, t0, ROUND, None, ALU.subtract))
                for piece in TWO_PI:
                    link(V.scalar_tensor_tensor(out=ang, in0=t0, scalar=-turns * piece, in1=ang,
                                                op0=ALU.mult, op1=ALU.add))
            link(V.tensor_scalar(ang, ang, PI, -PI, ALU.min, ALU.max))
            link(V.tensor_scalar(t0, ang, -1.0, None, ALU.mult))
            link(V.tensor_tensor(t0, t0, ang, ALU.min))
            V.tensor_scalar(t0, t0, 1.5707963267948966, None, ALU.add).then_inc(ang_ready, 1)

            def ada_rows(q, r):
                if q >= 2 and r == 0:
                    dve.wait_ge(mod_sum, q - 1)
                for k in range(4):
                    for part in range(2):
                        if k == 0:
                            dve.wait_ge(ada_in[2 * r + part], 16 * (q + 1))
                        step = 32 * q + 8 * r + 2 * k + part
                        if step >= 2:
                            dve.wait_ge(acc_step, step - 1)
                        a = acc[:, q % 2, part * 512:(part + 1) * 512]
                        src = ada_ring[:, 2 * r + part, k * 512:(k + 1) * 512]
                        c = cs[:, 4 * r + k:4 * r + k + 1]
                        if r == 0 and k == 0:
                            V.tensor_scalar(a, src, c, None, ALU.mult).then_inc(acc_step, 1)
                        else:
                            V.scalar_tensor_tensor(out=a, in0=src, scalar=c, in1=a, op0=ALU.mult,
                                                   op1=ALU.add).then_inc(acc_step, 1)

            def make_inv(name):
                i = NORM_NUMBER[name]
                dve.wait_ge(std_ready, i + 1)
                V.reciprocal(R[:, :], std[:, :]).then_inc(inv_ready, 1)
                dve.wait_ge(inv_ready, i + 1)

            def act_lo(n, slot, shift=None):
                dve.wait_ge(ahi_ready, n + 1)
                lo, h, hi = a_lo[:, slot, :], h32[:, n % 2, :], a_hi[:, slot, :].bitcast(f32)
                if shift is None:
                    ins = V.tensor_tensor(lo, h, hi, ALU.subtract)
                else:
                    ins = V.scalar_tensor_tensor(out=lo, in0=h, scalar=mods[:, shift + slot:shift + slot + 1],
                                                 in1=hi, op0=ALU.add, op1=ALU.subtract)
                ins.then_inc(alo_ready, 1)

            def modulated(n, t, gain):
                if n >= 2:
                    dve.wait_ge(alo_ready, n - 1)
                V.scalar_tensor_tensor(out=h32[:, n % 2, :], in0=xT[:, t, :], scalar=gain[:, t:t + 1], in1=R[:, :],
                                       op0=ALU.mult, op1=ALU.mult).then_inc(act32_ready, 1)

            def split_lo(w):
                n = w if w < N_IN else ring_number[("rope", 0) if w == W_ROPE else ("u", w - W_U) if w < W_O
                                                   else ("wo", w - W_O)] if w < W_F1 else N_FF1 + w - W_F1
                dve.wait_ge(hi_ready, w + 1)
                if w >= 2:
                    dve.wait_ge(w_used, w - 1)
                src, hi, lo = raw[:, n % RING, :], w_hi[:, w % 2, :].bitcast(f32), w_lo[:, w % 2, :]
                if w < N_IN:
                    src, hi, lo = src[:, 0:1792], hi[:, 0:1792], lo[:, 0:1792]
                elif w == W_ROPE:
                    src = src[:, 0:1024].rearrange("p (k c) -> p k c", c=64)
                    hi = hi.rearrange("p (k r c) -> p k r c", r=2, c=64)
                    lo = lo.rearrange("p (k r c) -> p k r c", r=2, c=64)
                    for r in range(2):
                        ins = V.tensor_tensor(lo[:, :, r, :], src, hi[:, :, r, :], ALU.subtract)
                    ins.then_inc(lo_ready, 1)
                    return
                V.tensor_tensor(lo, src, hi, ALU.subtract).then_inc(lo_ready, 1)

            dve.wait_ge(cs_ready, 1)
            for r in range(4):
                ada_rows(0, r)
            make_inv("x")

            def modulation(q):
                dve.wait_ge(mod_sum, q + 1)
                t = 4 * q
                V.tensor_tensor(mods[:, 16 + t:20 + t], ps[:, 7, 0:4], col("b_ada", 16 + t, 4), ALU.add)
                V.tensor_tensor(mods[:, t:t + 4], ps[:, 7, 4:8], col("b_ada", t, 4), ALU.add).then_inc(mod_read, 1)
                dve.wait_ge(mod_read, q + 1)
                link(V.scalar_tensor_tensor(out=gain1[:, t:t + 4], in0=mods[:, 16 + t:20 + t], scalar=1.0,
                                            in1=col("pre1", t, 4), op0=ALU.add, op1=ALU.mult))

            for k in range(KT):
                if k % 4 == 0:
                    modulation(k // 4)
                modulated(k, k, gain1)
                split_lo(k)
                act_lo(k, k, shift=0)
                if k < 12:
                    ada_rows(k // 4 + 1, k % 4)

            def ada_unit(i):
                hp, r = i // 8, i % 8
                n = ring_number["ada", i]
                arrived(dve, n)
                a = acc[:, hp % 2, :]
                if r == 0:
                    if hp < 2:
                        dve.wait_ge(mod_sum, 4)
                    else:
                        dve.wait_ge(b3_ready, CONV_B3[hp - 2] + 1)
                for k in range(2):
                    src = raw[:, n % RING, k * 1024:(k + 1) * 1024]
                    c = cs[:, 2 * r + k:2 * r + k + 1]
                    if r == 0 and k == 0:
                        link(V.tensor_scalar(a, src, c, None, ALU.mult))
                    elif k == 0:
                        link(V.scalar_tensor_tensor(out=a, in0=src, scalar=c, in1=a, op0=ALU.mult, op1=ALU.add))
                    else:
                        V.scalar_tensor_tensor(out=a, in0=src, scalar=c, in1=a, op0=ALU.mult,
                                               op1=ALU.add).then_inc(ada_used, 1)
                        dve.wait_ge(ada_used, i + 1)

            def process(idx):
                kind, i = ITEMS[idx]
                if kind in ("rope", "u", "wo"):
                    split_lo({"rope": W_ROPE, "u": W_U, "wo": W_O}[kind] + i)
                for (k2, i2), at in STREAM:
                    if k2 == "ada" and at == idx:
                        ada_unit(i2)

            def rotate(b3, dst):
                dve.wait_ge(b3_ready, b3 + 1)
                if b3:
                    dve.wait_ge(pe_rot, b3 - 1)
                V.tensor_tensor(rtmp, ps[:, 3, 0:SEQ], sinT[:, :], ALU.mult).then_inc(b3_read, 1)
                dve.wait_ge(b3_read, b3 + 1)
                link(V.tensor_tensor(dst, dst, cosT[:, :], ALU.mult))
                V.tensor_tensor(dst, dst, rtmp, ALU.add).then_inc(pe_rot, 1)

            def conv_read(hp):
                b3 = CONV_B3[hp]
                m0 = ADA_HALVES[hp][1]
                dve.wait_ge(b3_ready, b3 + 1)
                V.tensor_tensor(mods[:, m0:m0 + 8], ps[:, 3, 0:8], col("b_ada", m0, 8), ALU.add).then_inc(b3_read, 1)
                dve.wait_ge(b3_read, b3 + 1)

            process(0)
            process(1)
            make_inv("kv")
            for t in range(2):
                V.scalar_tensor_tensor(out=kv_lat[:, t, :], in0=kv_lat[:, t, :], scalar=col("kvn", t), in1=R[:, :],
                                       op0=ALU.mult, op1=ALU.mult).then_inc(latn_ready, 1)
            dve.wait_ge(latn_ready, 2)
            make_inv("q")
            for t in range(4):
                V.scalar_tensor_tensor(out=q_lat[:, t, :], in0=q_lat[:, t, :], scalar=col("qn", t), in1=R[:, :],
                                       op0=ALU.mult, op1=ALU.mult).then_inc(latn_ready, 1)
            dve.wait_ge(vgelu_ready, 1)
            for t in range(2):
                for j in range(2):
                    link(V.bn_stats(bst[:, t, j, :], v_tok[:, t, j * 512:(j + 1) * 512]))
            V.bn_aggr(mv[:, 0, :], bst[:, 0, :, :].rearrange("p a b -> p (a b)"))
            V.bn_aggr(mv[:, 1, :], bst[:, 1, :, :].rearrange("p a b -> p (a b)")).then_inc(vstat_ready, 1)
            process(2)
            dve.wait_ge(vstd_ready, 1)
            link(V.reciprocal(vrs[:, :], vstd[:, :]))
            dve.wait_ge(ln_in, 32)
            for t in range(2):
                link(V.tensor_scalar(v_tok[:, t, :], v_tok[:, t, :], mv[:, t, 0:1], vrs[:, t:t + 1],
                                     ALU.subtract, ALU.mult))
                link(V.tensor_tensor(v_tok[:, t, :], v_tok[:, t, :], ln_rows[:, 0, :], ALU.mult))
                V.tensor_tensor(v_tok[:, t, :], v_tok[:, t, :], ln_rows[:, 1, :], ALU.add).then_inc(vnorm_ready, 1)
            process(3)
            process(4)
            rotate(0, k_pe)
            process(5)
            process(6)
            conv_read(0)
            rotate(2, q_pe[:, 0, :])
            process(7)
            rotate(3, q_pe[:, 1, :])
            process(8)
            process(9)
            rotate(4, q_pe[:, 2, :])
            rotate(5, q_pe[:, 3, :])

            def row_max(h):
                dve.wait_ge(s_ready, h + 1)
                if h:
                    dve.wait_ge(exp_ready, 2 * h)
                V.memset(ps[0:64, 0, 64:128], NEG)
                link(V.memset(ps[0:64, 0, 320:384], NEG))
                V.reduce_max(mx[:, 0:1], ps[:, 0, 0:128], AX.X)
                link(V.reduce_max(mx[:, 1:2], ps[:, 0, 128:384], AX.X))
                V.tensor_scalar(nb[:, :], mx[:, :], -float(QHD) ** -0.5, None, ALU.mult).then_inc(nb_ready, 1)

            def normalise(h):
                dve.wait_ge(exp_ready, 2 * h + 2)
                link(V.reciprocal(rinv[:, :], rsum[:, :]))
                p = prob[:, h % 2, :]
                V.tensor_scalar(p[:, 0:128], p[:, 0:128], rinv[:, 0:1], None, ALU.mult)
                V.tensor_scalar(p[:, 128:384], p[:, 128:384], rinv[:, 1:2], None, ALU.mult).then_inc(p_ready, 1)

            def gate_u(g):
                t = h32[:, g % 2, :]
                if g >= 2:
                    dve.wait_ge(gm_out, g - 1)
                link(V.tensor_tensor(t.rearrange("p (n i) -> p n i", i=128),
                                     ps[:, 4 + g // 2, (g % 2) * 256:(g % 2) * 256 + 256].rearrange("p (n i) -> p n i", i=128),
                                     bs_rows[:, g * 128:(g + 1) * 128].rearrange("p (n i) -> p n i", n=1).to_broadcast([P, 2, 128]),
                                     ALU.add))
                V.tensor_tensor(u_t[:, g, :], t, u_t[:, g, :], ALU.mult).then_inc(gm_out, 1)

            def ada_after(idx):
                for (k2, i2), at in STREAM:
                    if k2 == "ada" and at == idx:
                        ada_unit(i2)

            for j in range(8):
                row_max(j)
                if j < 7:
                    split_lo(W_U + 3 + j)
                if j == 7:
                    dve.wait_ge(gm_ready, 2)
                    for g in range(4, 8):
                        gate_u(g)
                normalise(j)
                if j < 7:
                    ada_after(10 + j)
                if j == 1:
                    conv_read(1)
                    V.tensor_tensor(gate1[:, :], mods[:, 32:48], col("post1", 0, 16), ALU.mult).then_inc(gate_ready, 1)
                if j == 5:
                    conv_read(2)
                if j == 6:
                    dve.wait_ge(gm_ready, 1)
                    dve.wait_ge(gelu_u, 1)
                    dve.wait_ge(gm_in, 32)
                    for g in range(4):
                        gate_u(g)

            def normed(name, n0, slot0, src, gain):
                for t in range(8):
                    dve.wait_ge(alo_ready, n0 + t - 1)
                    V.scalar_tensor_tensor(out=h32[:, t % 2, :], in0=src[:, t, :], scalar=col(gain, t), in1=R[:, :],
                                           op0=ALU.mult, op1=ALU.mult).then_inc(act32_ready, 1)
                    if t:
                        act_lo(n0 + t - 1, slot0 + t - 1)
                act_lo(n0 + 7, slot0 + 7)

            make_inv("a")
            dve.wait_ge(w_used, W_O)
            normed("a", 16, 0, u_t, "ga")
            make_inv("m")
            normed("m", 24, 8, m_t, "gb")
            for i in range(17, 31):
                process(i)
                if i == 18:
                    conv_read(3)
                if i == 25:
                    conv_read(4)
            split_lo(W_F1)
            conv_read(5)
            split_lo(W_F1 + 1)
            link(V.scalar_tensor_tensor(out=gain2[:, :], in0=mods[:, 64:80], scalar=1.0, in1=col("pre2", 0, 16),
                                        op0=ALU.add, op1=ALU.mult))

            def add_normed(part, j, done):
                y2, x2 = part[:, 2 * j:2 * j + 2, :], xT[:, 2 * j:2 * j + 2, :]
                link(V.tensor_tensor(y2, y2, R[:, :].rearrange("p (t n) -> p t n", t=1).to_broadcast([P, 2, SEQ]),
                                     ALU.mult))
                V.tensor_tensor(x2, x2, y2, ALU.add).then_inc(done, 1)

            make_inv("y")
            dve.wait_ge(y_out, 16)
            for j in range(8):
                add_normed(y_t, j, x1_ready)
            make_inv("x1")
            for t in range(16):
                modulated(32 + t, t, gain2)
                if t:
                    act_lo(31 + t, t - 1, shift=48)
            act_lo(47, 15, shift=48)

            def ff_lo(s_unit, hi, used):
                s, w = s_unit
                dve.wait_ge(hi_ready, hi)
                dve.wait_ge(w_used, used)
                V.tensor_tensor(w_lo[:, w, :], raw[:, s, :], w_hi[:, w, :].bitcast(f32), ALU.subtract).then_inc(lo_ready, 1)

            def slots(n0, w0, j):
                return (n0 + j) % RING, (w0 + j) % 2

            acc_all = acc[:, :, :].rearrange("p a n -> p (a n)")
            link(V.memset(acc_all, 0.0))
            with dve.Fori(0, 16) as i:
                for j in (2, 3):
                    ff_lo(slots(N_FF1, W_F1, j), i * 4 + (W_F1 + j + 1), i * 4 + (W_F1 + j - 1))
                dve.wait_ge(g2_in, i * 16 + 16)
                V.scalar_tensor_tensor(out=acc_all, in0=ada_g2[:, :], scalar=cs[:, bass.ds(i, 1)], in1=acc_all,
                                       op0=ALU.mult, op1=ALU.add).then_inc(ada_used, 1)
                dve.wait_ge(ada_used, i + 49)
                for j in (4, 5):
                    ff_lo(slots(N_FF1, W_F1, j), i * 4 + (W_F1 + j + 1), i * 4 + (W_F1 + j - 1))
            dve.wait_ge(g2_sum, 1)
            V.tensor_tensor(mods[:, 80:96], ps[:, 7, 0:16], col("b_ada", 80, 16), ALU.add).then_inc(g2_ready, 1)
            dve.wait_ge(g2_ready, 1)
            V.tensor_tensor(gate2[:, :], mods[:, 80:96], col("post2", 0, 16), ALU.mult).then_inc(gate_ready, 1)

            def h_lo(i, j, n):
                dve.wait_ge(ahi_ready, n)
                V.tensor_tensor(a_lo[:, j % 4, :], h1[:, bass.ds(i * 1024 + j * SEQ, SEQ)], a_hi[:, j % 4, :].bitcast(f32),
                                ALU.subtract).then_inc(alo_ready, 1)

            for j in range(2):
                h_lo(0, j, 49 + j)
            with dve.Fori(0, 15) as i:
                for j in range(2, 6):
                    h_lo(i, j, i * 4 + (49 + j))
                    ff_lo(slots(N_FF2, W_F2, j), i * 4 + (W_F2 + j + 1), i * 4 + (W_F2 + j - 1))
            for j in range(2, 4):
                h_lo(15, j, 48 + 60 + j + 1)
                ff_lo(slots(N_FF2, W_F2, 60 + j), W_F2 + 60 + j + 1, W_F2 + 60 + j - 1)
            make_inv("f")
            dve.wait_ge(f_out, 16)
            for j in range(8):
                add_normed(f_t, j, o_ready)

        @block.tensor
        def _(pe):
            mm = nc.tensor.matmul

            def add_squares(name, j, dst):
                g = CHUNKS.index((name, j))
                pe.wait_ge(sq_ready, g + 1)
                for t in range(2):
                    ins = mm(dst, ones[:, :], sqb[:, g % 2, t * SEQ:(t + 1) * SEQ],
                             start=(j == 0 and t == 0), stop=(j == NORMS[name] - 1 and t == 1))
                ins.then_inc(sq_used, 1)

            def sum_ada(q):
                if q:
                    pe.wait_ge(mod_read, q)
                pe.wait_ge(acc_step, 32 * (q + 1))
                for f in range(8):
                    ins = mm(ps[:, 7, f:f + 1], acc[:, q % 2, f * P:(f + 1) * P], ones[:, 0:1], start=True, stop=True)
                ins.then_inc(mod_sum, 1)

            def three(dst, w, a, start, stop, stationary_weights=True):
                (wh, wl), (ah, al) = w, a
                for n, (x, y) in enumerate(((wh, ah), (wh, al), (wl, ah)) if stationary_weights else
                                           ((ah, wh), (ah, wl), (al, wh))):
                    ins = mm(dst, x, y, start=(start and n == 0), stop=(stop and n == 2), skip_group_check=True)
                return ins

            def in_rows(k):
                s = k % 2
                pe.wait_ge(lo_ready, k + 1)
                pe.wait_ge(alo_ready, k + 1)
                for t in range(2):
                    a = (a_hi[:, k, t * P:(t + 1) * P], a_lo[:, k, t * P:(t + 1) * P])
                    for n in range(2):
                        w = (w_hi[:, s, n * 512:(n + 1) * 512], w_lo[:, s, n * 512:(n + 1) * 512])
                        three(ps[:, 2 * t + n, :], w, a, k == 0, k == KT - 1, stationary_weights=False)
                for f in range(6):
                    c = 1024 + f * P
                    ins = three(ps[:, 4 + f // 2, (f % 2) * SEQ:(f % 2 + 1) * SEQ],
                                (w_hi[:, s, c:c + P], w_lo[:, s, c:c + P]), (a_hi[:, k, :], a_lo[:, k, :]),
                                k == 0 and f % 2 == 0, k == KT - 1)
                ins.then_inc(w_used, 1)

            pe.wait_ge(consts_ready, 2)
            for j in range(8):
                add_squares("x", j, ps[:, 0, 0:SEQ])
            for k in range(KT):
                if k % 4 == 0:
                    sum_ada(k // 4)
                in_rows(k)

            pe.wait_ge(lo_ready, W_ROPE + 1)
            pe.wait_ge(mod_read, 4)
            s = W_ROPE % 2
            for k in range(KT):
                ins = three(ps[:, 7, 0:SEQ], (w_hi[:, s, k * P:(k + 1) * P], w_lo[:, s, k * P:(k + 1) * P]),
                            (a_hi[:, k, :], a_lo[:, k, :]), k == 0, k == KT - 1)
            ins.then_inc(w_used, 1)

            def pair_unit(w, q, bank, act_tiles=None):
                pe.wait_ge(lo_ready, w + 1)
                for j in range(2):
                    for k in range(8):
                        if act_tiles is not None and j == 0:
                            pe.wait_ge(alo_ready, act_tiles + 8 * q + k + 1)
                        c = k * 256 + j * P
                        ins = three(ps[:, bank + j, 0:SEQ], (w_hi[:, w % 2, c:c + P], w_lo[:, w % 2, c:c + P]),
                                    (a_hi[:, 8 * q + k, :], a_lo[:, 8 * q + k, :]),
                                    q == 0 and k == 0, q == 1 and k == 7)
                ins.then_inc(w_used, 1)

            def u_unit(i):
                if i == 0:
                    pe.wait_ge(lat_ready, 2)
                if i == 2:
                    pe.wait_ge(rope_raw, 1)
                    pe.wait_ge(std_ready, 3)
                if i in (4, 6):
                    pe.wait_ge(u_out, i // 2 - 1)
                pair_unit(W_U + i, i % 2, 4 + 2 * ((i // 2) % 2))

            b3 = [0]

            def take_b3():
                if b3[0]:
                    pe.wait_ge(b3_read, b3[0])
                b3[0] += 1

            def conv(hp):
                take_b3()
                pe.wait_ge(ada_used, 8 * (hp + 1))
                for f in range(8):
                    ins = mm(ps[:, 3, f:f + 1], acc[:, hp % 2, f * P:(f + 1) * P], ones[:, 0:1], start=True, stop=True)
                ins.then_inc(b3_ready, 1)

            def swap_halves(src, n):
                take_b3()
                if n is None:
                    pe.wait_ge(rope_raw, 1)
                else:
                    pe.wait_ge(proj_out, n)
                mm(ps[:, 3, 0:SEQ], swap, src, start=True, stop=True).then_inc(b3_ready, 1)

            proj = [0]

            def project(terms, width):
                n = proj[0]
                if n >= 3:
                    pe.wait_ge(proj_out, n - 2)
                dst = ps[:, n % 3, 0:width]
                for m, (x, y) in enumerate(terms):
                    ins = mm(dst, x, y, start=(m == 0), stop=(m == len(terms) - 1))
                ins.then_inc(proj_ready, 1)
                proj[0] += 1
                return ins

            def kvb_unit(g):
                n = ring_number["kvb", g]
                arrived(pe, n)
                w = raw[:, n % RING, :].rearrange("p (k h c) -> p k h c", k=2, c=NOPE + VD)
                for h in range(4):
                    project([(w[:, k, h, 0:NOPE], kv_lat[:, k, :]) for k in range(2)], SEQ)
                for t in range(2):
                    m = proj[0]
                    pe.wait_ge(proj_out, m - 2)
                    for k in range(2):
                        ins = mm(ps[:, m % 3, :].rearrange("p (h c) -> p h c", c=P), kv_lat[:, k, t * P:(t + 1) * P],
                                 w[:, k, :, NOPE:NOPE + VD], start=(k == 0), stop=(k == 1))
                    ins.then_inc(proj_ready, 1)
                    proj[0] += 1

            def qb_unit(i):
                n = ring_number["qb", i]
                arrived(pe, n)
                w = raw[:, n % RING, 0:1536].rearrange("p (k c) -> p k c", k=4)
                m = proj[0]
                pe.wait_ge(proj_out, m - 2)
                for k in range(4):
                    ins = mm(ps[:, m % 3, 0:SEQ], w[:, k, 2 * NOPE:2 * QHD], q_lat[:, k, :], start=(k == 0), stop=(k == 3))
                ins.then_inc(proj_ready, 1)
                proj[0] += 1
                for h in range(2):
                    project([(w[:, k, h * NOPE:(h + 1) * NOPE], q_lat[:, k, :]) for k in range(4)], SEQ)

            u_unit(0)
            add_squares("kv", 0, ps[:, 6, 0:SEQ])
            for j in range(2):
                if j == 0:
                    pe.wait_ge(rope_raw, 1)
                add_squares("q", j, ps[:, 7, 0:SEQ])
            u_unit(1)
            pe.wait_ge(vgelu_ready, 1)
            pe.wait_ge(latn_ready, 2)
            kvb_unit(0)
            swap_halves(k_pe, None)
            kvb_unit(1)
            pe.wait_ge(latn_ready, 6)
            qb_unit(0)
            conv(0)
            qb_unit(1)
            swap_halves(q_pe[:, 0, :], 13)
            qb_unit(2)
            swap_halves(q_pe[:, 1, :], 16)
            qb_unit(3)
            swap_halves(q_pe[:, 2, :], 19)
            swap_halves(q_pe[:, 3, :], 22)

            def scores(h):
                r = (h % 2) * 64
                if h:
                    pe.wait_ge(exp_ready, 2 * h)
                else:
                    pe.wait_ge(proj_out, 24)
                pe.wait_ge(pe_rot, 2 + h // 2)
                for b in range(2):
                    dst = ps[:, 0, 128 * b:128 + 256 * b]
                    keys = P * (b + 1)
                    mm(dst, qT[:, h, b * P:(b + 1) * P], kT[:, h, 0:keys], start=True, stop=False)
                    ins = mm(dst, q_pe[r:r + 64, h // 2, b * P:(b + 1) * P], k_pe[r:r + 64, 0:keys],
                             start=False, stop=True)
                ins.then_inc(s_ready, 1)

            def transposes(h):
                pe.wait_ge(p_ready, h + 1)
                if h:
                    pe.wait_ge(pt_out, h)
                for b in range(3):
                    ins = nc.tensor.transpose(ps[:, 1, b * P:(b + 1) * P], prob[:, h % 2, b * P:(b + 1) * P], ident)
                ins.then_inc(pt_ready, 1)

            def values(h):
                pe.wait_ge(pt_out, h + 1)
                if h:
                    pe.wait_ge(m_out, h)
                pt = probT[:, h % 2, :]
                mm(ps[:, 2, 0:SEQ], v_att[:, 0, h * P:(h + 1) * P], pt[:, 0:256], start=True, stop=False,
                   skip_group_check=True)
                mm(ps[:, 2, P:SEQ], v_att[:, 1, h * P:(h + 1) * P], pt[:, 256:384], start=False, stop=True,
                   skip_group_check=True).then_inc(pv_ready, 1)

            def spatial(half):
                if half == 0:
                    pe.wait_ge(vnorm_ready, 2)
                    pe.wait_ge(ws_masked, 1)
                    pe.wait_ge(u_out, 3)
                else:
                    pe.wait_ge(u_out, 4)
                for g in range(4 * half, 4 * half + 4):
                    for n in range(2):
                        c = (g % 2) * 256 + n * P
                        ins = mm(ps[:, 4 + g // 2, c:c + P], v_tok[:, n, g * P:(g + 1) * P],
                                 wsT[:, g * P:(g + 1) * P], start=True, stop=True)
                ins.then_inc(gm_ready, 1)

            for j in range(8):
                scores(j)
                if j < 6:
                    u_unit(2 + j)
                if j == 6:
                    spatial(0)
                    spatial(1)
                    pe.wait_ge(b3_read, b3[0])
                    add_squares("m", 0, ps[:, 3, 0:SEQ])
                    add_squares("m", 1, ps[:, 3, 0:SEQ])
                if j == 7:
                    add_squares("m", 2, ps[:, 3, 0:SEQ])
                if j:
                    values(j - 1)
                transposes(j)
                if j == 0:
                    conv(1)
                if j == 4:
                    conv(2)
            for j in range(4):
                add_squares("a", j, ps[:, 0, 0:SEQ])
                if j == 1:
                    values(7)
            add_squares("m", 3, ps[:, 3, 0:SEQ])

            for i in range(16):
                p = i // 2
                if p < 2:
                    pe.wait_ge(gm_out, 8)
                elif i % 2 == 0:
                    pe.wait_ge(y_out, 2 * p - 2)
                pair_unit(W_O + i, i % 2, 4 + 2 * (p % 2), act_tiles=16 if i < 2 else None)
                if i % 2 and p:
                    if p == 1:
                        pe.wait_ge(m_out, 8)
                    add_squares("y", p - 1, ps[:, 2, 0:SEQ])
                if 15 + i in CONV_AFTER:
                    conv(CONV_AFTER[15 + i])
            add_squares("y", 7, ps[:, 2, 0:SEQ])
            pe.wait_ge(std_ready, 4)
            for j in range(8):
                add_squares("x1", j, ps[:, 1, 0:SEQ])

            def ff1_unit(i, j, w_wait, bank_wait, act_waits):
                w = (W_F1 + j) % 2
                q = j % 2
                pe.wait_ge(lo_ready, w_wait)
                if bank_wait is not None:
                    pe.wait_ge(h1_ready, bank_wait)
                for c in range(2):
                    for k in range(8):
                        if act_waits and c == 0:
                            pe.wait_ge(alo_ready, 32 + 8 * q + k + 1)
                        o = k * 256 + c * P
                        ins = three(ps[:, 2 * (j // 2) + c, 0:SEQ], (w_hi[:, w, o:o + P], w_lo[:, w, o:o + P]),
                                    (a_hi[:, 8 * q + k, :], a_lo[:, 8 * q + k, :]),
                                    q == 0 and k == 0, q == 1 and k == 7)
                        if q == 1 and k == 7 and c == 0:
                            ins.then_inc(z_ready, 1)
                ins.then_inc(w_used, 1)

            pe.wait_ge(std_ready, 7)
            pe.wait_ge(b3_read, 11)
            for j in range(4):
                ff1_unit(0, j, W_F1 + j + 1, None, j < 2)
            with pe.Fori(1, 16) as i:
                for j in range(4):
                    ff1_unit(i, j, i * 4 + (W_F1 + j + 1), i * 4 + (2 * (j // 2) - 2) if j % 2 == 0 else None, False)

            pe.wait_ge(ada_used, 64)
            for f in range(16):
                ins = mm(ps[:, 7, f:f + 1], acc[:, f // 8, (f % 8) * P:(f % 8 + 1) * P], ones[:, 0:1],
                         start=True, stop=True)
            ins.then_inc(g2_sum, 1)

            def ff2_dst(d):
                return ps[:, d // 2, (d % 2) * SEQ:(d % 2 + 1) * SEQ]

            def ff2_part(w, j, d, first, last):
                return three(ff2_dst(d), (w_hi[:, w, d * P:(d + 1) * P], w_lo[:, w, d * P:(d + 1) * P]),
                             (a_hi[:, j, :], a_lo[:, j, :]), first and d % 2 == 0, last)

            def ff2_unit(j, w_wait, a_wait, first=False):
                w = (W_F2 + j) % 2
                pe.wait_ge(lo_ready, w_wait)
                pe.wait_ge(alo_ready, a_wait)
                for d in range(16):
                    if first and d == 14:
                        pe.wait_ge(g2_ready, 1)
                    ins = ff2_part(w, j, d, first, False)
                ins.then_inc(w_used, 1)

            pe.wait_ge(h1_ready, 64)
            for j in range(4):
                ff2_unit(j, W_F2 + j + 1, 48 + j + 1, first=(j == 0))
            with pe.Fori(1, 15) as i:
                for j in range(4):
                    ff2_unit(j, i * 4 + (W_F2 + j + 1), i * 4 + (48 + j + 1))
            for j in range(2):
                ff2_unit(j, W_F2 + 60 + j + 1, 48 + 60 + j + 1)
            pe.wait_ge(lo_ready, W_F2 + 64)
            pe.wait_ge(alo_ready, 48 + 64)
            for d in range(16):
                for j in (2, 3):
                    ins = ff2_part((W_F2 + j) % 2, j, d, False, j == 3)
                if d % 2:
                    ins.then_inc(f_ready, 1)
            for j in range(8):
                if j == 0:
                    pe.wait_ge(f_out, 2)
                add_squares("f", j, ps[:, 0, 0:SEQ])


CONV_B3 = [1, 6, 7, 8, 9, 10]

_COLUMNS = [("c", "c"), ("b_ada", "b_ada"), ("pre1", "pre_norm1_g"), ("post1", "post_norm1_g"),
            ("pre2", "pre_norm2_g"), ("post2", "post_norm2_g"), ("qn", "q_norm_g"), ("kvn", "kv_norm_g"),
            ("ga", "grp_norm_a_g"), ("gb", "grp_norm_b_g")]


def kernel(**inputs):
    import numpy as np
    import concourse.bacc as bacc
    from concourse.bass_utils import run_bass_kernel_spmd

    a = {k: np.asarray(v) for k, v in inputs.items()}
    qb = a["w_q_b"][0].reshape(QL, HEADS // 2, 2, QHD)
    qb = np.concatenate([qb[..., :NOPE].reshape(QL, 4, 2 * NOPE), qb[..., NOPE:].reshape(QL, 4, 2 * ROPE)], axis=2)
    arrays = {
        "xT": np.ascontiguousarray(a["x"][0].T),
        "positions": a["positions"].reshape(1, SEQ),
        "cols": np.ascontiguousarray(np.concatenate([a[src].reshape(-1, P) for _, src in _COLUMNS], axis=0).T),
        "w_sT": np.ascontiguousarray(a["w_s"][0].transpose(2, 0, 1)).reshape(P, GROUPS * P),
        "b_s": a["b_s"].reshape(1, GROUPS * P),
        "ln_v_g": a["ln_v_g"].reshape(1, GW),
        "ln_v_b": a["ln_v_b"].reshape(1, GW),
        "w_ada": a["w_ada"][0], "w_in": a["w_in"][0], "w_q_b": np.ascontiguousarray(qb.reshape(QL, HEADS * QHD)), "w_kv_b": a["w_kv_b"][0],
        "w_o": a["w_o"][0], "w_ff1": a["w_ff1"][0], "w_ff2": a["w_ff2"][0],
    }
    consts = np.zeros((P, NCONST), np.float32)
    rows = np.arange(P)
    consts[rows, C_IDENT + rows] = 1.0
    consts[rows, C_SWAP + (rows ^ 32)] = 1.0
    f = np.float32(ROPE_THETA) ** (-np.arange(0, ROPE, 2, dtype=np.float32) / np.float32(ROPE))
    consts[:, C_FREQ] = np.where(rows % 64 < 32, -1.0, 1.0) * f[rows % 32]
    arrays["consts"] = consts

    nc = bacc.Bacc("TRN2", target_bir_lowering=False, num_devices=1)
    aps = {k: nc.dram_tensor("in_" + k, v.shape, mybir.dt.from_np(v.dtype), kind="ExternalInput").ap() for k, v in arrays.items()}
    out = nc.dram_tensor("outT", (D, SEQ), mybir.dt.float32, kind="ExternalOutput").ap()
    block_kernel(nc, aps, out)
    r = run_bass_kernel_spmd(nc, [{"in_" + k: v for k, v in arrays.items()}], core_ids=[0])
    return np.ascontiguousarray(r.results[0]["outT"].T).reshape(1, SEQ, D)
```

```python
import concourse.bass as bass
from concourse import mybir
from contextlib import ExitStack

P = 128
SEQ = 256
D = 2048
KT = D // P
CHUNK = 64
GW = 1024
GROUPS = 8
HEADS = 8
NOPE, ROPE, VD = 128, 64, 128
QL, KVL = 512, 256
QHD = NOPE + ROPE
DFF = 8192
FT = DFF // P
EPS = 1e-6
NEG = -1e30
ROPE_THETA = 10000.0
UNIT = 2048
RING = 4

COLS = {}
_at = 0
for _name, _n in (("c", 16), ("b_ada", 96), ("pre1", 16), ("post1", 16), ("pre2", 16), ("post2", 16),
                  ("qn", 4), ("kvn", 2), ("ga", 8), ("gb", 8)):
    COLS[_name] = (_at, _at + _n)
    _at += _n
NCOLS = _at
C_IDENT, C_SWAP, C_FREQ, NCONST = 0, 128, 256, 257

TWO_PI = (6.28125, 0.0019350051879882812, 3.0199159819504e-07)
ROUND = 12582912.0
PI = 3.1415925

NORMS = {"x": 8, "kv": 1, "q": 2, "a": 4, "m": 4, "y": 8, "x1": 8, "f": 1}
FOLDED = ("y",)
NORM_NUMBER = {_name: _i for _i, _name in enumerate(NORMS)}
FIRST_F = 6
CHUNKS = ([("x", _j) for _j in range(8)] + [("kv", 0), ("q", 0), ("q", 1), ("m", 0), ("m", 1), ("m", 2)]
          + [("a", _j) for _j in range(4)] + [("m", 3)]
          + [(_name, _j) for _name in ("y", "x1") for _j in range(8)] + [("f", 0)])

W_ROPE = KT
W_U = W_ROPE + 1
W_O = W_U + 8
W_F1A = W_O + 16
W_F1 = W_F1A + KT
TILES_A = 12
TURNS = (FT - TILES_A) // 4
W_F2 = W_F1 + 4 * TURNS

ITEMS = ([("in", k) for k in range(KT)] + [("rope", 0), ("u", 0), ("u", 1), ("kvb", 0), ("kvb", 1)]
         + [("qb", i) for i in range(4)] + [("u", i) for i in range(2, 8)] + [("wo", i) for i in range(16)]
         + [("f1", k) for k in range(KT)])
ADA_AFTER = {("in", 12): 1, ("in", 13): 1, ("in", 14): 1, ("in", 15): 2, ("rope", 0): 1, ("u", 0): 1, ("u", 1): 1,
             ("kvb", 0): 1, ("kvb", 1): 1, ("qb", 0): 1, ("qb", 1): 1, ("qb", 2): 1, ("qb", 3): 1, ("u", 2): 1,
             ("u", 7): 1, ("wo", 0): 1, ("wo", 1): 3, ("wo", 2): 1, ("wo", 3): 1, ("wo", 4): 1, ("wo", 5): 1}
ADA_AFTER.update({("u", i): 2 for i in range(3, 7)})
LATE_AFTER = {("wo", 7 + i): (i,) for i in range(8)}
LATE_AFTER.update({("wo", 15): (8, 9, 10), ("f1", 1): (11, 12), ("f1", 2): (13,), ("f1", 3): (14,), ("f1", 4): (15,)})
LATE_COUNT = 16
LATE_SUM = 5
STREAM = []
ADA_UNITS = {}
_at = 0
for _item in ITEMS:
    STREAM.append(_item)
    ADA_UNITS[_item] = range(_at, _at + ADA_AFTER.get(_item, 0))
    STREAM += [("ada", i) for i in ADA_UNITS[_item]]
    STREAM += [("late", i) for i in LATE_AFTER.get(_item, ())]
    _at += ADA_AFTER.get(_item, 0)
ADA_COUNT = _at
RING_NUMBER = {_item: _i for _i, _item in enumerate(STREAM)}
N_FF1 = len(STREAM)
N_FF2 = N_FF1 + 4 * TURNS
ADA_HALVES = [(2 * D, 32), (2 * D + 1024, 40), (4 * D, 64), (3 * D, 48)]
LATE_HALVES = [(4 * D + 1024, 72), (3 * D + 1024, 56)]
G2_AFTER = (9, 12, 15)
CONV_AFTER = {6: 3}
SPLIT_NUMBER = {"in": 0, "rope": W_ROPE, "u": W_U, "wo": W_O, "f1": W_F1A}
SPLIT_ITEMS = {SPLIT_NUMBER[_kind] + _i: (_kind, _i) for _kind, _i in ITEMS if _kind in SPLIT_NUMBER}


def block_kernel(nc, A, out):
    f32, f32r, i32 = mybir.dt.float32, mybir.dt.float32r, mybir.dt.int32
    ALU = mybir.AluOpType
    ACT = mybir.ActivationFunctionType
    AX = mybir.AxisListType

    w_ada, w_in, w_qb, w_kvb = A["w_ada"], A["w_in"], A["w_q_b"], A["w_kv_b"]
    w_o, w_ff1, w_ff2 = A["w_o"], A["w_ff1"], A["w_ff2"]

    ctx = ExitStack()
    with ctx:
        def sb(name, shape, dt=f32):
            return ctx.enter_context(nc.sbuf_tensor(name, shape, dt))

        def sem(name):
            return ctx.enter_context(nc.semaphore(name))

        xT = sb("xT", [P, KT, SEQ])
        big = sb("big", [P, FT * SEQ])
        raw = sb("raw", [P, RING, UNIT])
        w_hi = sb("w_hi", [P, 2, UNIT], f32r)
        w_lo = sb("w_lo", [P, 2, UNIT], f32r)
        a_hi = sb("a_hi", [P, KT, SEQ], f32r)
        a_lo = sb("a_lo", [P, KT, SEQ], f32r)
        cols = sb("cols", [P, NCOLS])
        cst = sb("cst", [P, NCONST])
        ones = sb("ones", [P, P])
        eps = sb("eps", [P, 1])
        cs = sb("cs", [P, KT])
        mods = sb("mods", [P, 96])
        gain1 = sb("gain1", [P, KT])
        gain2 = sb("gain2", [P, KT])
        gate1 = sb("gate1", [P, KT])
        gate2 = sb("gate2", [P, KT])
        cosT = sb("cosT", [P, SEQ])
        sinT = sb("sinT", [P, SEQ])
        std = sb("std", [P, SEQ])
        R = sb("R", [P, SEQ])
        h32 = sb("h32", [P, 2, SEQ])
        sqb = sb("sqb", [P, 2, 2 * SEQ])
        gm_w = sb("gm_w", [P, 2048])
        acc = sb("acc", [P, 2, 1024])
        mx = sb("mx", [P, 2])
        nb = sb("nb", [P, 2])
        rsum = sb("rsum", [P, 2])
        rinv = sb("rinv", [P, 2])
        bst = sb("bst", [P, 2, 2, 6])
        mv = sb("mv", [P, 2, 2])
        vstd = sb("vstd", [P, 2])
        vrs = sb("vrs", [P, 2])
        ps = ctx.enter_context(nc.psum_tensor("ps", [P, 8, 512], f32))

        wsT = gm_w[:, 0:1024]
        bs_rows = gm_w[:, 1024:2048]
        ada_g2 = gm_w
        ident = cst[:, C_IDENT:C_IDENT + P]
        swap = cst[:, C_SWAP:C_SWAP + P]
        freq = cst[:, C_FREQ:C_FREQ + 1]

        def region(lo, n):
            return big[:, lo:lo + n]
        ada_ring = region(0, 8 * UNIT).rearrange("p (s n) -> p s n", s=8)
        rope_a = raw[:, 0, 0:512].rearrange("p (s n) -> p s n", s=2)
        v_tok = region(0, 2048).rearrange("p (t n) -> p t n", t=2)
        u_all = region(2048, 2048)
        u_t = u_all.rearrange("p (t n) -> p t n", n=SEQ)
        q_lat = region(4096, 1024).rearrange("p (t n) -> p t n", n=SEQ)
        kv_lat = region(5120, 512).rearrange("p (t n) -> p t n", n=SEQ)
        prob = region(4096, 768).rearrange("p (s n) -> p s n", s=2)
        probT = region(4864, 768).rearrange("p (s n) -> p s n", s=2)
        k_pe = region(5632, 256)
        qT = region(5888, 2048).rearrange("p (t n) -> p t n", n=SEQ)
        q_pe = region(7936, 1024).rearrange("p (t n) -> p t n", n=SEQ)
        kT = region(8960, 2048).rearrange("p (t n) -> p t n", n=SEQ)
        v_att = region(11008, 2048).rearrange("p (t n) -> p t n", t=2)
        m_all = region(13056, 2048)
        m_t = m_all.rearrange("p (t n) -> p t n", n=SEQ)
        ln_rows = m_all.rearrange("p (t n) -> p t n", t=2)
        rtmp = region(15104, 256)
        y_all = region(6144, 4096)
        y_t = y_all.rearrange("p (t n) -> p t n", n=SEQ)
        f_t = region(0, 4096).rearrange("p (t n) -> p t n", n=SEQ)
        h1 = big

        small_in = sem("small_in")
        x_in = sem("x_in")
        gm_in = sem("gm_in")
        ws_masked = sem("ws_masked")
        ln_in = sem("ln_in")
        raw_in = [sem(f"raw_in{s}") for s in range(RING)]
        ada_in = [sem(f"ada_in{s}") for s in range(8)]
        g2_in = sem("g2_in")
        out_done = sem("out_done")
        consts_ready = sem("consts_ready")
        cs_ready = sem("cs_ready")
        hi_ready = sem("hi_ready")
        lo_ready = sem("lo_ready")
        w_used = sem("w_used")
        ada_pe_used = sem("ada_pe_used")
        acc_step = sem("acc_step")
        ada_used = sem("ada_used")
        late_sum = sem("late_sum")
        late_read = sem("late_read")
        acc_cleared = sem("acc_cleared")
        mod_sum = sem("mod_sum")
        mod_read = sem("mod_read")
        act32_ready = sem("act32_ready")
        ahi_ready = sem("ahi_ready")
        alo_ready = sem("alo_ready")
        sq_ready = sem("sq_ready")
        sq_folded = sem("sq_folded")
        sq_used = sem("sq_used")
        std_ready = sem("std_ready")
        inv_ready = sem("inv_ready")
        ang_ready = sem("ang_ready")
        trig_ready = sem("trig_ready")
        lat_ready = sem("lat_ready")
        vgelu_ready = sem("vgelu_ready")
        vstat_ready = sem("vstat_ready")
        vstd_ready = sem("vstd_ready")
        vnorm_ready = sem("vnorm_ready")
        latn_ready = sem("latn_ready")
        rope_raw = sem("rope_raw")
        proj_ready = sem("proj_ready")
        proj_out = sem("proj_out")
        b3_ready = sem("b3_ready")
        b3_read = sem("b3_read")
        pe_rot = sem("pe_rot")
        u_out = sem("u_out")
        s_ready = sem("s_ready")
        nb_ready = sem("nb_ready")
        exp_ready = sem("exp_ready")
        p_ready = sem("p_ready")
        pt_ready = sem("pt_ready")
        pt_out = sem("pt_out")
        pv_ready = sem("pv_ready")
        m_out = sem("m_out")
        gelu_u = sem("gelu_u")
        gm_ready = sem("gm_ready")
        gm_out = sem("gm_out")
        y_half = sem("y_half")
        y_out = sem("y_out")
        gate_ready = sem("gate_ready")
        x1_ready = sem("x1_ready")
        z_ready = sem("z_ready")
        relu_ready = sem("relu_ready")
        h1_ready = sem("h1_ready")
        g2_sum = sem("g2_sum")
        g2_ready = sem("g2_ready")
        f_ready = sem("f_ready")
        f_squares = sem("f_squares")
        f_summed = sem("f_summed")
        f_out = sem("f_out")
        o_ready = sem("o_ready")
        act_step = sem("act_step")
        dve_step = sem("dve_step")

        G2_BASE = ADA_COUNT + LATE_COUNT
        H1_DONE = TILES_A // 2 + 2 * TURNS

        def col(name, t=0, n=1):
            return cols[:, COLS[name][0] + t:COLS[name][0] + t + n]

        def consumer(n):
            if n >= N_FF1:
                return lo_ready, W_F1 + n - N_FF1 + 1
            kind, i = STREAM[n]
            if kind == "ada":
                return ada_used, i + 1
            if kind == "late":
                return ada_used, ADA_COUNT + i + 1
            if kind == "kvb":
                return proj_ready, 6 * (i + 1)
            if kind == "qb":
                return proj_ready, 12 + 3 * (i + 1)
            return lo_ready, SPLIT_NUMBER[kind] + i + 1

        def arrivals(n):
            return 16 * (n // RING + 1)

        def arrived(eng, n):
            eng.wait_ge(raw_in[n % RING], arrivals(n))

        block = ctx.enter_context(nc.Block())

        @block.sync
        def _(sp):
            def load_ada(q, r):
                for part in range(2):
                    if q:
                        if r == 0:
                            sp.wait_ge(ada_pe_used, q)
                        else:
                            sp.wait_ge(acc_step, 24 * (q - 1) + 8 * r - 1 + part)
                    c0 = (1 - part) * D + q * 512
                    sp.dma_start(ada_ring[:, 2 * r + part, :].rearrange("p (k c) -> p k c", c=512),
                                 w_ada[r * 512:(r + 1) * 512, c0:c0 + 512].rearrange("(k p) c -> p k c", p=P)
                                 ).then_inc(ada_in[2 * r + part], 16)

            def slot_free(n):
                if n >= RING:
                    sp.wait_ge(*consumer(n - RING))

            load_ada(0, 0)
            sp.dma_start(xT[:, :, :], A["xT"].rearrange("(t p) n -> p t n", p=P)).then_inc(x_in, 16)
            for r in range(1, 4):
                load_ada(0, r)
            sp.wait_ge(trig_ready, 2)
            for n, (kind, i) in enumerate(STREAM):
                if kind == "in" and 2 <= i < 14:
                    for r in ((0, 1), (2,), (3,), ())[(i - 2) % 4]:
                        load_ada((i - 2) // 4 + 1, r)
                slot_free(n)
                slot = raw[:, n % RING, :]
                if kind == "in":
                    dst, src = slot[:, 0:1792], w_in[i * P:(i + 1) * P, 1024:2816]
                elif kind == "rope":
                    dst = slot[:, 0:1024].rearrange("p (k c) -> p k c", c=64)
                    src = w_in[:, 2816:2880].rearrange("(k p) c -> p k c", p=P)
                elif kind in ("u", "wo"):
                    dst = slot.rearrange("p (k c) -> p k c", c=512)
                    r0, c0 = (i % 4) * 512, (i // 4) * 512
                    src = (w_in if kind == "u" else w_o)[r0:r0 + 512, c0:c0 + 512].rearrange("(k p) c -> p k c", p=P)
                elif kind == "kvb":
                    dst = slot.rearrange("p (k c) -> p k c", c=1024)
                    src = w_kvb[:, i * 1024:(i + 1) * 1024].rearrange("(k p) c -> p k c", p=P)
                elif kind == "qb":
                    dst = slot[:, 0:1536].rearrange("p (k c) -> p k c", c=384)
                    src = w_qb[:, i * 384:(i + 1) * 384].rearrange("(k p) c -> p k c", p=P)
                elif kind == "f1":
                    dst, src = slot[:, 0:TILES_A * P], w_ff1[i * P:(i + 1) * P, 0:TILES_A * P]
                else:
                    if kind == "ada":
                        c0, r0 = ADA_HALVES[i // 8][0], (i % 8) * 256
                    else:
                        c0, r0 = LATE_HALVES[i // 8][0], (i % 8) * 256
                    dst = slot.rearrange("p (k c) -> p k c", c=1024)
                    src = w_ada[r0:r0 + 256, c0:c0 + 1024].rearrange("(k p) c -> p k c", p=P)
                sp.dma_start(dst, src).then_inc(raw_in[n % RING], 16)

            def load_ff1(i, j, after):
                sp.wait_ge(*after)
                s = (N_FF1 + j) % RING
                c0 = i * 1024 + (TILES_A * P + (j // 4) * 512)
                r0 = (j % 4) * 512
                sp.dma_start(raw[:, s, :].rearrange("p (k c) -> p k c", c=512),
                             w_ff1[r0:r0 + 512, bass.ds(c0, 512)].rearrange("(k p) c -> p k c", p=P)
                             ).then_inc(raw_in[s], 16)

            for j in range(4):
                load_ff1(0, j, consumer(N_FF1 + j - RING))
            for j in range(4, 8):
                load_ff1(0, j, (lo_ready, W_F1 + j - 3))
            with sp.Fori(1, TURNS // 2) as i:
                for j in range(8):
                    load_ff1(i, j, (lo_ready, i * 8 + (W_F1 + j - 3)))
            for j in range(4):
                load_ff1(TURNS // 2, j, (lo_ready, W_F2 - 4 + j - 3))

            def load_ff2(i, j, n):
                sp.wait_ge(lo_ready, n)
                s = (N_FF2 + j) % RING
                sp.dma_start(raw[:, s, :], w_ff2[bass.ds(i * 512 + j * P, P), :]).then_inc(raw_in[s], 16)

            with sp.Fori(0, 16) as i:
                for j in range(4):
                    load_ff2(i, j, i * 4 + (W_F2 + j - 3))
            for g in range(4):
                sp.wait_ge(o_ready, 2 * g + 2)
                sp.dma_start(out[g * 512:(g + 1) * 512, :].rearrange("(t p) n -> p t n", p=P),
                             xT[:, 4 * g:4 * g + 4, :]).then_inc(out_done, 16)
            sp.wait_ge(out_done, 64)

        @block.gpsimd
        def _(pool):
            nc.gpsimd.memset(ones[:, :], 1.0).then_inc(consts_ready, 1)
            nc.gpsimd.memset(eps[:, :], EPS).then_inc(consts_ready, 1)
            pool.wait_ge(consts_ready, 2)
            pool.wait_ge(gm_in, 32)
            nc.gpsimd.memset(wsT.rearrange("p (g i) -> p g i", i=P)[CHUNK:P, :, 0:CHUNK], 0.0).then_inc(ws_masked, 1)
            pool.wait_ge(ws_masked, 1)
            pool.wait_ge(late_sum, 1)
            nc.gpsimd.memset(acc[:, :, :], 0.0).then_inc(acc_cleared, 1)
            pool.wait_ge(gm_out, 8)
            pool.dma_start(ada_g2[:, :], w_ada[0:P, 5 * D:6 * D]).then_inc(g2_in, 16)
            with pool.Fori(1, KT) as row:
                pool.wait_ge(ada_used, row + G2_BASE)
                pool.dma_start(ada_g2[:, :], w_ada[bass.ds(row * P, P), 5 * D:6 * D]).then_inc(g2_in, 16)

        @block.scalar
        def _(act):
            steps = [0]

            def link(ins):
                steps[0] += 1
                ins.then_inc(act_step, 1)
                act.wait_ge(act_step, steps[0])

            act.dma_start(cols[:, :], A["cols"]).then_inc(small_in, 16)
            act.dma_start(cst[:, :], A["consts"]).then_inc(small_in, 16)
            act.dma_start(h32[:, 0, :].bitcast(i32), A["positions"].to_broadcast([P, SEQ])).then_inc(small_in, 16)
            act.dma_start(wsT, A["w_sT"]).then_inc(gm_in, 16)
            act.dma_start(bs_rows, A["b_s"].to_broadcast([P, 1024])).then_inc(gm_in, 16)
            act.wait_ge(small_in, 48)
            nc.scalar.activation(cs[:, :], col("c", 0, 16), ACT.Silu).then_inc(cs_ready, 1)

            def split_hi(w):
                n = RING_NUMBER[SPLIT_ITEMS[w]] if w < W_F1 else N_FF1 + w - W_F1
                arrived(act, n)
                if w >= 2:
                    act.wait_ge(w_used, w - 1)
                src, dst = raw[:, n % RING, :], w_hi[:, w % 2, :]
                if w < KT or w >= W_F1A and w < W_F1:
                    width = 1792 if w < KT else TILES_A * P
                    src, dst = src[:, 0:width], dst[:, 0:width]
                elif w == W_ROPE:
                    for r in range(2):
                        ins = nc.scalar.activation(
                            dst.rearrange("p (k r c) -> p k r c", r=2, c=64)[:, :, r, :],
                            src[:, 0:1024].rearrange("p (k c) -> p k c", c=64), ACT.Copy)
                    ins.then_inc(hi_ready, 1)
                    return
                nc.scalar.activation(dst, src, ACT.Copy).then_inc(hi_ready, 1)

            def act_hi(n, slot, shift=None):
                act.wait_ge(act32_ready, n + 1)
                if shift is None:
                    ins = nc.scalar.activation(a_hi[:, slot, :], h32[:, n % 2, :], ACT.Copy)
                else:
                    ins = nc.scalar.activation(a_hi[:, slot, :], h32[:, n % 2, :], ACT.Identity,
                                               bias=mods[:, shift + slot:shift + slot + 1])
                ins.then_inc(ahi_ready, 1)

            def squares(name, j, src):
                g = CHUNKS.index((name, j))
                if g >= 2:
                    act.wait_ge(sq_used, g - 1)
                dst = sqb[:, g % 2, :]
                if len(src.shape) == 3:
                    dst = dst.rearrange("p (t n) -> p t n", t=2)
                nc.scalar.activation(dst, src, ACT.Square).then_inc(sq_ready, 1)

            def make_std(name, width, src):
                i = NORM_NUMBER[name]
                act.wait_ge(sq_used, CHUNKS.index((name, NORMS[name] - 1)) + 1)
                if i:
                    act.wait_ge(inv_ready, i)
                nc.scalar.activation(std[:, :], src, ACT.Sqrt, bias=eps[:, 0:1], scale=1.0 / width).then_inc(std_ready, 1)

            act.wait_ge(ang_ready, 1)
            nc.scalar.activation(sinT[:, :], rope_a[:, 0, :], ACT.Sin).then_inc(trig_ready, 1)
            nc.scalar.activation(cosT[:, :], rope_a[:, 1, :], ACT.Sin).then_inc(trig_ready, 1)
            act.wait_ge(x_in, 16)
            act.wait_ge(consts_ready, 2)
            for j in range(8):
                squares("x", j, xT[:, 2 * j:2 * j + 2, :].rearrange("p t n -> p (t n)"))
            make_std("x", D, ps[:, 0, 0:SEQ])

            for k in range(KT):
                split_hi(k)
                act_hi(k, k, shift=0)
            split_hi(W_ROPE)
            act.wait_ge(w_used, KT)
            nc.scalar.activation(kv_lat.rearrange("p t n -> p (t n)"), ps[:, 6, :], ACT.Copy).then_inc(lat_ready, 1)
            nc.scalar.activation(q_lat.rearrange("p t n -> p (t n)"), ps[:, 4:6, :].rearrange("p b n -> p (b n)"),
                                 ACT.Copy).then_inc(lat_ready, 1)
            act.wait_ge(lat_ready, 2)
            act.wait_ge(acc_step, 96)
            act.wait_ge(ada_pe_used, 4)
            for i, name in enumerate(("ln_v_g", "ln_v_b")):
                act.dma_start(ln_rows[:, i, :], A[name].to_broadcast([P, 1024])).then_inc(ln_in, 16)
            squares("kv", 0, kv_lat.rearrange("p t n -> p (t n)"))
            squares("q", 0, q_lat[:, 0:2, :].rearrange("p t n -> p (t n)"))
            split_hi(W_U)
            act.wait_ge(w_used, W_ROPE + 1)
            nc.scalar.activation(k_pe, ps[:, 7, 0:SEQ], ACT.Copy).then_inc(rope_raw, 1)
            squares("q", 1, q_lat[:, 2:4, :].rearrange("p t n -> p (t n)"))
            make_std("kv", KVL, ps[:, 6, 0:SEQ])
            make_std("q", QL, ps[:, 7, 0:SEQ])
            split_hi(W_U + 1)
            nc.scalar.activation(v_tok.rearrange("p t n -> p (t n)"), ps[:, 0:4, :].rearrange("p b n -> p (b n)"),
                                 ACT.Gelu).then_inc(vgelu_ready, 1)

            def u_evac(q):
                act.wait_ge(w_used, W_U + 4 * q + 4)
                nc.scalar.activation(u_all[:, q * 1024:(q + 1) * 1024],
                                     ps[:, 4 + 2 * q:6 + 2 * q, :].rearrange("p b n -> p (b n)"), ACT.Copy).then_inc(u_out, 1)

            proj = [0]

            def proj_evac(dst, width):
                n = proj[0]
                act.wait_ge(proj_ready, n + 1)
                nc.scalar.activation(dst, ps[:, n % 3, 0:width], ACT.Copy).then_inc(proj_out, 1)
                proj[0] += 1

            for g in range(2):
                for h in range(4 * g, 4 * g + 4):
                    proj_evac(kT[:, h, :], SEQ)
                for t in range(2):
                    proj_evac(v_att[:, t, g * 512:(g + 1) * 512], 512)
            for i in range(4):
                proj_evac(q_pe[:, i, :], SEQ)
                proj_evac(qT[:, 2 * i, :], SEQ)
                proj_evac(qT[:, 2 * i + 1, :], SEQ)
            split_hi(W_U + 2)
            act.wait_ge(vstat_ready, 1)
            nc.scalar.activation(vstd[:, :], mv[:, :, 1], ACT.Sqrt, bias=eps[:, 0:1]).then_inc(vstd_ready, 1)
            split_hi(W_U + 3)

            def exps(h):
                act.wait_ge(nb_ready, h + 1)
                s = h % 2
                nc.scalar.activation(prob[:, s, 0:128], ps[:, 0, 0:128], ACT.Exp, bias=nb[:, 0:1],
                                     scale=float(QHD) ** -0.5, accum_out=rsum[:, 0:1]).then_inc(exp_ready, 1)
                nc.scalar.activation(prob[:, s, 128:384], ps[:, 0, 128:384], ACT.Exp, bias=nb[:, 1:2],
                                     scale=float(QHD) ** -0.5, accum_out=rsum[:, 1:2]).then_inc(exp_ready, 1)

            def pt_evac(h):
                act.wait_ge(pt_ready, h + 1)
                nc.scalar.activation(probT[:, h % 2, :], ps[:, 1, 0:384], ACT.Copy).then_inc(pt_out, 1)

            def m_evac(h):
                act.wait_ge(pv_ready, h + 1)
                if h == 0:
                    act.wait_ge(vnorm_ready, 2)
                nc.scalar.activation(m_t[:, h, :], ps[:, 2, 0:SEQ], ACT.Copy).then_inc(m_out, 1)

            for j in range(8):
                exps(j)
                if j == 6:
                    act.wait_ge(u_out, 2)
                    nc.scalar.activation(u_all, u_all, ACT.Gelu).then_inc(gelu_u, 1)
                if j == 7:
                    act.wait_ge(vstd_ready, 1)
                    nc.scalar.activation(vstd[:, 0:1], eps[:, :], ACT.Sqrt)
                if j in (6, 7):
                    for c in ((0, 1) if j == 6 else (2,)):
                        act.wait_ge(m_out, 2 * c + 2)
                        squares("m", c, m_all[:, c * 512:(c + 1) * 512])
                if j:
                    m_evac(j - 1)
                if j == 7:
                    act.wait_ge(gm_out, 4)
                    for c in range(2):
                        squares("a", c, u_all[:, c * 512:(c + 1) * 512])
                pt_evac(j)
                if j in (1, 5):
                    u_evac(j // 4)
                if j < 6:
                    split_hi(W_U + 4 + j)
            for c in range(2, 4):
                act.wait_ge(gm_out, 2 * c + 2)
                squares("a", c, u_all[:, c * 512:(c + 1) * 512])
            m_evac(7)
            make_std("a", GW, ps[:, 0, 0:SEQ])
            act.wait_ge(m_out, 8)
            squares("m", 3, m_all[:, 1536:2048])
            make_std("m", GW, ps[:, 3, 0:SEQ])
            for t in range(16):
                act_hi(16 + t, t)
                if t in (7, 11):
                    split_hi(W_O + 2 + t // 8)

            def y_bank(c):
                b = 4 + c % 4
                squares("y", c, ps[:, b, :])
                for t in range(2):
                    nc.scalar.activation(y_t[:, 2 * c + t, :], ps[:, b, t * SEQ:(t + 1) * SEQ], ACT.Copy,
                                         scale=gate1[:, 2 * c + t:2 * c + t + 1]).then_inc(y_out, 1)

            act.wait_ge(gate_ready, 1)
            for i in range(4, 16):
                split_hi(W_O + i)
                if i % 4 == 1:
                    y_bank(i // 4 * 2 - 2)
                    y_bank(i // 4 * 2 - 1)
            act.wait_ge(y_half, 1)
            y_bank(6)
            split_hi(W_F1A)
            act.wait_ge(w_used, W_O + 16)
            y_bank(7)
            make_std("y", D, ps[:, 2, 0:SEQ])
            for j in range(8):
                if j == 4:
                    split_hi(W_F1A + 1)
                act.wait_ge(x1_ready, j + 1)
                squares("x1", j, xT[:, 2 * j:2 * j + 2, :].rearrange("p t n -> p (t n)"))
            make_std("x1", D, ps[:, 1, 0:SEQ])
            for t in range(8):
                act_hi(32 + t, t, shift=48)
            for k in range(2, 7):
                split_hi(W_F1A + k)
            for t in range(8, 13):
                act_hi(32 + t, t, shift=48)
            split_hi(W_F1A + 7)
            for t in range(13, 16):
                act_hi(32 + t, t, shift=48)
            for k in range(8, 16):
                split_hi(W_F1A + k)
            split_hi(W_F1)

            def relu2_bank(b):
                if b < TILES_A // 2 - 1:
                    act.wait_ge(z_ready, b + 1)
                else:
                    act.wait_ge(w_used, W_F1)
                nc.scalar.activation(sqb[:, b % 2, :], ps[:, b, :], ACT.Relu).then_inc(relu_ready, 1)
                act.wait_ge(relu_ready, b + 1)
                nc.scalar.activation(h1[:, b * 512:(b + 1) * 512], sqb[:, b % 2, :], ACT.Square).then_inc(h1_ready, 1)

            act.wait_ge(x1_ready, 8)
            for b in range(4):
                relu2_bank(b)
            split_hi(W_F1 + 1)
            for b in range(4, TILES_A // 2):
                relu2_bank(b)

            def ff_hi(s_unit, arrived_at, used):
                s, w = s_unit
                act.wait_ge(raw_in[s], arrived_at)
                act.wait_ge(w_used, used)
                nc.scalar.activation(w_hi[:, w, :], raw[:, s, :], ACT.Copy).then_inc(hi_ready, 1)

            def slots(n0, w0, j):
                return (n0 + j) % RING, (w0 + j) % 2

            def relu2(i, n, b):
                if b == 0:
                    act.wait_ge(z_ready, i * 2 + (TILES_A // 2 + n))
                else:
                    act.wait_ge(w_used, i * 8 + (W_F1 + 4 * n + 4))
                nc.scalar.activation(sqb[:, b, :], ps[:, 2 * n + b, :], ACT.Relu).then_inc(relu_ready, 1)
                act.wait_ge(relu_ready, i * 4 + (TILES_A // 2 + 2 * n + b + 1))
                nc.scalar.activation(h1[:, bass.ds(i * 2048 + (TILES_A * SEQ + n * 1024 + b * 512), 512)],
                                     sqb[:, b, :], ACT.Square).then_inc(h1_ready, 1)

            def ff1_hi(i, j):
                ff_hi(slots(N_FF1, W_F1, j), i * 32 + arrivals(N_FF1 + j), i * 8 + (W_F1 + j - 1))

            with act.Fori(0, TURNS // 2) as i:
                for j in range(2, 10):
                    ff1_hi(i, j)
                    if j % 4 == 0:
                        relu2(i, j // 4 - 1, 0)
                    if j % 4 == 1:
                        relu2(i, j // 4 - 1, 1)

            def h_hi(i, j, used, done=H1_DONE):
                act.wait_ge(w_used, used)
                act.wait_ge(h1_ready, done)
                nc.scalar.activation(a_hi[:, j % 4, :], h1[:, bass.ds(i * 1024 + j * SEQ, SEQ)], ACT.Copy).then_inc(ahi_ready, 1)

            last = TURNS // 2
            for j in range(2, 5):
                ff1_hi(last, j)
            for j in range(2):
                h_hi(0, j, W_F2 - 3, done=1)
            relu2(last, 0, 0)
            ff1_hi(last, 5)
            relu2(last, 0, 1)

            with act.Fori(0, 15) as i:
                for j in range(2, 6):
                    h_hi(i, j, i * 4 + (W_F2 + j - 3))
                    ff_hi(slots(N_FF2, W_F2, j), i * 16 + arrivals(N_FF2 + j), i * 4 + (W_F2 + j - 1))
            for j in range(2, 4):
                h_hi(15, j, W_F2 + 60 + j - 3)
                ff_hi(slots(N_FF2, W_F2, 60 + j), arrivals(N_FF2 + 60 + j), W_F2 + 60 + j - 1)
            act.wait_ge(gate_ready, 2)

            def gated_f(t):
                nc.scalar.activation(f_t[:, t, :], ps[:, t // 2, (t % 2) * SEQ:(t % 2 + 1) * SEQ], ACT.Copy,
                                     scale=gate2[:, t:t + 1]).then_inc(f_out, 1)

            for b in range(8):
                act.wait_ge(f_ready, b + 1)
                if b >= 2:
                    act.wait_ge(f_summed, max(b - 2, 1))
                nc.scalar.activation(sqb[:, b % 2, :], ps[:, b, :], ACT.Square).then_inc(f_squares, 1)
                if b % 2:
                    gated_f(b // 2)
            for t in range(4, FIRST_F):
                gated_f(t)
            make_std("f", D, ps[:, 0, 0:SEQ])
            for t in range(FIRST_F, KT):
                gated_f(t)

        @block.vector
        def _(dve):
            steps = [0]

            def link(ins):
                steps[0] += 1
                ins.then_inc(dve_step, 1)
                dve.wait_ge(dve_step, steps[0])

            V = nc.vector
            dve.wait_ge(small_in, 48)
            ang, t0 = rope_a[:, 0, :], rope_a[:, 1, :]
            link(V.tensor_copy(ang, h32[:, 0, :].bitcast(i32)))
            link(V.tensor_scalar(ang, ang, freq, None, ALU.mult))
            for turns in (4096.0, 1.0):
                link(V.tensor_scalar(t0, ang, 1.0 / (turns * 6.283185307179586), ROUND, ALU.mult, ALU.add))
                link(V.tensor_scalar(t0, t0, ROUND, None, ALU.subtract))
                for piece in TWO_PI:
                    link(V.scalar_tensor_tensor(out=ang, in0=t0, scalar=-turns * piece, in1=ang,
                                                op0=ALU.mult, op1=ALU.add))
            link(V.tensor_scalar(ang, ang, PI, -PI, ALU.min, ALU.max))
            link(V.tensor_scalar(t0, ang, -1.0, None, ALU.mult))
            link(V.tensor_tensor(t0, t0, ang, ALU.min))
            V.tensor_scalar(t0, t0, 1.5707963267948966, None, ALU.add).then_inc(ang_ready, 1)

            def ada_rows(q, r):
                if q >= 2 and r == 1:
                    dve.wait_ge(mod_sum, q - 1)
                for k in range(4):
                    for part in range(2):
                        if k == 0:
                            dve.wait_ge(ada_in[2 * r + part], 16 * (q + 1))
                        step = 24 * q + 8 * (r - 1) + 2 * k + part
                        if step >= 2:
                            dve.wait_ge(acc_step, step - 1)
                        a = acc[:, q % 2, part * 512:(part + 1) * 512]
                        src = ada_ring[:, 2 * r + part, k * 512:(k + 1) * 512]
                        c = cs[:, 4 * r + k:4 * r + k + 1]
                        if r == 1 and k == 0:
                            V.tensor_scalar(a, src, c, None, ALU.mult).then_inc(acc_step, 1)
                        else:
                            V.scalar_tensor_tensor(out=a, in0=src, scalar=c, in1=a, op0=ALU.mult,
                                                   op1=ALU.add).then_inc(acc_step, 1)

            def fold(name, j):
                g = CHUNKS.index((name, j))
                dve.wait_ge(sq_ready, g + 1)
                V.tensor_tensor(sqb[:, g % 2, 0:SEQ], sqb[:, g % 2, 0:SEQ], sqb[:, g % 2, SEQ:2 * SEQ],
                                ALU.add).then_inc(sq_folded, 1)

            def make_inv(name):
                i = NORM_NUMBER[name]
                dve.wait_ge(std_ready, i + 1)
                V.reciprocal(R[:, :], std[:, :]).then_inc(inv_ready, 1)
                dve.wait_ge(inv_ready, i + 1)

            def act_lo(n, slot, shift=None):
                dve.wait_ge(ahi_ready, n + 1)
                lo, h, hi = a_lo[:, slot, :], h32[:, n % 2, :], a_hi[:, slot, :].bitcast(f32)
                if shift is None:
                    ins = V.tensor_tensor(lo, h, hi, ALU.subtract)
                else:
                    ins = V.scalar_tensor_tensor(out=lo, in0=h, scalar=mods[:, shift + slot:shift + slot + 1],
                                                 in1=hi, op0=ALU.add, op1=ALU.subtract)
                ins.then_inc(alo_ready, 1)

            def modulated(n, t, gain):
                if n >= 2:
                    dve.wait_ge(alo_ready, n - 1)
                V.scalar_tensor_tensor(out=h32[:, n % 2, :], in0=xT[:, t, :], scalar=gain[:, t:t + 1], in1=R[:, :],
                                       op0=ALU.mult, op1=ALU.mult).then_inc(act32_ready, 1)

            def split_lo(w):
                n = RING_NUMBER[SPLIT_ITEMS[w]] if w < W_F1 else N_FF1 + w - W_F1
                dve.wait_ge(hi_ready, w + 1)
                if w >= 2:
                    dve.wait_ge(w_used, w - 1)
                src, hi, lo = raw[:, n % RING, :], w_hi[:, w % 2, :].bitcast(f32), w_lo[:, w % 2, :]
                if w < KT or w >= W_F1A and w < W_F1:
                    width = 1792 if w < KT else TILES_A * P
                    src, hi, lo = src[:, 0:width], hi[:, 0:width], lo[:, 0:width]
                elif w == W_ROPE:
                    src = src[:, 0:1024].rearrange("p (k c) -> p k c", c=64)
                    hi = hi.rearrange("p (k r c) -> p k r c", r=2, c=64)
                    lo = lo.rearrange("p (k r c) -> p k r c", r=2, c=64)
                    for r in range(2):
                        ins = V.tensor_tensor(lo[:, :, r, :], src, hi[:, :, r, :], ALU.subtract)
                    ins.then_inc(lo_ready, 1)
                    return
                V.tensor_tensor(lo, src, hi, ALU.subtract).then_inc(lo_ready, 1)

            dve.wait_ge(cs_ready, 1)
            for r in range(1, 4):
                ada_rows(0, r)
            make_inv("x")

            def modulation(q):
                dve.wait_ge(mod_sum, q + 1)
                t = 4 * q
                V.tensor_tensor(mods[:, 16 + t:20 + t], ps[:, 7, 0:4], col("b_ada", 16 + t, 4), ALU.add)
                V.tensor_tensor(mods[:, t:t + 4], ps[:, 7, 4:8], col("b_ada", t, 4), ALU.add).then_inc(mod_read, 1)
                dve.wait_ge(mod_read, q + 1)
                link(V.scalar_tensor_tensor(out=gain1[:, t:t + 4], in0=mods[:, 16 + t:20 + t], scalar=1.0,
                                            in1=col("pre1", t, 4), op0=ALU.add, op1=ALU.mult))

            def sum_rows(n, a, r, done, first, free):
                arrived(dve, n)
                if first:
                    dve.wait_ge(*free)
                for k in range(2):
                    src = raw[:, n % RING, k * 1024:(k + 1) * 1024]
                    c = cs[:, 2 * r + k:2 * r + k + 1]
                    if first and k == 0:
                        link(V.tensor_scalar(a, src, c, None, ALU.mult))
                    elif k == 0:
                        link(V.scalar_tensor_tensor(out=a, in0=src, scalar=c, in1=a, op0=ALU.mult, op1=ALU.add))
                    else:
                        V.scalar_tensor_tensor(out=a, in0=src, scalar=c, in1=a, op0=ALU.mult,
                                               op1=ALU.add).then_inc(ada_used, 1)
                        dve.wait_ge(ada_used, done)

            def ada_unit(i):
                hp, r = i // 8, i % 8
                sum_rows(RING_NUMBER["ada", i], acc[:, hp % 2, :], r, i + 1, r == 0, (mod_sum, 3 + hp) if hp < 2
                         else (b3_ready, CONV_B3[hp - 2] + 1))
            def late_unit(i):
                half, r = i // 8, i % 8
                sum_rows(RING_NUMBER["late", i], acc[:, half, :], r, ADA_COUNT + i + 1, r == 0, (b3_ready, CONV_B3[2 + half] + 1))

            def late_after(kind, i):
                for unit in LATE_AFTER.get((kind, i), ()):
                    late_unit(unit)

            def ada_after(kind, i):
                for unit in ADA_UNITS[kind, i]:
                    ada_unit(unit)

            def process(kind, i):
                if kind in SPLIT_NUMBER:
                    split_lo(SPLIT_NUMBER[kind] + i)
                ada_after(kind, i)
                late_after(kind, i)

            for k in range(KT):
                if k % 4 == 0:
                    modulation(k // 4)
                modulated(k, k, gain1)
                split_lo(k)
                act_lo(k, k, shift=0)
                if k < 12 and k % 4 < 3:
                    ada_rows(k // 4 + 1, k % 4 + 1)
                ada_after("in", k)

            def rotate(b3, dst):
                dve.wait_ge(b3_ready, b3 + 1)
                if b3:
                    dve.wait_ge(pe_rot, b3 - 1)
                V.tensor_tensor(rtmp, ps[:, 3, 0:SEQ], sinT[:, :], ALU.mult).then_inc(b3_read, 1)
                dve.wait_ge(b3_read, b3 + 1)
                link(V.tensor_tensor(dst, dst, cosT[:, :], ALU.mult))
                V.tensor_tensor(dst, dst, rtmp, ALU.add).then_inc(pe_rot, 1)

            def conv_read(hp):
                b3 = CONV_B3[hp]
                m0 = ADA_HALVES[hp][1]
                dve.wait_ge(b3_ready, b3 + 1)
                V.tensor_tensor(mods[:, m0:m0 + 8], ps[:, 3, 0:8], col("b_ada", m0, 8), ALU.add).then_inc(b3_read, 1)
                dve.wait_ge(b3_read, b3 + 1)

            process("rope", 0)
            split_lo(W_U)
            make_inv("kv")
            for t in range(2):
                V.scalar_tensor_tensor(out=kv_lat[:, t, :], in0=kv_lat[:, t, :], scalar=col("kvn", t), in1=R[:, :],
                                       op0=ALU.mult, op1=ALU.mult).then_inc(latn_ready, 1)
            dve.wait_ge(latn_ready, 2)
            make_inv("q")
            for t in range(4):
                V.scalar_tensor_tensor(out=q_lat[:, t, :], in0=q_lat[:, t, :], scalar=col("qn", t), in1=R[:, :],
                                       op0=ALU.mult, op1=ALU.mult).then_inc(latn_ready, 1)
            ada_after("u", 0)
            process("u", 1)
            process("kvb", 0)
            process("kvb", 1)
            rotate(0, k_pe)
            dve.wait_ge(vgelu_ready, 1)
            for t in range(2):
                for j in range(2):
                    link(V.bn_stats(bst[:, t, j, :], v_tok[:, t, j * 512:(j + 1) * 512]))
            V.bn_aggr(mv[:, 0, :], bst[:, 0, :, :].rearrange("p a b -> p (a b)"))
            V.bn_aggr(mv[:, 1, :], bst[:, 1, :, :].rearrange("p a b -> p (a b)")).then_inc(vstat_ready, 1)
            process("qb", 0)
            process("qb", 1)
            conv_read(0)
            rotate(2, q_pe[:, 0, :])
            process("qb", 2)
            rotate(3, q_pe[:, 1, :])
            ada_after("qb", 3)
            rotate(4, q_pe[:, 2, :])
            rotate(5, q_pe[:, 3, :])
            process("u", 2)
            def row_max(h):
                dve.wait_ge(s_ready, h + 1)
                if h:
                    dve.wait_ge(exp_ready, 2 * h)
                V.memset(ps[0:64, 0, 64:128], NEG)
                link(V.memset(ps[0:64, 0, 320:384], NEG))
                V.reduce_max(mx[:, 0:1], ps[:, 0, 0:128], AX.X)
                link(V.reduce_max(mx[:, 1:2], ps[:, 0, 128:384], AX.X))
                V.tensor_scalar(nb[:, :], mx[:, :], -float(QHD) ** -0.5, None, ALU.mult).then_inc(nb_ready, 1)

            def normalise(h):
                dve.wait_ge(exp_ready, 2 * h + 2)
                link(V.reciprocal(rinv[:, :], rsum[:, :]))
                p = prob[:, h % 2, :]
                V.tensor_scalar(p[:, 0:128], p[:, 0:128], rinv[:, 0:1], None, ALU.mult)
                V.tensor_scalar(p[:, 128:384], p[:, 128:384], rinv[:, 1:2], None, ALU.mult).then_inc(p_ready, 1)

            def gate_u(g):
                t = h32[:, g % 2, :]
                if g >= 2:
                    dve.wait_ge(gm_out, g - 1)
                link(V.tensor_tensor(t.rearrange("p (n i) -> p n i", i=128),
                                     ps[:, 4 + g // 2, (g % 2) * 256:(g % 2) * 256 + 256].rearrange("p (n i) -> p n i", i=128),
                                     bs_rows[:, g * 128:(g + 1) * 128].rearrange("p (n i) -> p n i", n=1).to_broadcast([P, 2, 128]),
                                     ALU.add))
                V.tensor_tensor(u_t[:, g, :], t, u_t[:, g, :], ALU.mult).then_inc(gm_out, 1)

            def layer_norm(t):
                if t == 0:
                    dve.wait_ge(vstd_ready, 1)
                    link(V.reciprocal(vrs[:, :], vstd[:, :]))
                    dve.wait_ge(ln_in, 32)
                link(V.tensor_scalar(v_tok[:, t, :], v_tok[:, t, :], mv[:, t, 0:1], vrs[:, t:t + 1],
                                     ALU.subtract, ALU.mult))
                link(V.tensor_tensor(v_tok[:, t, :], v_tok[:, t, :], ln_rows[:, 0, :], ALU.mult))
                V.tensor_tensor(v_tok[:, t, :], v_tok[:, t, :], ln_rows[:, 1, :], ALU.add).then_inc(vnorm_ready, 1)

            for j in range(8):
                row_max(j)
                if j < 7:
                    split_lo(W_U + 3 + j)
                normalise(j)
                if j == 0:
                    layer_norm(0)
                    layer_norm(1)
                if j < 6:
                    ada_after(*SPLIT_ITEMS[W_U + 3 + j])
                if j == 6:
                    ada_unit(ADA_UNITS["wo", 1][0])
                if j == 7:
                    dve.wait_ge(gm_ready, 2)
                    for g in range(4, 8):
                        gate_u(g)
                    for unit in ADA_UNITS["wo", 1][1:]:
                        ada_unit(unit)
                if j == 1:
                    conv_read(1)
                    V.tensor_tensor(gate1[:, :], mods[:, 32:48], col("post1", 0, 16), ALU.mult).then_inc(gate_ready, 1)
                if j == 5:
                    conv_read(2)
                if j == 6:
                    dve.wait_ge(gm_ready, 1)
                    dve.wait_ge(gelu_u, 1)
                    dve.wait_ge(gm_in, 32)
                    for g in range(4):
                        gate_u(g)

            def normed(first, after, src, gain):
                for t in range(first, after):
                    dve.wait_ge(alo_ready, 15 + t)
                    V.scalar_tensor_tensor(out=h32[:, t % 2, :], in0=src[:, t % 8, :], scalar=col(gain, t % 8),
                                           in1=R[:, :], op0=ALU.mult, op1=ALU.mult).then_inc(act32_ready, 1)
                    if t > first:
                        act_lo(15 + t, t - 1)
                act_lo(15 + after, after - 1)

            make_inv("a")
            dve.wait_ge(w_used, W_O)
            normed(0, 8, u_t, "ga")
            ada_after("wo", 2)
            ada_after("wo", 3)
            split_lo(W_O + 2)
            make_inv("m")
            normed(8, 12, m_t, "gb")
            split_lo(W_O + 3)
            normed(12, 16, m_t, "gb")
            for i in range(4, 16):
                process("wo", i)
                if i % 4 in (1, 2):
                    fold("y", i // 4 * 2 - 3 + i % 4)
                for at, hp in CONV_AFTER.items():
                    if i == at + 1:
                        conv_read(hp)
            def make_gain2(t):
                link(V.scalar_tensor_tensor(out=gain2[:, t:t + 8], in0=mods[:, 64 + t:72 + t], scalar=1.0,
                                            in1=col("pre2", t, 8), op0=ALU.add, op1=ALU.mult))
            make_gain2(0)

            def add_normed(part, j, done):
                y2, x2 = part[:, 2 * j:2 * j + 2, :], xT[:, 2 * j:2 * j + 2, :]
                link(V.tensor_tensor(y2, y2, R[:, :].rearrange("p (t n) -> p t n", t=1).to_broadcast([P, 2, SEQ]),
                                     ALU.mult))
                V.tensor_tensor(x2, x2, y2, ALU.add).then_inc(done, 1)

            fold("y", 6)
            fold("y", 7)
            split_lo(W_F1A)
            make_inv("y")
            dve.wait_ge(y_out, 16)
            for j in range(8):
                add_normed(y_t, j, x1_ready)
            late_unit(11)
            make_inv("x1")

            def operand_tiles(first, after):
                for t in range(first, after):
                    modulated(32 + t, t, gain2)
                    if t > first:
                        act_lo(31 + t, t - 1, shift=48)
                act_lo(31 + after, after - 1, shift=48)

            operand_tiles(0, 4)
            split_lo(W_F1A + 1)
            operand_tiles(4, 8)
            late_unit(12)
            for k in range(2, 5):
                process("f1", k)
            split_lo(W_F1A + 5)
            dve.wait_ge(late_sum, 1)
            for half, (_, m0) in enumerate(LATE_HALVES):
                ins = V.tensor_tensor(mods[:, m0:m0 + 8], ps[:, 7, 8 * half:8 * half + 8], col("b_ada", m0, 8), ALU.add)
            ins.then_inc(late_read, 1)
            dve.wait_ge(late_read, 1)
            make_gain2(8)
            operand_tiles(8, 10)
            split_lo(W_F1A + 6)
            operand_tiles(10, 13)
            split_lo(W_F1A + 7)
            operand_tiles(13, 16)

            acc_all = acc[:, :, :].rearrange("p a n -> p (a n)")

            def g2_rows(row):
                dve.wait_ge(g2_in, row * 16 + 16)
                V.scalar_tensor_tensor(out=acc_all, in0=ada_g2[:, :], scalar=cs[:, bass.ds(row, 1)], in1=acc_all,
                                       op0=ALU.mult, op1=ALU.add).then_inc(ada_used, 1)
                dve.wait_ge(ada_used, row + (G2_BASE + 1))

            for k in range(8, 16):
                split_lo(W_F1A + k)
                if k in G2_AFTER:
                    if k == G2_AFTER[0]:
                        dve.wait_ge(acc_cleared, 1)
                    g2_rows(G2_AFTER.index(k))
            split_lo(W_F1)
            split_lo(W_F1 + 1)

            def ff_lo(s_unit, hi, used):
                s, w = s_unit
                dve.wait_ge(hi_ready, hi)
                dve.wait_ge(w_used, used)
                V.tensor_tensor(w_lo[:, w, :], raw[:, s, :], w_hi[:, w, :].bitcast(f32), ALU.subtract).then_inc(lo_ready, 1)

            def slots(n0, w0, j):
                return (n0 + j) % RING, (w0 + j) % 2

            def ff1_lo(i, j):
                ff_lo(slots(N_FF1, W_F1, j), i * 8 + (W_F1 + j + 1), i * 8 + (W_F1 + j - 1))

            with dve.Fori(0, TURNS // 2) as i:
                for j in range(2, 10):
                    ff1_lo(i, j)
                    if j % 4 == 3:
                        g2_rows(i * 2 + (len(G2_AFTER) + j // 4))

            def h_lo(i, j, n):
                dve.wait_ge(ahi_ready, n)
                V.tensor_tensor(a_lo[:, j % 4, :], h1[:, bass.ds(i * 1024 + j * SEQ, SEQ)], a_hi[:, j % 4, :].bitcast(f32),
                                ALU.subtract).then_inc(alo_ready, 1)

            last = TURNS // 2
            g2_rows(15)
            for j in range(2, 5):
                ff1_lo(last, j)
            for j in range(2):
                h_lo(0, j, 49 + j)
            dve.wait_ge(g2_sum, 1)
            V.tensor_tensor(mods[:, 80:96], ps[:, 7, 0:16], col("b_ada", 80, 16), ALU.add).then_inc(g2_ready, 1)
            ff1_lo(last, 5)
            dve.wait_ge(g2_ready, 1)
            V.tensor_tensor(gate2[:, :], mods[:, 80:96], col("post2", 0, 16), ALU.mult).then_inc(gate_ready, 1)

            with dve.Fori(0, 15) as i:
                for j in range(2, 6):
                    h_lo(i, j, i * 4 + (49 + j))
                    ff_lo(slots(N_FF2, W_F2, j), i * 4 + (W_F2 + j + 1), i * 4 + (W_F2 + j - 1))
            for j in range(2, 4):
                h_lo(15, j, 48 + 60 + j + 1)
                ff_lo(slots(N_FF2, W_F2, 60 + j), W_F2 + 60 + j + 1, W_F2 + 60 + j - 1)
            f_sq = h32[:, :, :].rearrange("p t n -> p (t n)")
            for b in range(1, 8):
                dve.wait_ge(f_squares, b + 1)
                if b > 1:
                    dve.wait_ge(f_summed, b - 1)
                V.tensor_tensor(f_sq, sqb[:, 0, :] if b == 1 else f_sq, sqb[:, b % 2, :], ALU.add).then_inc(f_summed, 1)
            dve.wait_ge(f_summed, 7)
            V.tensor_tensor(h32[:, 0, :], h32[:, 0, :], h32[:, 1, :], ALU.add).then_inc(f_summed, 1)
            make_inv("f")
            for j in range(8):
                dve.wait_ge(f_out, 2 * j + 2)
                add_normed(f_t, j, o_ready)

        @block.tensor
        def _(pe):
            mm = nc.tensor.matmul

            def add_squares(name, j, dst):
                g = CHUNKS.index((name, j))
                tiles = 2
                if name in FOLDED:
                    tiles = 1
                    pe.wait_ge(sq_folded, FOLDED.index(name) * 8 + j + 1)
                else:
                    pe.wait_ge(sq_ready, g + 1)
                for t in range(tiles):
                    ins = mm(dst, ones[:, :], sqb[:, g % 2, t * SEQ:(t + 1) * SEQ],
                             start=(j == 0 and t == 0), stop=(j == NORMS[name] - 1 and t == tiles - 1))
                ins.then_inc(sq_used, 1)

            def ada_products(q):
                if q:
                    pe.wait_ge(mod_read, q)
                for part in range(2):
                    pe.wait_ge(ada_in[part], 16 * (q + 1))
                    for t in range(4):
                        for k in range(4):
                            c = k * 512 + t * P
                            ins = mm(ps[:, 7, 4 * part + t:4 * part + t + 1], ada_ring[:, part, c:c + P], cs[:, k:k + 1],
                                     start=(part == 0 and t == 0 and k == 0), stop=False, skip_group_check=True)
                ins.then_inc(ada_pe_used, 1)

            def sum_ada(q):
                pe.wait_ge(acc_step, 24 * (q + 1))
                for f in range(8):
                    ins = mm(ps[:, 7, f:f + 1], acc[:, q % 2, f * P:(f + 1) * P], ones[:, 0:1],
                             start=False, stop=True, skip_group_check=True)
                ins.then_inc(mod_sum, 1)

            def three(dst, w, a, start, stop, stationary_weights=True):
                (wh, wl), (ah, al) = w, a
                for n, (x, y) in enumerate(((wh, ah), (wh, al), (wl, ah)) if stationary_weights else
                                           ((ah, wh), (ah, wl), (al, wh))):
                    ins = mm(dst, x, y, start=(start and n == 0), stop=(stop and n == 2), skip_group_check=True)
                return ins

            def in_rows(k):
                s = k % 2
                pe.wait_ge(lo_ready, k + 1)
                pe.wait_ge(alo_ready, k + 1)
                for t in range(2):
                    a = (a_hi[:, k, t * P:(t + 1) * P], a_lo[:, k, t * P:(t + 1) * P])
                    for n in range(2):
                        w = (w_hi[:, s, n * 512:(n + 1) * 512], w_lo[:, s, n * 512:(n + 1) * 512])
                        three(ps[:, 2 * t + n, :], w, a, k == 0, k == KT - 1, stationary_weights=False)
                for f in range(6):
                    c = 1024 + f * P
                    ins = three(ps[:, 4 + f // 2, (f % 2) * SEQ:(f % 2 + 1) * SEQ],
                                (w_hi[:, s, c:c + P], w_lo[:, s, c:c + P]), (a_hi[:, k, :], a_lo[:, k, :]),
                                k == 0 and f % 2 == 0, k == KT - 1)
                ins.then_inc(w_used, 1)

            pe.wait_ge(consts_ready, 2)
            for j in range(8):
                add_squares("x", j, ps[:, 0, 0:SEQ])
            pe.wait_ge(cs_ready, 1)
            ada_products(0)
            for k in range(KT):
                if k == 0 or k % 4 == 3 and k < 12:
                    sum_ada((k + 1) // 4)
                in_rows(k)
                if k % 4 == 0 and k < 12:
                    ada_products(k // 4 + 1)

            pe.wait_ge(lo_ready, W_ROPE + 1)
            pe.wait_ge(mod_read, 4)
            s = W_ROPE % 2
            for k in range(KT):
                ins = three(ps[:, 7, 0:SEQ], (w_hi[:, s, k * P:(k + 1) * P], w_lo[:, s, k * P:(k + 1) * P]),
                            (a_hi[:, k, :], a_lo[:, k, :]), k == 0, k == KT - 1)
            ins.then_inc(w_used, 1)

            def acc_sums(step, done):
                for f in (2 * step, 2 * step + 1):
                    ins = mm(ps[:, 7, f:f + 1], acc[:, f // 8, (f % 8) * P:(f % 8 + 1) * P], ones[:, 0:1],
                             start=True, stop=True)
                if step == 7:
                    ins.then_inc(done, 1)

            def quad_unit(w_slot, quarter, bank, first_act=None, half_done=None, sums=None):
                wh, wl = w_hi[:, w_slot, :], w_lo[:, w_slot, :]
                order = [(k, t) for k in range(4) for t in range(4)]
                if first_act is None:
                    order = [(k, t) for t in range(4) for k in range(4)]
                for k, t in order:
                    if first_act is not None and t == 0:
                        pe.wait_ge(alo_ready, first_act + k + 1)
                    c, tile = k * 512 + t * P, 4 * quarter + k
                    ins = three(ps[:, bank + t // 2, (t % 2) * SEQ:(t % 2 + 1) * SEQ], (wh[:, c:c + P], wl[:, c:c + P]),
                                (a_hi[:, tile, :], a_lo[:, tile, :]),
                                quarter == 0 and k == 0 and t % 2 == 0, quarter == 3 and k == 3)
                    if half_done is not None and quarter == 3 and (k, t) == (3, 1):
                        ins.then_inc(half_done, 1)
                    if sums is not None and k + 4 * t < 8:
                        acc_sums(k + 4 * t, sums)
                ins.then_inc(w_used, 1)

            def u_unit(i):
                if i == 0:
                    pe.wait_ge(lat_ready, 2)
                if i == 4:
                    pe.wait_ge(rope_raw, 1)
                    pe.wait_ge(std_ready, 3)
                pe.wait_ge(lo_ready, W_U + i + 1)
                quad_unit((W_U + i) % 2, i % 4, 4 + 2 * (i // 4))

            b3 = [0]

            def take_b3():
                if b3[0]:
                    pe.wait_ge(b3_read, b3[0])
                b3[0] += 1

            def conv(hp):
                take_b3()
                pe.wait_ge(ada_used, 8 * (hp + 1))
                for f in range(8):
                    ins = mm(ps[:, 3, f:f + 1], acc[:, hp % 2, f * P:(f + 1) * P], ones[:, 0:1], start=True, stop=True)
                ins.then_inc(b3_ready, 1)

            def swap_halves(src, n):
                take_b3()
                if n is None:
                    pe.wait_ge(rope_raw, 1)
                else:
                    pe.wait_ge(proj_out, n)
                mm(ps[:, 3, 0:SEQ], swap, src, start=True, stop=True).then_inc(b3_ready, 1)

            proj = [0]

            def project(terms, width):
                n = proj[0]
                if n >= 3:
                    pe.wait_ge(proj_out, n - 2)
                dst = ps[:, n % 3, 0:width]
                for m, (x, y) in enumerate(terms):
                    ins = mm(dst, x, y, start=(m == 0), stop=(m == len(terms) - 1))
                ins.then_inc(proj_ready, 1)
                proj[0] += 1
                return ins

            def kvb_unit(g):
                n = RING_NUMBER["kvb", g]
                arrived(pe, n)
                w = raw[:, n % RING, :].rearrange("p (k h c) -> p k h c", k=2, c=NOPE + VD)
                for h in range(4):
                    project([(w[:, k, h, 0:NOPE], kv_lat[:, k, :]) for k in range(2)], SEQ)
                for t in range(2):
                    m = proj[0]
                    pe.wait_ge(proj_out, m - 2)
                    for k in range(2):
                        ins = mm(ps[:, m % 3, :].rearrange("p (h c) -> p h c", c=P), kv_lat[:, k, t * P:(t + 1) * P],
                                 w[:, k, :, NOPE:NOPE + VD], start=(k == 0), stop=(k == 1))
                    ins.then_inc(proj_ready, 1)
                    proj[0] += 1

            def qb_unit(i):
                n = RING_NUMBER["qb", i]
                arrived(pe, n)
                w = raw[:, n % RING, 0:1536].rearrange("p (k c) -> p k c", k=4)
                m = proj[0]
                pe.wait_ge(proj_out, m - 2)
                for k in range(4):
                    ins = mm(ps[:, m % 3, 0:SEQ], w[:, k, 2 * NOPE:2 * QHD], q_lat[:, k, :], start=(k == 0), stop=(k == 3))
                ins.then_inc(proj_ready, 1)
                proj[0] += 1
                for h in range(2):
                    project([(w[:, k, h * NOPE:(h + 1) * NOPE], q_lat[:, k, :]) for k in range(4)], SEQ)

            pe.wait_ge(lat_ready, 2)
            add_squares("kv", 0, ps[:, 6, 0:SEQ])
            pe.wait_ge(rope_raw, 1)
            for j in range(2):
                add_squares("q", j, ps[:, 7, 0:SEQ])
            u_unit(0)
            u_unit(1)
            pe.wait_ge(vgelu_ready, 1)
            pe.wait_ge(latn_ready, 2)
            kvb_unit(0)
            swap_halves(k_pe, None)
            kvb_unit(1)
            pe.wait_ge(latn_ready, 6)
            qb_unit(0)
            conv(0)
            qb_unit(1)
            swap_halves(q_pe[:, 0, :], 13)
            qb_unit(2)
            swap_halves(q_pe[:, 1, :], 16)
            qb_unit(3)
            swap_halves(q_pe[:, 2, :], 19)
            swap_halves(q_pe[:, 3, :], 22)

            def scores(h):
                r = (h % 2) * 64
                if h:
                    pe.wait_ge(exp_ready, 2 * h)
                else:
                    pe.wait_ge(proj_out, 24)
                pe.wait_ge(pe_rot, 2 + h // 2)
                for b in range(2):
                    dst = ps[:, 0, 128 * b:128 + 256 * b]
                    keys = P * (b + 1)
                    mm(dst, qT[:, h, b * P:(b + 1) * P], kT[:, h, 0:keys], start=True, stop=False)
                    ins = mm(dst, q_pe[r:r + 64, h // 2, b * P:(b + 1) * P], k_pe[r:r + 64, 0:keys],
                             start=False, stop=True)
                ins.then_inc(s_ready, 1)

            def transposes(h):
                pe.wait_ge(p_ready, h + 1)
                if h:
                    pe.wait_ge(pt_out, h)
                for b in range(3):
                    ins = nc.tensor.transpose(ps[:, 1, b * P:(b + 1) * P], prob[:, h % 2, b * P:(b + 1) * P], ident)
                ins.then_inc(pt_ready, 1)

            def values(h):
                pe.wait_ge(pt_out, h + 1)
                if h:
                    pe.wait_ge(m_out, h)
                pt = probT[:, h % 2, :]
                mm(ps[:, 2, 0:SEQ], v_att[:, 0, h * P:(h + 1) * P], pt[:, 0:256], start=True, stop=False,
                   skip_group_check=True)
                mm(ps[:, 2, P:SEQ], v_att[:, 1, h * P:(h + 1) * P], pt[:, 256:384], start=False, stop=True,
                   skip_group_check=True).then_inc(pv_ready, 1)

            def spatial(half):
                if half == 0:
                    pe.wait_ge(vnorm_ready, 2)
                    pe.wait_ge(ws_masked, 1)
                    pe.wait_ge(u_out, 1)
                else:
                    pe.wait_ge(u_out, 2)
                for g in range(4 * half, 4 * half + 4):
                    for n in range(2):
                        c = (g % 2) * 256 + n * P
                        ins = mm(ps[:, 4 + g // 2, c:c + P], v_tok[:, n, g * P:(g + 1) * P],
                                 wsT[:, g * P:(g + 1) * P], start=True, stop=True)
                ins.then_inc(gm_ready, 1)

            for j in range(8):
                scores(j)
                if j < 6:
                    u_unit(2 + j)
                if j in (1, 5):
                    conv(1 if j == 1 else 2)
                if j == 6:
                    spatial(0)
                    spatial(1)
                    pe.wait_ge(b3_read, b3[0])
                    add_squares("m", 0, ps[:, 3, 0:SEQ])
                    add_squares("m", 1, ps[:, 3, 0:SEQ])
                if j == 7:
                    add_squares("m", 2, ps[:, 3, 0:SEQ])
                if j:
                    values(j - 1)
                transposes(j)
            for j in range(4):
                add_squares("a", j, ps[:, 0, 0:SEQ])
                if j == 1:
                    values(7)
            add_squares("m", 3, ps[:, 3, 0:SEQ])

            for i in range(16):
                q = i // 4
                if i == 0:
                    pe.wait_ge(gm_out, 4)
                elif i == 4:
                    pe.wait_ge(gm_out, 8)
                elif i % 4 == 0:
                    pe.wait_ge(y_out, 4 * q - 4)
                pe.wait_ge(lo_ready, W_O + i + 1)
                quad_unit((W_O + i) % 2, i % 4, 4 + 2 * (q % 2), first_act=16 + 4 * i if i < 4 else None,
                          half_done=y_half if q == 3 else None)
                if i % 4 == 2 and q:
                    if q == 1:
                        pe.wait_ge(m_out, 8)
                    add_squares("y", 2 * q - 2, ps[:, 2, 0:SEQ])
                    add_squares("y", 2 * q - 1, ps[:, 2, 0:SEQ])
                if i in CONV_AFTER:
                    conv(CONV_AFTER[i])
            add_squares("y", 6, ps[:, 2, 0:SEQ])
            add_squares("y", 7, ps[:, 2, 0:SEQ])
            pe.wait_ge(std_ready, 4)
            for j in range(8):
                add_squares("x1", j, ps[:, 1, 0:SEQ])

            pe.wait_ge(std_ready, 7)
            pe.wait_ge(b3_read, 9)
            pe.wait_ge(y_out, 16)
            for k in range(KT):
                if k == LATE_SUM:
                    pe.wait_ge(ada_used, G2_BASE)
                    for f in range(16):
                        ins = mm(ps[:, 7, f:f + 1], acc[:, f // 8, (f % 8) * P:(f % 8 + 1) * P], ones[:, 0:1],
                                 start=True, stop=True)
                    ins.then_inc(late_sum, 1)
                pe.wait_ge(lo_ready, W_F1A + k + 1)
                pe.wait_ge(alo_ready, 32 + k + 1)
                w = (W_F1A + k) % 2
                for t in range(TILES_A):
                    ins = three(ps[:, t // 2, (t % 2) * SEQ:(t % 2 + 1) * SEQ],
                                (w_hi[:, w, t * P:(t + 1) * P], w_lo[:, w, t * P:(t + 1) * P]),
                                (a_hi[:, k, :], a_lo[:, k, :]), k == 0 and t % 2 == 0, k == KT - 1)
                    if k == KT - 1 and t % 2 and t < TILES_A - 1:
                        ins.then_inc(z_ready, 1)
                ins.then_inc(w_used, 1)

            def ff1_turn(n, w_done, relus):
                for j in range(4):
                    pe.wait_ge(lo_ready, w_done + (j + 1))
                    if j == 0:
                        pe.wait_ge(relu_ready, relus)
                    quad_unit((W_F1 + j) % 2, j, 2 * n, half_done=z_ready)

            for n in range(2):
                ff1_turn(n, W_F1 + 4 * n, 2 + 2 * n)
            with pe.Fori(1, TURNS // 2) as i:
                for n in range(2):
                    ff1_turn(n, i * 8 + (W_F1 + 4 * n), i * 4 + (4 + 2 * n))
            for j in range(4):
                if j == 3:
                    pe.wait_ge(ada_used, G2_BASE + 16)
                pe.wait_ge(lo_ready, W_F2 - 4 + j + 1)
                if j == 0:
                    pe.wait_ge(relu_ready, H1_DONE - 4)
                quad_unit((W_F1 + j) % 2, j, 0, half_done=z_ready, sums=g2_sum if j == 3 else None)

            def ff2_dst(d):
                return ps[:, d // 2, (d % 2) * SEQ:(d % 2 + 1) * SEQ]

            def ff2_part(w, j, d, first, last):
                return three(ff2_dst(d), (w_hi[:, w, d * P:(d + 1) * P], w_lo[:, w, d * P:(d + 1) * P]),
                             (a_hi[:, j, :], a_lo[:, j, :]), first and d % 2 == 0, last)

            def ff2_unit(j, w_wait, a_wait, first=False):
                w = (W_F2 + j) % 2
                pe.wait_ge(lo_ready, w_wait)
                pe.wait_ge(alo_ready, a_wait)
                for d in (*range(8, 16), *range(8)) if first else range(16):
                    if first and d == 14:
                        pe.wait_ge(g2_ready, 1)
                    if first and d == 0:
                        pe.wait_ge(relu_ready, H1_DONE)
                    ins = ff2_part(w, j, d, first, False)
                ins.then_inc(w_used, 1)

            for j in range(4):
                ff2_unit(j, W_F2 + j + 1, 48 + j + 1, first=(j == 0))
            with pe.Fori(1, 15) as i:
                for j in range(4):
                    ff2_unit(j, i * 4 + (W_F2 + j + 1), i * 4 + (48 + j + 1))
            for j in range(3):
                ff2_unit(j, W_F2 + 60 + j + 1, 48 + 60 + j + 1)
            pe.wait_ge(lo_ready, W_F2 + 64)
            pe.wait_ge(alo_ready, 48 + 64)
            for b in range(8):
                for d in (2 * b, 2 * b + 1):
                    ins = ff2_part((W_F2 + 3) % 2, 3, d, False, True)
                ins.then_inc(f_ready, 1)
            pe.wait_ge(f_summed, 8)
            pe.wait_ge(f_out, 2)
            mm(ps[:, 0, 0:SEQ], ones[:, :], h32[:, 0, :], start=True, stop=True).then_inc(sq_used, 1)



CONV_B3 = [1, 6, 7, 8]

_COLUMNS = [("c", "c"), ("b_ada", "b_ada"), ("pre1", "pre_norm1_g"), ("post1", "post_norm1_g"),
            ("pre2", "pre_norm2_g"), ("post2", "post_norm2_g"), ("qn", "q_norm_g"), ("kvn", "kv_norm_g"),
            ("ga", "grp_norm_a_g"), ("gb", "grp_norm_b_g")]


def kernel(**inputs):
    import numpy as np
    import concourse.bacc as bacc
    from concourse.bass_utils import run_bass_kernel_spmd

    a = {k: np.asarray(v) for k, v in inputs.items()}
    qb = a["w_q_b"][0].reshape(QL, HEADS // 2, 2, QHD)
    qb = np.concatenate([qb[..., :NOPE].reshape(QL, 4, 2 * NOPE), qb[..., NOPE:].reshape(QL, 4, 2 * ROPE)], axis=2)
    arrays = {
        "xT": np.ascontiguousarray(a["x"][0].T),
        "positions": a["positions"].reshape(1, SEQ),
        "cols": np.ascontiguousarray(np.concatenate([a[src].reshape(-1, P) for _, src in _COLUMNS], axis=0).T),
        "w_sT": np.ascontiguousarray(a["w_s"][0].transpose(2, 0, 1)).reshape(P, GROUPS * P),
        "b_s": a["b_s"].reshape(1, GROUPS * P),
        "ln_v_g": a["ln_v_g"].reshape(1, GW),
        "ln_v_b": a["ln_v_b"].reshape(1, GW),
        "w_ada": a["w_ada"][0], "w_in": a["w_in"][0], "w_q_b": np.ascontiguousarray(qb.reshape(QL, HEADS * QHD)), "w_kv_b": a["w_kv_b"][0],
        "w_o": a["w_o"][0], "w_ff1": a["w_ff1"][0], "w_ff2": a["w_ff2"][0],
    }
    consts = np.zeros((P, NCONST), np.float32)
    rows = np.arange(P)
    consts[rows, C_IDENT + rows] = 1.0
    consts[rows, C_SWAP + (rows ^ 32)] = 1.0
    f = np.float32(ROPE_THETA) ** (-np.arange(0, ROPE, 2, dtype=np.float32) / np.float32(ROPE))
    consts[:, C_FREQ] = np.where(rows % 64 < 32, -1.0, 1.0) * f[rows % 32]
    arrays["consts"] = consts

    nc = bacc.Bacc("TRN2", target_bir_lowering=False, num_devices=1)
    aps = {k: nc.dram_tensor("in_" + k, v.shape, mybir.dt.from_np(v.dtype), kind="ExternalInput").ap() for k, v in arrays.items()}
    out = nc.dram_tensor("outT", (D, SEQ), mybir.dt.float32, kind="ExternalOutput").ap()
    block_kernel(nc, aps, out)
    r = run_bass_kernel_spmd(nc, [{"in_" + k: v for k, v in arrays.items()}], core_ids=[0])
    return np.ascontiguousarray(r.results[0]["outT"].T).reshape(1, SEQ, D)
```
